# Optimizing a Trainium2 kernel written in Bass

```python
import math, functools
import jax, jax.numpy as jnp
from jax import lax
import numpy as np

D_MODEL = 1024
BATCH = 1
SEQ = 128
DEPTH = 2
DEC_BATCH = 1
DEC_SEQ = 256
PAST_LEN = 128

GRID_W = 64
HEAD_DIM = 64
D_ATT = D_MODEL // 2
D_CMLP = D_MODEL // 4
D_CONV = D_MODEL - D_ATT - D_CMLP
D_MIX = D_ATT + D_CMLP + D_CONV
H_ATT = D_ATT // HEAD_DIM
H_CMLP = D_CMLP // HEAD_DIM
CHUNK = 128
CONV_W = 3
NA_KH = 8
NA_KW = 16
NA_QB = 16
NA_KB = 32
D_IN = 3 * D_ATT + 2 * D_CMLP + 3 * D_CONV
D_FF = 2816
N_EXPERTS = 8
TOP_K = 2
N_MOD = 6
EPS = 1e-6
NEG_INF = -1e30
N_DENSE = (DEPTH + 1) // 2
N_MOE = DEPTH // 2

kernel_name = "hybrid_natten_gmlp_shortconv_dit_step"

def rms_norm(x, g):
    xf = x.astype(jnp.float32)
    y = xf * lax.rsqrt(jnp.mean(xf * xf, axis=-1, keepdims=True) + EPS)
    return (y * g.astype(jnp.float32)).astype(x.dtype)

def ada_modulation(cvec, w, b):
    mod = jax.nn.silu(cvec) @ w + b
    return mod.reshape(cvec.shape[0], N_MOD, 1, D_MODEL)

def split_projection(p):
    sizes = [D_ATT] * 3 + [D_CMLP] * 2 + [D_CONV] * 3
    offs = [int(o) for o in np.cumsum(sizes)[:-1]]
    return jnp.split(p, offs, axis=-1)

def context_attention(q, k, v):
    s = jnp.einsum('bqhd,bkhd->bhqk', q, k).astype(jnp.float32) * (HEAD_DIM ** -0.5)
    p = jax.nn.softmax(s, axis=-1).astype(v.dtype)
    return jnp.einsum('bhqk,bkhd->bqhd', p, v)

def neighbourhood_attention(q, k, v, k_ctx, v_ctx, rpb):
    bsz, n, nh, dh = q.shape
    rows = n // GRID_W
    kh = min(NA_KH, rows)
    ncb = GRID_W // NA_QB
    r = jnp.arange(rows)
    row_start = jnp.clip(r - kh // 2, 0, rows - kh)
    row_idx = row_start[:, None] + jnp.arange(kh)
    qcol = jnp.arange(ncb)[:, None] * NA_QB + jnp.arange(NA_QB)
    kb0 = jnp.clip(jnp.arange(ncb) * NA_QB - NA_KW // 2, 0, GRID_W - NA_KB)
    col_idx = kb0[:, None] + jnp.arange(NA_KB)
    col_start = jnp.clip(qcol - NA_KW // 2, 0, GRID_W - NA_KW)
    kcol = col_idx[:, None, :]
    valid = (kcol >= col_start[:, :, None]) & (kcol < col_start[:, :, None] + NA_KW)
    kg = k.reshape(bsz, rows, GRID_W, nh, dh)
    vg = v.reshape(bsz, rows, GRID_W, nh, dh)
    ri = row_idx[:, :, None, None]
    ci = col_idx[None, None, :, :]
    kl = kg[:, ri, ci]
    vl = vg[:, ri, ci]
    qb = q.reshape(bsz, rows, ncb, NA_QB, nh, dh)
    scale = HEAD_DIM ** -0.5
    s_loc = jnp.einsum('brnqhd,brinkhd->bhrnqik', qb, kl).astype(jnp.float32) * scale
    dr_i = (row_idx - r[:, None]) + (NA_KH - 1)
    dc_i = jnp.clip(kcol - qcol[:, :, None] + (NA_KW - 1), 0, 2 * NA_KW - 2)
    bias = rpb[:, dr_i[:, None, None, :, None], dc_i[None, :, :, None, :]]
    s_loc = s_loc + bias[None].astype(jnp.float32)
    s_loc = jnp.where(valid[None, None, None, :, :, None, :], s_loc, NEG_INF)
    s_ctx = jnp.einsum('brnqhd,bkhd->bhrnqk', qb, k_ctx).astype(jnp.float32) * scale
    n_loc = kh * NA_KB
    s = jnp.concatenate([s_loc.reshape(bsz, nh, rows, ncb, NA_QB, n_loc), s_ctx], axis=-1)
    p = jax.nn.softmax(s, axis=-1).astype(v.dtype)
    p_loc = p[..., :n_loc].reshape(bsz, nh, rows, ncb, NA_QB, kh, NA_KB)
    p_ctx = p[..., n_loc:]
    o = (jnp.einsum('bhrnqik,brinkhd->brnqhd', p_loc, vl)
         + jnp.einsum('bhrnqk,bkhd->brnqhd', p_ctx, v_ctx))
    return o.reshape(bsz, n, nh, dh)

def chunk_gating_mlp(u, vm, g_v, w_s, b_s):
    bsz, n, _ = u.shape
    u = jax.nn.gelu(u)
    vm = rms_norm(jax.nn.gelu(vm), g_v)
    vc = vm.reshape(bsz, n // CHUNK, CHUNK, H_CMLP, HEAD_DIM)
    mixed = jnp.einsum('hpq,bcqhd->bcphd', w_s, vc) + b_s.T[None, None, :, :, None]
    return u * mixed.reshape(bsz, n, D_CMLP)

def short_gated_conv(bg, cg, hx, w_conv):
    z = cg * hx
    n = z.shape[1]
    pad = CONV_W // 2
    zp = jnp.pad(z, ((0, 0), (pad, pad), (0, 0)))
    y = sum(zp[:, j:j + n] * w_conv[:, j] for j in range(CONV_W))
    return bg * y

def token_mixer(h, w_in, w_out, g_v, w_s, b_s, w_conv, attend):
    bsz, n, _ = h.shape
    q, k, v, u, vm, bg, cg, hx = split_projection(h @ w_in)
    q = q.reshape(bsz, n, H_ATT, HEAD_DIM)
    k = k.reshape(bsz, n, H_ATT, HEAD_DIM)
    v = v.reshape(bsz, n, H_ATT, HEAD_DIM)
    o_att = attend(q, k, v).reshape(bsz, n, D_ATT)
    o_mlp = chunk_gating_mlp(u, vm, g_v, w_s, b_s)
    o_conv = short_gated_conv(bg, cg, hx, w_conv)
    y = jnp.concatenate([o_att, o_mlp, o_conv], axis=-1) @ w_out
    return y, k, v

def swiglu(x, w_gu, w_d):
    g, u = jnp.split(x @ w_gu, 2, axis=-1)
    return (jax.nn.silu(g) * u) @ w_d

def moe_swiglu(x, w_router, w_gu, w_d):
    t = x.reshape(-1, D_MODEL)
    logits = (t @ w_router).astype(jnp.float32)
    top_v, top_i = lax.top_k(logits, TOP_K)
    gates = jax.nn.softmax(top_v, axis=-1)
    combine = jnp.sum(jax.nn.one_hot(top_i, N_EXPERTS, dtype=jnp.float32) * gates[..., None], axis=-2)
    combine = combine.astype(x.dtype)
    out = jnp.zeros_like(t)
    for e in range(N_EXPERTS):
        out = out + combine[:, e:e + 1] * swiglu(t, w_gu[e], w_d[e])
    return out.reshape(x.shape)

def setup_inputs(seed: int = 0) -> dict:
    key = jax.random.key(seed)
    ks = jax.random.split(key, 24)
    nrm = lambda k, shape, s: jax.random.normal(k, shape, jnp.float32) * s
    cache_shape = (DEC_BATCH, DEPTH, PAST_LEN, H_ATT, HEAD_DIM)
    return {
        'x_prompt': nrm(ks[0], (BATCH, SEQ, D_MODEL), 1.0),
        'x_sample': nrm(ks[1], (DEC_BATCH, DEC_SEQ, D_MODEL), 1.0),
        'cache_k': nrm(ks[2], cache_shape, 1.0),
        'cache_v': nrm(ks[3], cache_shape, 1.0),
        'c': nrm(ks[4], (DEC_BATCH, D_MODEL), 1.0),
        'c_ctx': nrm(ks[5], (D_MODEL,), 1.0),
        'w_ada': nrm(ks[6], (DEPTH, D_MODEL, N_MOD * D_MODEL), 0.5 * D_MODEL ** -0.5),
        'b_ada': nrm(ks[7], (DEPTH, N_MOD * D_MODEL), 0.01),
        'norm_g': 1.0 + nrm(ks[8], (DEPTH, 4, D_MODEL), 0.01),
        'w_in': nrm(ks[9], (DEPTH, D_MODEL, D_IN), D_MODEL ** -0.5),
        'w_out': nrm(ks[10], (DEPTH, D_MIX, D_MODEL), D_MIX ** -0.5),
        'rpb': nrm(ks[11], (DEPTH, H_ATT, 2 * NA_KH - 1, 2 * NA_KW - 1), 0.1),
        'g_v': 1.0 + nrm(ks[12], (DEPTH, D_CMLP), 0.01),
        'w_s': nrm(ks[13], (DEPTH, H_CMLP, CHUNK, CHUNK), CHUNK ** -0.5),
        'b_s': 1.0 + nrm(ks[14], (DEPTH, H_CMLP, CHUNK), 0.01),
        'w_conv': nrm(ks[15], (DEPTH, D_CONV, CONV_W), CONV_W ** -0.5),
        'w_ffn_gu': nrm(ks[16], (N_DENSE, D_MODEL, 2 * D_FF), D_MODEL ** -0.5),
        'w_ffn_d': nrm(ks[17], (N_DENSE, D_FF, D_MODEL), D_FF ** -0.5),
        'w_router': nrm(ks[18], (N_MOE, D_MODEL, N_EXPERTS), D_MODEL ** -0.5),
        'w_moe_gu': nrm(ks[19], (N_MOE, N_EXPERTS, D_MODEL, 2 * D_FF), D_MODEL ** -0.5),
        'w_moe_d': nrm(ks[20], (N_MOE, N_EXPERTS, D_FF, D_MODEL), D_FF ** -0.5),
    }

def reference(x_prompt, x_sample, cache_k, cache_v, c, c_ctx, w_ada, b_ada, norm_g,
              w_in, w_out, rpb, g_v, w_s, b_s, w_conv, w_ffn_gu, w_ffn_d,
              w_router, w_moe_gu, w_moe_d):
    def run_layer(x, cvec, l, attend):
        mod = ada_modulation(cvec, w_ada[l], b_ada[l])
        sh_m, sc_m, gt_m, sh_f, sc_f, gt_f = (mod[:, i] for i in range(N_MOD))
        h = rms_norm(x, norm_g[l, 0]) * (1 + sc_m) + sh_m
        y, k, v = token_mixer(h, w_in[l], w_out[l], g_v[l], w_s[l], b_s[l], w_conv[l], attend)
        x = x + gt_m * rms_norm(y, norm_g[l, 1])
        h = rms_norm(x, norm_g[l, 2]) * (1 + sc_f) + sh_f
        if l % 2 == 0:
            f = swiglu(h, w_ffn_gu[l // 2], w_ffn_d[l // 2])
        else:
            f = moe_swiglu(h, w_router[l // 2], w_moe_gu[l // 2], w_moe_d[l // 2])
        x = x + gt_f * rms_norm(f, norm_g[l, 3])
        return x, k, v

    cvec_ctx = c_ctx[None]
    xp = x_prompt
    ks_list, vs_list = [], []
    for l in range(DEPTH):
        xp, k, v = run_layer(xp, cvec_ctx, l, context_attention)
        ks_list.append(k)
        vs_list.append(v)
    new_cache_k = jnp.stack(ks_list, axis=1)
    new_cache_v = jnp.stack(vs_list, axis=1)

    xs = x_sample
    for l in range(DEPTH):
        attend = functools.partial(neighbourhood_attention, k_ctx=cache_k[:, l], v_ctx=cache_v[:, l], rpb=rpb[l])
        xs, _, _ = run_layer(xs, c, l, attend)
    return (xp, xs, new_cache_k, new_cache_v)


_drawn_inputs = setup_inputs


def setup_inputs(seed=0):
    import zlib

    import numpy as np

    out = dict(_drawn_inputs(seed))
    spreads = {}
    factors = {'rpb': 200.0,
     'g_v': 141.561,
     'b_s': 200.0,
     'cache_k': 8.0,
     'cache_v': 5.527,
     'norm_g': 2.875}
    for name, (base, spread) in spreads.items():
        noise = np.random.default_rng([zlib.crc32(name.encode()), seed]).standard_normal(out[name].shape)
        drawn = base * np.exp(spread * noise) if base else spread * noise
        out[name] = __import__('jax').numpy.asarray(drawn.astype(out[name].dtype))
    for name, factor in factors.items():
        out[name] = (out[name] * factor).astype(out[name].dtype)
    return out
```

```python
from contextlib import ExitStack

import concourse.bass as bass
from concourse import mybir

F32 = mybir.dt.float32
F32R = mybir.dt.float32r
I32 = mybir.dt.int32
U32 = mybir.dt.uint32
ALU = mybir.AluOpType
ACT = mybir.ActivationFunctionType
AX_X = mybir.AxisListType.X

P = 128
NT = 3
D = 1024
KT = D // P
DEPTH = 2
HD = 64
NH = 8
D_ATT, D_CM, D_CV = 512, 256, 256
D_IN = 3 * D_ATT + 2 * D_CM + 3 * D_CV
OQ, OK, OV = 0, D_ATT, 2 * D_ATT
OU = 3 * D_ATT
OVM = OU + D_CM
OB = OVM + D_CM
OC = OB + D_CV
OH = OC + D_CV
D_FF = 2816
FK = D_FF // P
NE = 8
N_MOD = 6
EPS = 1e-6
NEG = -1e30
GW = 64
KH, KW = 8, 16
NDR = 6
ROWS = 4
SCALE = HD ** -0.5

CHUNK = 2048
RAW = 3
SPL = 3
ADA_B = N_MOD * D // 512
WIN_B = 6
N_ADA, N_WIN, N_WOUT = 2 * ADA_B, 11, 4
GU_B = D_FF // 256
N_GU, N_WD = 2 * GU_B, FK // 2
N_FFN = N_GU + N_WD
ADA0 = [0, N_ADA + N_WIN + N_WOUT + N_FFN]
WIN0 = [a + N_ADA for a in ADA0]
WOUT0 = [a + N_WIN for a in WIN0]
FFN0 = WOUT0[0] + N_WOUT
EXP0 = WOUT0[1] + N_WOUT
assert EXP0 % RAW == 0 and N_FFN % RAW == 0


def mix_col(kt):
    return [OQ, OQ + 128, OQ + 256, OQ + 384, OU, OU + 128, OB, OB + 128][kt]


def build(nc, x_prompt, x_sample, cache_k, cache_v, c, c_ctx, w_ada, b_ada, norm_g, w_in, w_out, rpb,
          g_v, w_s, b_s, w_conv, w_ffn_gu, w_ffn_d, w_router, w_moe_gu, w_moe_d,
          y_prompt, y_sample, new_k, new_v, x_park, rpb_pad):
    with ExitStack() as ctx:
        ctx.enter_context(nc.allow_non_contiguous_dma(reason="a few small vectors go to columns"))

        def sb(name, shape, dt=F32):
            return ctx.enter_context(nc.sbuf_tensor(name, shape, dt))

        def sem(name):
            return ctx.enter_context(nc.semaphore(name))

        raw = [sb(f"raw{i}", [P, CHUNK]) for i in range(RAW)]
        whi = [sb(f"whi{i}", [P, CHUNK], F32R) for i in range(SPL)]
        wlo = [sb(f"wlo{i}", [P, CHUNK], F32R) for i in range(SPL)]
        xhi = sb("xhi", [P, KT, NT * P], F32R)
        xlo = sb("xlo", [P, KT, NT * P], F32R)
        x = sb("x", [P, NT, D])
        f = sb("f", [P, NT, D])
        ident = sb("ident", [P, P])
        shift = sb("shift", [P, 4, P])
        iota = sb("iota", [P, NT * P])
        sel = sb("sel", [P, 2])
        selb = sb("selb", [P, 2, P])
        win_mask = sb("win_mask", [P, GW])
        sil = sb("sil", [P, KT, 2])
        silh = sb("silh", [P, KT, 2], F32R)
        sill = sb("sill", [P, KT, 2])
        gcol = sb("gcol", [P, DEPTH, 2, KT])
        modc = sb("modc", [P, 4, KT, 2])
        ss = sb("ss", [P, 10, NT])
        rs = sb("rs", [P, 10, NT])
        nm = sb("nm", [P, 2, 2])
        den = sb("den", [P, 2])
        rden = sb("rden", [P, 2])
        gate_f = sb("gate_f", [P, D])
        arena = nc.sbuf_base
        arena += -arena % 64
        end = [arena]

        def at(name, off, shape, dt=F32):
            n = 4
            for s in shape[1:]:
                n *= s
            end[0] = max(end[0], arena + off + n)
            assert arena + off + n <= nc.sbuf_usable_end, (name, arena + off + n, nc.sbuf_usable_end)
            return nc.alloc_sbuf_tensor_at(name, shape, dt, offset=arena + off)

        hf = at("hf", 0, [P, KT, NT * P])
        pr = at("pr", 0, [P, NT, D_IN])
        qT = at("qT", 33792, [P, 4, NT * P])
        kT = at("kT", 39936, [P, 4, NT * P])
        modrow = at("modrow", 33792, [P, 2, 512])
        ckT = at("ckT", 46080, [P, 4, P])
        bias = at("bias", 48128, [P, NH, NDR * GW])
        cv = at("cv", 60416, [P, D_ATT])
        pS = at("pS", 62464, [P, 2, 384])
        ck = at("ck", 62464, [P, D_ATT])
        pT = at("pT", 65536, [P, 2, 384])
        z = at("z", 65536, [P, NT, D_CV])
        cS = at("cS", 62464, [P, KT, P], F32R)
        ws = at("ws", 39936, [P, 4, P])
        wsT = at("wsT", 68608, [P, 4, P])
        gvb = at("gvb", 70656, [P, D_CM])
        wcb = at("wcb", 71680, [P, D_CV, 3])
        bs = at("bs", 74752, [P, 4])
        gate_m = at("gate_m", 74784, [P, D])
        hhi = at("hhi", 0, [P, FK, NT * P], F32R)
        hlo = at("hlo", 33792, [P, FK, NT * P], F32R)
        pg = at("pg", 67584, [P, NT, 256])
        perm = at("perm", 70656, [P, NT, NT * P])
        yhi = at("yhi", 0, [P, NT, D], F32R)
        ylo = at("ylo", 12288, [P, NT, D], F32R)
        permT = at("permT", 24576, [P, NT, NT * P], F32R)
        wr = at("wr", 33792, [P, KT, NE])
        lg = at("lg", 34048, [P, NT, NE])
        m8 = at("m8", 34144, [P, NT, NE])
        ix = at("ix", 34240, [P, NT, NE], U32)
        ixf = at("ixf", 34336, [P, NT, NE])
        hot = at("hot", 34432, [P, NT, NE])
        ge = at("ge", 34528, [P, NT, 4])
        hot1 = at("hot1", 34624, [P, NT, NE])
        rt = at("rt", 75264, [P, 3, NT, NE])
        cnt = at("cnt", 75264 + 288, [P, NE])
        ntile = at("ntile", 75264 + 320, [P, NE], I32)
        cur = at("cur", 75264 + 352, [P, 3, NT])
        ones = at("ones", 75904, [P, P])
        before = at("before", 76416, [P, P])
        pad = at("pad", 60416, [P, 127])

        ps = ctx.enter_context(nc.psum_tensor("ps", [P, 8, 512], F32))

        s_const = sem("s_const")
        s_x = sem("s_x")
        s_c = sem("s_c")
        s_gcol = sem("s_gcol")
        s_raw = [sem(f"s_raw{i}") for i in range(RAW)]
        s_hi = sem("s_hi")
        s_lo = sem("s_lo")
        s_pe = sem("s_pe")
        s_dv = sem("s_dv")
        s_ac = sem("s_ac")
        s_po = sem("s_po")
        s_sil = sem("s_sil")
        s_cs = sem("s_cs")
        s_brz = sem("s_brz")
        s_brow = [sem(f"s_brow{i}") for i in range(2)]
        s_gb = sem("s_gb")
        s_ada = sem("s_ada")
        s_modr = sem("s_modr")
        s_colmm = sem("s_colmm")
        s_modc = sem("s_modc")
        s_ss = sem("s_ss")
        s_ms = sem("s_ms")
        s_sq = sem("s_sq")
        s_xn = sem("s_xn")
        s_tr = sem("s_tr")
        s_hf = sem("s_hf")
        s_xhi = sem("s_xhi")
        s_xlo = sem("s_xlo")
        s_win = sem("s_win")
        s_pr = sem("s_pr")
        s_kv = sem("s_kv")
        s_ld = [[sem(f"s_ld{l}_{n}") for n in range(6)] for l in range(DEPTH)]
        s_pad = sem("s_pad")
        s_bias = sem("s_bias")
        s_gel = sem("s_gel")
        s_wsp = sem("s_wsp")
        s_wst = sem("s_wst")
        s_vn = sem("s_vn")
        s_mix = sem("s_mix")
        s_cm = sem("s_cm")
        s_z = sem("s_z")
        s_sh = sem("s_sh")
        s_cvd = sem("s_cvd")
        s_qk = sem("s_qk")
        s_qka = sem("s_qka")
        s_qkd = sem("s_qkd")
        s_sc = sem("s_sc")
        s_sm = sem("s_sm")
        s_ex = sem("s_ex")
        s_pt = sem("s_pt")
        s_ptc = sem("s_ptc")
        s_pv = sem("s_pv")
        s_o = sem("s_o")
        s_mt = sem("s_mt")
        s_mhi = sem("s_mhi")
        s_mlo = sem("s_mlo")
        s_y = sem("s_y")
        s_yc = sem("s_yc")
        s_gt = sem("s_gt")
        s_xr = sem("s_xr")
        s_gu = sem("s_gu")
        s_sg = sem("s_sg")
        s_pm = sem("s_pm")
        s_ht = sem("s_ht")
        s_hhi = sem("s_hhi")
        s_hlo = sem("s_hlo")
        s_yf = sem("s_yf")
        s_park = sem("s_park")
        s_back = sem("s_back")
        s_wr = sem("s_wr")
        s_bt = sem("s_bt")
        s_btc = sem("s_btc")
        s_lg = sem("s_lg")
        s_rt = sem("s_rt")
        s_rte = sem("s_rte")
        s_hot = sem("s_hot")
        s_cur = sem("s_cur")
        s_tri = sem("s_tri")
        s_pos = sem("s_pos")
        s_nt = sem("s_nt")
        s_perm = sem("s_perm")
        s_ga = sem("s_ga")
        s_ghi = sem("s_ghi")
        s_glo = sem("s_glo")
        s_yhi = sem("s_yhi")
        s_ylo = sem("s_ylo")
        s_pmt = sem("s_pmt")
        s_pmc = sem("s_pmc")
        s_scm = sem("s_scm")
        s_acc = sem("s_acc")
        s_out = sem("s_out")

        N_CONST = 10

        UNITS = [(0, h) for h in range(NH)] + [(t, h) for t in (1, 2) for h in range(NH)]
        NU = len(UNITS)

        def chunk_src(n):
            def rows(w, k):
                w = w.rearrange("(k p) n -> p k n", p=P)
                return [w[:, 0:k // 2, :], w[:, k // 2:k, :]], k

            for l in range(DEPTH):
                if ADA0[l] <= n < ADA0[l] + N_ADA:
                    b, h = divmod(n - ADA0[l], 2)
                    return rows(w_ada[l, 512 * h:512 * h + 512, 512 * b:512 * b + 512], 4)
                if WIN0[l] <= n < WIN0[l] + N_WIN:
                    b, h = divmod(n - WIN0[l], 2)
                    if b == 5:
                        return rows(w_in[l, :, 2560:2816], 8)
                    return rows(w_in[l, 512 * h:512 * h + 512, 512 * b:512 * b + 512], 4)
                if WOUT0[l] <= n < WOUT0[l] + N_WOUT:
                    q = n - WOUT0[l]
                    return rows(w_out[l, 256 * q:256 * q + 256, :], 2)
            return ffn_src(w_ffn_gu[0], w_ffn_d[0], n - FFN0)

        def ffn_src(gu, dn, j):
            if j < N_GU:
                b, h = divmod(j, 2)
                v = gu.rearrange("(k p) n -> p k n", p=P)
                return [v[:, 4 * h:4 * h + 4, o + 256 * b:o + 256 * b + 256] for o in (0, D_FF)], 0
            q = j - N_GU
            v = dn.rearrange("(k p) n -> p k n", p=P)
            return [v[:, 2 * q:2 * q + 1, :], v[:, 2 * q + 1:2 * q + 2, :]], 2

        def raw_parts(i, k):
            if k == 0:
                v = raw[i][:, :].rearrange("p (k n) -> p k n", k=4)
                return [v[:, :, 0:256], v[:, :, 256:512]]
            v = raw[i][:, :].rearrange("p (k n) -> p k n", k=k)
            return [v[:, 0:k // 2, :], v[:, k // 2:k, :]]

        class Chain:

            def __init__(self, eng, s):
                self.eng, self.s, self.n = eng, s, 0

            def __call__(self, ins):
                self.n += 1
                ins.then_inc(self.s, 1)
                self.eng.wait_ge(self.s, self.n)

        block = ctx.enter_context(nc.Block())

        @block.sync
        def _(sp):
            def load(n):
                if n >= RAW:
                    sp.wait_ge(s_lo, n - RAW + 1)
                src, k = chunk_src(n)
                for to, of in zip(raw_parts(n % RAW, k), src):
                    sp.dma_start(to, of).then_inc(s_raw[n % RAW], 16)

            sp.dma_start(sil[:, :, 0], c_ctx.rearrange("(k p) -> p k", p=P)).then_inc(s_c, 16)
            sp.dma_start(sil[:, :, 1], c[0].rearrange("(k p) -> p k", p=P)).then_inc(s_c, 16)
            for n in range(RAW):
                load(n)
            sp.dma_start(x[:, 0, :], x_prompt[0]).then_inc(s_x, 16)
            sp.dma_start(x[:, 1:3, :], x_sample[0].rearrange("(t p) d -> p t d", p=P)).then_inc(s_x, 16)
            for n in range(RAW, EXP0):
                load(n)
            with sp.Fori(0, NE) as e:
                gu = w_moe_gu[0, bass.ds(e, 1), :, :].rearrange("e k n -> (e k) n")
                dn = w_moe_d[0, bass.ds(e, 1), :, :].rearrange("e k n -> (e k) n")
                for j in range(N_FFN):
                    sp.wait_ge(s_lo, e * N_FFN + (EXP0 + j - RAW + 1))
                    src, k = ffn_src(gu, dn, j)
                    for to, of in zip(raw_parts(j % RAW, k), src):
                        sp.dma_start(to, of).then_inc(s_raw[j % RAW], 16)

        @block.gpsimd
        def _(pool):
            chain = Chain(pool, s_po)
            for l in range(DEPTH):
                for i in range(2):
                    pool.dma_start(gcol[:, l, i, :], norm_g[l, 2 * i].rearrange("(k p) -> p k", p=P)
                                   ).then_inc(s_gcol, 16)

            const = Chain(pool, s_const)
            chain(pool.memset(ident[:, :], 0.0))
            chain(pool.memset(shift[:, :, :], 0.0))
            chain(pool.memset(sel[:, :], 0.0))
            chain(pool.memset(win_mask[:, :], 0.0))
            const(pool.iota(iota[:, :], [[1, NT * P]], base=0, channel_multiplier=0,
                            allow_small_or_imprecise_dtypes=True))
            const(pool.affine_select(out=ident[:, :], in_=ident[:, :], compare_op=ALU.not_equal, fill=1.0,
                                     base=0, pattern=[[-1, P]], channel_multiplier=1))
            for i, base in enumerate((1, -1, -(P - 1), P - 1)):
                const(pool.affine_select(out=shift[:, i, :], in_=shift[:, i, :], compare_op=ALU.not_equal,
                                         fill=1.0, base=base, pattern=[[-1, P]], channel_multiplier=1))
            for o in (0, 64):
                chain(pool.affine_select(out=sel[:, :], in_=sel[:, :], compare_op=ALU.not_equal, fill=1.0,
                                         base=-o, pattern=[[-32, 2]], channel_multiplier=1))
            for g in range(2):
                const(pool.tensor_copy(selb[:, g, :], sel[:, g:g + 1].to_broadcast([P, P])))
            for o in (0, GW):
                m = win_mask[o:o + GW, 0:GW - KW]
                chain(pool.affine_select(out=m, in_=m, compare_op=ALU.is_ge, fill=NEG, base=KW // 2,
                                         pattern=[[1, GW - KW]], channel_multiplier=-1))
                m = win_mask[o:o + GW, KW:GW]
                const(pool.affine_select(out=m, in_=m, compare_op=ALU.is_ge, fill=NEG, base=KW // 2 - 1 - KW,
                                         pattern=[[-1, GW - KW]], channel_multiplier=1))

            for l in range(DEPTH):
                if l:
                    pool.wait_ge(s_xr, 6)
                chain(pool.memset(f[:, 2, :], 0.0))
                pool.dma_start(f[:, 0, :], bass.AP(norm_g.tensor, norm_g[l, 1, :].offset, [[0, P], [1, D]])
                               ).then_inc(s_gb, 16)
                pool.dma_start(f[:, 1, :], bass.AP(norm_g.tensor, norm_g[l, 3, :].offset, [[0, P], [1, D]])
                               ).then_inc(s_gb, 16)

                def brow(b):
                    if b >= 2:
                        pool.wait_ge(s_modr, ADA_B * l + b - 1)
                    o = b_ada[l, 512 * b:512 * b + 512].offset
                    pool.dma_start(f[0:33:32, 2, 512 * (b % 2):512 * (b % 2) + 512],
                                   bass.AP(b_ada.tensor, o, [[0, 2], [1, 512]])).then_inc(s_brow[b % 2], 16)

                brow(0)
                brow(1)
                chain(pool.memset(pad[:, :], NEG))
                for h in range(NH):
                    pool.dma_start(pad[7 * h:7 * h + 7, 48:79], rpb[l, h, 4:11, :]).then_inc(s_pad, 16)
                pool.wait_ge(s_pad, (16 * NH + 16) * (l + 1) - 16)
                pool.dma_start(rpb_pad[l], pad[0:56, :].rearrange("p (a k) -> p a k", a=1).to_broadcast([56, GW, 127])
                               ).then_inc(s_pad, 16)
                pool.wait_ge(s_pad, (16 * NH + 16) * (l + 1))
                for h in range(NH):
                    for r2 in range(2):
                        o = rpb_pad[l].offset + (7 * h + 1 - r2) * GW * 127 + GW - 1
                        pool.dma_start(bias[GW * r2:GW * r2 + GW, h, :].rearrange("p (m k) -> p m k", m=NDR),
                                       bass.AP(rpb_pad.tensor, o, [[126, GW], [GW * 127, NDR], [1, GW]])
                                       ).then_inc(s_ld[l][0], 16)
                pool.dma_start(ws[:, :, :], w_s[l].rearrange("h p q -> p h q")).then_inc(s_ld[l][1], 16)
                pool.dma_start(gvb[:, :], bass.AP(g_v.tensor, g_v[l].offset, [[0, P], [1, D_CM]])
                               ).then_inc(s_ld[l][2], 16)
                pool.dma_start(bs[:, :], b_s[l].rearrange("h p -> p h")).then_inc(s_ld[l][2], 16)
                pool.dma_start(wcb[:, :, :].rearrange("p c j -> p (c j)"),
                               bass.AP(w_conv.tensor, w_conv[l].offset, [[0, P], [1, 3 * D_CV]])
                               ).then_inc(s_ld[l][3], 16)
                pool.dma_start(cv[:, :], cache_v[0, l].rearrange("p h d -> p (h d)")).then_inc(s_ld[l][5], 16)
                for b in range(2, ADA_B):
                    brow(b)
                pool.wait_ge(s_modc, l + 1)
                pool.dma_start(ck[:, :], cache_k[0, l].rearrange("p h d -> p (h d)")).then_inc(s_ld[l][4], 16)
            pool.wait_ge(s_xr, 9)
            pool.dma_start(x_park.rearrange("(t p) d -> p t d", p=P), x[:, :, :]).then_inc(s_park, 16)
            pool.dma_start(wr[:, :, :], w_router[0].rearrange("(k p) e -> p k e", p=P)).then_inc(s_wr, 16)
            chain(pool.memset(ones[:, :], 1.0))
            chain(pool.memset(before[:, :], 1.0))
            pool.affine_select(out=before[:, :], in_=before[:, :], compare_op=ALU.is_gt, fill=0.0, base=0,
                               pattern=[[1, P]], channel_multiplier=-1).then_inc(s_tri, 1)
            pool.wait_ge(s_acc, NT * NE + 1)
            pool.wait_ge(s_park, 16)
            pool.dma_start(x[:, :, :], x_park.rearrange("(t p) d -> p t d", p=P)).then_inc(s_back, 16)

        @block.scalar
        def _(act):
            chain = Chain(act, s_ac)
            state = {"n": 0}

            def split(n, j=None):
                s = (n if j is None else j) % SPL
                if j is None:
                    act.wait_ge(s_raw[s], 32 * (n // RAW + 1))
                    if n >= SPL:
                        act.wait_ge(s_pe, n - SPL + 1)
                else:
                    e = n
                    act.wait_ge(s_raw[s], e * (32 * N_FFN // RAW) + 32 * ((EXP0 + j) // RAW + 1))
                    act.wait_ge(s_pe, e * N_FFN + (EXP0 + j - SPL + 1))
                act.activation(whi[s][:, :], raw[s][:, :], ACT.Copy).then_inc(s_hi, 1)

            def upto(n):
                while state["n"] <= min(n, EXP0 + 1):
                    split(state["n"])
                    state["n"] += 1

            def rms(r, src, width):
                for t in range(NT):
                    ins = act.activation(src[1][t], src[0][t], ACT.Square, accum_out=ss[:, r, t:t + 1])
                ins.then_inc(s_ss, 1)
                act.wait_ge(s_ms, r + 1)
                act.activation(ss[:, r, :], rs[:, r, :], ACT.Sqrt).then_inc(s_sq, 1)

            def norm(s, l, half):
                r = 5 * l + 3 * half
                if s:
                    act.wait_ge(s_xr, 3 * s)
                else:
                    act.wait_ge(s_x, 32)
                if half == 0:
                    act.wait_ge(s_modc, l + 1)
                rms(r, ([x[:, t, :] for t in range(NT)], [f[:, t, :] for t in range(NT)]), D)
                act.wait_ge(s_modc, l + 1)
                for kt in range(KT):
                    act.wait_ge(s_tr, KT * s + kt + 1)
                    p6 = ps[:, 6 + kt % 2, :]
                    sh, sc = modc[:, 2 * half, kt, :], modc[:, 2 * half + 1, kt, :]
                    act.activation(hf[:, kt, 0:P], p6[:, 0:P], ACT.Identity, bias=sh[:, 0:1], scale=sc[:, 0:1])
                    ins = act.activation(hf[:, kt, P:3 * P], p6[:, P:3 * P], ACT.Identity,
                                         bias=sh[:, 1:2], scale=sc[:, 1:2])
                    ins.then_inc(s_hf, 1)
                    if s == 3:
                        continue
                    act.wait_ge(s_hf, KT * s + kt + 1)
                    act.activation(xhi[:, kt, :], hf[:, kt, :], ACT.Copy).then_inc(s_xhi, 1)

            def residual(s, l, half, n_next):
                r = 5 * l + 2 + 2 * half
                if s < 3:
                    for t in range(NT):
                        if t < NT - 1:
                            act.wait_ge(s_y, 2 * s + t + 1)
                        else:
                            act.wait_ge(s_pe, (WOUT0[l] + N_WOUT) if half == 0 else FFN0 + N_FFN)
                        act.activation(f[:, t, :], ps[:, 2 * t:2 * t + 2, :].rearrange("p a n -> p (a n)"),
                                       ACT.Copy).then_inc(s_yc, 1)
                    act.wait_ge(s_yc, NT * (s + 1))
                else:
                    act.wait_ge(s_acc, NT * NE + 1)
                flat = hf[:, :, :].rearrange("p a n -> p (a n)")
                junk = [flat[:, D * t:D * t + D] for t in range(NT)]
                rms(r, ([f[:, t, :] for t in range(NT)], junk), D)

            act.wait_ge(s_c, 32)
            chain(act.activation(sil[:, :, :], sil[:, :, :], ACT.Silu))
            act.activation(silh[:, :, :], sil[:, :, :], ACT.Copy).then_inc(s_sil, 1)

            def ffn(T, k, n0, e=None):
                def ahead(j):
                    if e is None:
                        upto(n0 + j)
                    else:
                        while state["j"] <= min(j, N_FFN - 1):
                            split(e, state["j"])
                            state["j"] += 1

                state["j"] = 2

                def hi(b):
                    for i in range(2):
                        act.wait_ge(s_ht, k * 2 * GU_B + 2 * b + i + 1)
                        act.activation(hhi[:, 2 * b + i, 0:P * T], ps[:, 6 + i, 0:P * T], ACT.Copy
                                       ).then_inc(s_hhi, 1)

                for b in range(GU_B):
                    ahead(2 * b + 3)
                    if e is None:
                        act.wait_ge(s_pe, n0 + 2 * b + 2)
                    else:
                        act.wait_ge(s_pe, e * N_FFN + (EXP0 + 2 * b + 2))
                    if b:
                        act.wait_ge(s_ht, k * 2 * GU_B + 2 * b)
                    for t in range(T):
                        ins = act.activation(pg[:, t, :], ps[:, 2 * t + b % 2, 0:256], ACT.Silu)
                    ins.then_inc(s_sg, 1)
                    if b:
                        hi(b - 1)
                hi(GU_B - 1)
                for j in range(N_GU, N_FFN):
                    ahead(j)

            def expert(T, e):
                k = e + 1
                for kt in range(KT):
                    act.wait_ge(s_ga, e * KT + kt + 1)
                    act.activation(xhi[:, kt, 0:P * T], ps[:, 6 + kt % 2, 0:P * T], ACT.Copy).then_inc(s_ghi, 1)
                ffn(T, k, None, e)
                act.wait_ge(s_pe, e * N_FFN + (EXP0 + N_FFN))
                for t in range(T):
                    ins = act.activation(yhi[:, t, :], ps[:, 2 * t:2 * t + 2, :].rearrange("p a n -> p (a n)"),
                                         ACT.Copy)
                ins.then_inc(s_yhi, 1)
                for t in range(T):
                    act.wait_ge(s_pmt, e * NT + t + 1)
                    act.activation(permT[:, t, :], ps[:, 6 + t % 2, 0:NT * P], ACT.Copy).then_inc(s_pmc, 1)
                if T < NT:
                    act.wait_ge(s_pmc, e * NT + T)
                    act.sem_inc(s_pmc, NT - T)

            for l in range(DEPTH):
                upto(WIN0[l] + 1)
                norm(2 * l, l, 0)
                for b in range(WIN_B):
                    upto(WIN0[l] + 2 * b + 3 if b < 5 else WIN0[l] + N_WIN + 1)
                    w = 512 if b < 5 else 256
                    for t in range(NT):
                        if t < NT - 1:
                            act.wait_ge(s_win, 2 * WIN_B * l + 2 * b + t + 1)
                        else:
                            act.wait_ge(s_pe, WIN0[l] + min(2 * b + 2, N_WIN))
                        act.activation(pr[:, t, 512 * b:512 * b + w], ps[:, 2 * t + b % 2, 0:w], ACT.Copy
                                       ).then_inc(s_pr, 1)
                    if b == 2:
                        act.wait_ge(s_pr, NT * WIN_B * l + 9)
                        act.dma_start(new_k[0, l].rearrange("p h d -> p (h d)"), pr[:, 0, OK:OK + D_ATT]
                                      ).then_inc(s_kv, 16)
                        act.dma_start(new_v[0, l].rearrange("p h d -> p (h d)"), pr[:, 0, OV:OV + D_ATT]
                                      ).then_inc(s_kv, 16)
                act.wait_ge(s_pr, NT * WIN_B * (l + 1))
                act.activation(pr[:, :, OU:OU + 512], pr[:, :, OU:OU + 512], ACT.Gelu_apprx_tanh).then_inc(s_gel, 1)
                act.wait_ge(s_gel, l + 1)
                rms(5 * l + 1, ([pr[:, t, OVM:OVM + D_CM] for t in range(NT)],
                                [f[:, t, 0:D_CM] for t in range(NT)]), D_CM)
                for i in range(0, 9, 2):
                    act.wait_ge(s_qk, 9 * l + i + 1)
                    if i == 8:
                        dst, w = ckT[:, :, :].rearrange("p a n -> p (a n)"), 4 * P
                    else:
                        dst, w = (qT if i < 4 else kT)[:, i % 4, :], NT * P
                    act.activation(dst, ps[:, 6 + i % 2, 0:w], ACT.Copy).then_inc(s_qka, 1)

                def exp(u):
                    w = P if UNITS[u][0] == 0 else 384
                    act.wait_ge(s_sm, NU * l + u + 1)
                    if u >= 2:
                        act.wait_ge(s_o, NU * l + u - 1)
                    act.activation(pS[:, u % 2, 0:w], pS[:, u % 2, 0:w], ACT.Exp, bias=nm[:, u % 2, 1:2],
                                   accum_out=den[:, u % 2:u % 2 + 1]).then_inc(s_ex, 1)

                def pt_copy(u):
                    w = P if UNITS[u][0] == 0 else 384
                    act.wait_ge(s_pt, NU * l + u + 1)
                    if u >= 2:
                        act.wait_ge(s_pv, NU * l + u - 1)
                    act.activation(pT[:, u % 2, 0:w], ps[:, 2 + u % 2, 0:w], ACT.Copy).then_inc(s_ptc, 1)

                for u in range(NU + 1):
                    if u < NU:
                        exp(u)
                    if u >= 1:
                        pt_copy(u - 1)
                for kt in range(KT):
                    act.wait_ge(s_mt, KT * l + kt + 1)
                    act.activation(xhi[:, kt, :], ps[:, 6 + kt % 2, 0:384], ACT.Copy).then_inc(s_mhi, 1)
                upto(WOUT0[l] + N_WOUT + 1)
                act.wait_ge(s_kv, 32 * (l + 1))
                residual(2 * l, l, 0, None)
                norm(2 * l + 1, l, 1)
                if l == 0:
                    upto(FFN0 + 1)
                    ffn(NT, 0, FFN0)
                    upto(ADA0[1] + 1)
                    residual(1, 0, 1, None)
            act.wait_ge(s_park, 16)
            for i in range(6):
                act.wait_ge(s_bt, i + 1)
                t, h = divmod(i, 2)
                act.activation(x[:, t, 512 * h:512 * h + 512], ps[:, 6 + i % 2, :], ACT.Copy).then_inc(s_btc, 1)
            for t in range(NT):
                act.wait_ge(s_rt, 1)
                ins = act.activation(ge[:, t, 1:2], ge[:, t, 0:1], ACT.Exp)
            ins.then_inc(s_rte, 1)
            upto(EXP0 + 1)
            act.wait_ge(s_nt, 1)
            with act.Fori(0, NE) as e:
                T = act.value_load(ntile[0:1, bass.ds(e, 1)], min_val=1, max_val=3)
                with act.If(T < 2):
                    expert(1, e)
                with act.Else():
                    with act.If(T < 3):
                        expert(2, e)
                    with act.Else():
                        expert(3, e)
                with act.If(e < NE - 1):
                    split(e + 1, 0)
                    split(e + 1, 1)
            residual(3, 1, 1, None)
            for t in range(NT):
                act.wait_ge(s_xr, 9 + t + 1)
                out = y_prompt[0] if t == 0 else y_sample[0, P * (t - 1):P * t, :]
                act.dma_start(out, x[:, t, :]).then_inc(s_out, 16)
            act.wait_ge(s_out, 48)

        @block.vector
        def _(dve):
            chain = Chain(dve, s_dv)
            state = {"n": 0}

            def split(n, j=None):
                s = (n if j is None else j) % SPL
                if j is None:
                    dve.wait_ge(s_hi, n + 1)
                else:
                    dve.wait_ge(s_hi, n * N_FFN + (EXP0 + j + 1))
                dve.tensor_tensor(wlo[s][:, :], raw[s][:, :], whi[s][:, :].bitcast(F32), ALU.subtract
                                  ).then_inc(s_lo, 1)

            def upto(n):
                while state["n"] <= min(n, EXP0 + 1):
                    split(state["n"])
                    state["n"] += 1

            def rms(r, width):
                dve.wait_ge(s_ss, r + 1)
                dve.tensor_scalar(rs[:, r, :], ss[:, r, :], 1.0 / width, EPS, ALU.mult, ALU.add).then_inc(s_ms, 1)
                dve.wait_ge(s_sq, r + 1)
                chain(dve.reciprocal(rs[:, r, :], ss[:, r, :]))

            def norm(s, l, half):
                r = 5 * l + 3 * half
                rms(r, D)
                for t in range(NT):
                    dve.tensor_scalar(f[:, t, :], x[:, t, :], rs[:, r, t:t + 1], None, ALU.mult).then_inc(s_xn, 1)
                for kt in range(KT if s < 3 else 0):
                    dve.wait_ge(s_xhi, KT * s + kt + 1)
                    dve.tensor_tensor(xlo[:, kt, :], hf[:, kt, :], xhi[:, kt, :].bitcast(F32), ALU.subtract
                                      ).then_inc(s_xlo, 1)

            def residual(s, l, half):
                r = 5 * l + 2 + 2 * half
                rms(r, D)
                for t in range(NT):
                    g = min(t, 1)
                    dve.wait_ge(s_gt, 2 * s + g + 1)
                    if s == 3 and t == 0:
                        dve.wait_ge(s_back, 16)
                    chain(dve.scalar_tensor_tensor(
                        out=f[:, t, :], in0=f[:, t, :], scalar=rs[:, r, t:t + 1],
                        in1=ps[:, 2 * g:2 * g + 2, :].rearrange("p a n -> p (a n)"), op0=ALU.mult, op1=ALU.mult))
                    dve.tensor_tensor(x[:, t, :], x[:, t, :], f[:, t, :], ALU.add).then_inc(s_xr, 1)

            dve.wait_ge(s_sil, 1)
            chain(dve.tensor_tensor(sill[:, :, :], sil[:, :, :], silh[:, :, :].bitcast(F32), ALU.subtract))

            def ffn(T, k, n0, e=None):
                def ahead(j):
                    if e is None:
                        upto(n0 + j)
                    else:
                        while state["j"] <= min(j, N_FFN - 1):
                            split(e, state["j"])
                            state["j"] += 1

                state["j"] = 2

                def lo(b):
                    for i in range(2):
                        dve.wait_ge(s_hhi, k * 2 * GU_B + 2 * b + i + 1)
                        dve.tensor_tensor(hlo[:, 2 * b + i, 0:P * T], ps[:, 6 + i, 0:P * T],
                                          hhi[:, 2 * b + i, 0:P * T].bitcast(F32), ALU.subtract).then_inc(s_hlo, 1)

                for b in range(GU_B):
                    ahead(2 * b + 3)
                    dve.wait_ge(s_sg, k * GU_B + b + 1)
                    for t in range(T):
                        ins = dve.tensor_tensor(pg[:, t, :], pg[:, t, :], ps[:, 2 * t + b % 2, 256:512], ALU.mult)
                    ins.then_inc(s_pm, 1)
                    if b:
                        lo(b - 1)
                lo(GU_B - 1)
                for j in range(N_GU, N_FFN):
                    ahead(j)

            def expert(T, e):
                k = e + 1
                dve.wait_ge(s_cur, e + 1)
                for t in range(NT):
                    ins = dve.tensor_scalar(perm[:, t, 0:P * T], iota[:, 0:P * T], cur[:, 1, t:t + 1],
                                            cur[:, 2, t:t + 1], ALU.is_equal, ALU.mult)
                ins.then_inc(s_perm, 1)
                for kt in range(KT):
                    dve.wait_ge(s_ghi, e * KT + kt + 1)
                    dve.tensor_tensor(xlo[:, kt, 0:P * T], ps[:, 6 + kt % 2, 0:P * T],
                                      xhi[:, kt, 0:P * T].bitcast(F32), ALU.subtract).then_inc(s_glo, 1)
                ffn(T, k, None, e)
                dve.wait_ge(s_yhi, e + 1)
                for t in range(T):
                    ins = dve.tensor_tensor(ylo[:, t, :], ps[:, 2 * t:2 * t + 2, :].rearrange("p a n -> p (a n)"),
                                            yhi[:, t, :].bitcast(F32), ALU.subtract)
                ins.then_inc(s_ylo, 1)

            for l in range(DEPTH):
                if l:
                    dve.wait_ge(s_xr, 6)
                for i in range(4):
                    src = silh[:, :, :].bitcast(F32) if i < 2 else sill[:, :, :]
                    g = i % 2
                    ins = dve.tensor_copy(cS[:, :, 32 * i:32 * i + 32], src[:, :, g:g + 1].to_broadcast([P, KT, 32]))
                ins.then_inc(s_cs, 1)
                dve.wait_ge(s_gb, 32 * (l + 1))
                for b in range(ADA_B):
                    upto(ADA0[l] + min(2 * b + 3, N_ADA - 1))
                    mod, h = divmod(b, 2)
                    dve.wait_ge(s_pe, ADA0[l] + 2 * b + 2)
                    dve.wait_ge(s_brow[b % 2], 16 * (ADA_B // 2 * l + b // 2 + 1))
                    row = f[:, 2, 512 * (b % 2):512 * (b % 2) + 512]
                    if mod in (2, 5):
                        gate = (gate_m if mod == 2 else gate_f)[:, 512 * h:512 * h + 512]
                        chain(dve.tensor_tensor(gate, ps[:, b % 2, :], row, ALU.add))
                        dve.tensor_tensor(gate, gate, f[:, mod // 3, 512 * h:512 * h + 512], ALU.mult
                                          ).then_inc(s_modr, 1)
                    else:
                        c_idx = [0, 1, None, 2, 3][mod]
                        if 2 * c_idx + h >= 2:
                            dve.wait_ge(s_colmm, 8 * l + 2 * c_idx + h - 1)
                        dve.tensor_tensor(modrow[:, b % 2, :], ps[:, b % 2, :], row, ALU.add).then_inc(s_modr, 1)
                dve.wait_ge(s_colmm, 8 * (l + 1))
                dve.wait_ge(s_gcol, 16 * 2 * DEPTH)
                for m in range(4):
                    src = ps[:, 2, 16 * m:16 * m + 16].rearrange("p (k g) -> p k g", g=2)
                    if m % 2 == 0:
                        ins = dve.tensor_copy(modc[:, m, :, :], src)
                    else:
                        for g in range(2):
                            ins = dve.scalar_tensor_tensor(
                                out=modc[:, m, :, g], in0=src[:, :, g], scalar=1.0,
                                in1=gcol[:, l, m // 2, :], op0=ALU.add, op1=ALU.mult)
                ins.then_inc(s_modc, 1)
                upto(WIN0[l] + 1)
                norm(2 * l, l, 0)
                upto(WIN0[l] + N_WIN + 1)
                dve.wait_ge(s_ld[l][2], 32)
                rms(5 * l + 1, D_CM)
                for t in range(NT):
                    v = pr[:, t, OVM:OVM + D_CM]
                    ins = dve.scalar_tensor_tensor(out=v, in0=v, scalar=rs[:, 5 * l + 1, t:t + 1],
                                                   in1=gvb[:, :], op0=ALU.mult, op1=ALU.mult)
                ins.then_inc(s_vn, 1)
                dve.tensor_tensor(z[:, :, :], pr[:, :, OC:OC + D_CV], pr[:, :, OH:OH + D_CV], ALU.mult
                                  ).then_inc(s_z, 1)
                dve.wait_ge(s_wsp, l + 1)
                dve.tensor_copy(wsT[:, :, :].rearrange("p a n -> p (a n)"), ps[:, 6, :]).then_inc(s_wst, 1)
                dve.wait_ge(s_ld[l][0], 16 * 2 * NH)
                dve.wait_ge(s_const, N_CONST)
                dve.tensor_tensor(bias[:, :, :].rearrange("p h (m k) -> p (h m) k", k=GW),
                                  bias[:, :, :].rearrange("p h (m k) -> p (h m) k", k=GW),
                                  win_mask[:, :].rearrange("p (a k) -> p a k", a=1).to_broadcast([P, NH * NDR, GW]),
                                  ALU.add).then_inc(s_bias, 1)
                dve.wait_ge(s_mix, l + 1)
                for t in range(NT):
                    for h in range(4):
                        u = pr[:, t, OU + 64 * h:OU + 64 * h + 64]
                        ins = dve.scalar_tensor_tensor(out=u, in0=ps[:, t, 64 * h:64 * h + 64],
                                                       scalar=bs[:, h:h + 1], in1=u, op0=ALU.add, op1=ALU.mult)
                ins.then_inc(s_cm, 1)
                dve.wait_ge(s_sh, l + 1)
                dve.wait_ge(s_ld[l][3], 16)
                dve.wait_ge(s_z, l + 1)

                def tap(j):
                    return wcb[:, :, j].rearrange("p (a c) -> p a c", a=1).to_broadcast([P, NT, D_CV])

                yc, yt = pr[:, :, OC:OC + D_CV], pr[:, :, OH:OH + D_CV]
                yb = pr[:, :, OB:OB + D_CV]
                chain(dve.tensor_tensor(yc, z[:, :, :], tap(1), ALU.mult))
                chain(dve.tensor_tensor(yt, ps[:, 3:6, 0:256], tap(0), ALU.mult))
                chain(dve.tensor_tensor(yc, yc, yt, ALU.add))
                chain(dve.tensor_tensor(yt, ps[:, 3:6, 256:512], tap(2), ALU.mult))
                chain(dve.tensor_tensor(yc, yc, yt, ALU.add))
                dve.tensor_tensor(yb, yb, yc, ALU.mult).then_inc(s_cvd, 1)
                for i in range(1, 9, 2):
                    dve.wait_ge(s_qk, 9 * l + i + 1)
                    dst = qT[:, i, :] if i < 4 else kT[:, i - 4, :]
                    dve.tensor_copy(dst, ps[:, 7, 0:384]).then_inc(s_qkd, 1)
                dve.wait_ge(s_bias, l + 1)

                def soft(u):
                    t, h = UNITS[u]
                    s = u % 2
                    dve.wait_ge(s_sc, NU * l + u + 1)
                    if u >= 2:
                        dve.wait_ge(s_pt, NU * l + u - 1)
                    if t == 0:
                        w = P
                        chain(dve.tensor_scalar(pS[:, s, 0:P], ps[:, s, 0:P], SCALE, None, ALU.mult))
                    else:
                        w = 384
                        m0 = 2 - 2 * (t - 1)
                        dve.scalar_tensor_tensor(out=pS[:, s, 0:256], in0=ps[:, s, 0:256], scalar=SCALE,
                                                 in1=bias[:, h, GW * m0:GW * (m0 + 4)], op0=ALU.mult, op1=ALU.add)
                        chain(dve.tensor_scalar(pS[:, s, 256:384], ps[:, s, 256:384], SCALE, None, ALU.mult))
                    chain(dve.tensor_reduce(nm[:, s, 0:1], pS[:, s, 0:w], AX_X, ALU.max))
                    dve.tensor_scalar(nm[:, s, 1:2], nm[:, s, 0:1], -1.0, None, ALU.mult).then_inc(s_sm, 1)

                def out(u):
                    t, h = UNITS[u]
                    s = u % 2
                    dve.wait_ge(s_pv, NU * l + u + 1)
                    chain(dve.reciprocal(rden[:, s:s + 1], den[:, s:s + 1]))
                    dve.tensor_scalar(pr[:, t, 64 * h:64 * h + 64], ps[:, 4 + s, 0:64], rden[:, s:s + 1], None,
                                      ALU.mult).then_inc(s_o, 1)

                for u in range(NU + 2):
                    if u >= 2:
                        out(u - 2)
                    if u < NU:
                        soft(u)
                for kt in range(KT):
                    dve.wait_ge(s_mhi, KT * l + kt + 1)
                    dve.tensor_tensor(xlo[:, kt, :], ps[:, 6 + kt % 2, 0:384], xhi[:, kt, :].bitcast(F32),
                                      ALU.subtract).then_inc(s_mlo, 1)
                upto(WOUT0[l] + N_WOUT + 1)
                residual(2 * l, l, 0)
                norm(2 * l + 1, l, 1)
                if l == 0:
                    upto(FFN0 + 1)
                    ffn(NT, 0, FFN0)
                    upto(ADA0[1] + 1)
                    residual(1, 0, 1)
            dve.wait_ge(s_lg, 1)
            for t in range(NT):
                chain(dve.tensor_copy(lg[:, t, :], ps[:, t, 0:NE]))
                chain(dve.max(m8[:, t, :], lg[:, t, :]))
                ins = dve.tensor_tensor(ge[:, t, 0:1], m8[:, t, 1:2], m8[:, t, 0:1], ALU.subtract)
            ins.then_inc(s_rt, 1)
            for t in range(NT):
                chain(dve.max_index(ix[:, t, :], m8[:, t, :], lg[:, t, :]))
                chain(dve.tensor_copy(ixf[:, t, :], ix[:, t, :]))
            dve.wait_ge(s_rte, 1)
            for t in range(NT):
                chain(dve.tensor_scalar(ge[:, t, 2:3], ge[:, t, 1:2], 1.0, None, ALU.add))
                chain(dve.reciprocal(ge[:, t, 2:3], ge[:, t, 2:3]))
                chain(dve.tensor_tensor(ge[:, t, 3:4], ge[:, t, 1:2], ge[:, t, 2:3], ALU.mult))
                chain(dve.tensor_scalar(hot[:, t, :], iota[:, 0:NE], ixf[:, t, 0:1], None, ALU.is_equal))
                chain(dve.tensor_scalar(hot1[:, t, :], iota[:, 0:NE], ixf[:, t, 1:2], None, ALU.is_equal))
                chain(dve.tensor_scalar(rt[:, 0, t, :], hot1[:, t, :], ge[:, t, 3:4], None, ALU.mult))
                chain(dve.scalar_tensor_tensor(out=rt[:, 0, t, :], in0=hot[:, t, :], scalar=ge[:, t, 2:3],
                                               in1=rt[:, 0, t, :], op0=ALU.mult, op1=ALU.add))
                ins = dve.tensor_tensor(rt[:, 2, t, :], hot[:, t, :], hot1[:, t, :], ALU.add)
            ins.then_inc(s_hot, 1)
            dve.wait_ge(s_pos, 1)
            for t in range(NT):
                chain(dve.tensor_copy(rt[:, 1, t, :], ps[:, t, 64:64 + NE]))
            chain(dve.tensor_scalar(cnt[:, :], ps[:, 3, 0:NE], float(P), None, ALU.is_gt))
            chain(dve.tensor_scalar(lg[:, 0, :], ps[:, 3, 0:NE], float(2 * P), 1.0, ALU.is_gt, ALU.add))
            dve.tensor_tensor(ntile[:, :], cnt[:, :], lg[:, 0, :], ALU.add).then_inc(s_nt, 1)
            dve.wait_ge(s_nt, 1)
            dve.memset(f[:, :, :], 0.0).then_inc(s_acc, 1)
            upto(EXP0 + 1)
            with dve.Fori(0, NE) as e:
                T = dve.value_load(ntile[0:1, bass.ds(e, 1)], min_val=1, max_val=3)
                dve.wait_ge(s_acc, e * NT + 1)
                for i in range(3):
                    for t in range(NT):
                        ins = dve.tensor_copy(cur[:, i, t:t + 1], rt[:, i, t, bass.ds(e, 1)])
                ins.then_inc(s_cur, 1)
                with dve.If(T < 2):
                    expert(1, e)
                with dve.Else():
                    with dve.If(T < 3):
                        expert(2, e)
                    with dve.Else():
                        expert(3, e)
                for t in range(NT):
                    dve.wait_ge(s_scm, e * NT + t + 1)
                    dve.scalar_tensor_tensor(out=f[:, t, :], in0=ps[:, 2 * t:2 * t + 2, :].rearrange("p a n -> p (a n)"),
                                             scalar=cur[:, 0, t:t + 1], in1=f[:, t, :], op0=ALU.mult, op1=ALU.add
                                             ).then_inc(s_acc, 1)
                with dve.If(e < NE - 1):
                    split(e + 1, 0)
                    split(e + 1, 1)
            residual(3, 1, 1)

        @block.tensor
        def _(pe):
            def three(out, a_hi, a_lo, w_hi, w_lo, start, stop):
                pe.matmul(out, a_hi, w_hi, start=start, stop=False)
                pe.matmul(out, a_hi, w_lo, start=False, stop=False)
                return pe.matmul(out, a_lo, w_hi, start=False, stop=stop)

            def halves(n, k):
                return (whi[n % SPL][:, :].rearrange("p (k n) -> p k n", k=k),
                        wlo[n % SPL][:, :].rearrange("p (k n) -> p k n", k=k))

            def ada(l):
                pe.wait_ge(s_cs, l + 1)
                def turn(b):
                    mod, h = divmod(b, 2)
                    if mod in (2, 5):
                        return
                    m = [0, 1, None, 2, 3][mod]
                    pe.wait_ge(s_modr, ADA_B * l + b + 1)
                    for j in range(4):
                        o = 16 * m + 2 * (4 * h + j)
                        ins = pe.matmul(ps[:, 2, o:o + 2], modrow[:, b % 2, P * j:P * j + P], sel[:, :],
                                        start=True, stop=True)
                    ins.then_inc(s_colmm, 1)

                for b in range(ADA_B):
                    if b >= 2:
                        pe.wait_ge(s_modr, ADA_B * l + b - 1)
                    for h in range(2):
                        n = ADA0[l] + 2 * b + h
                        pe.wait_ge(s_lo, n + 1)
                        hi, lo = halves(n, 4)
                        for k in range(4):
                            a = cS[:, 4 * h + k, :]
                            pe.matmul(ps[:, b % 2, :], a, hi[:, k, :], start=(h == 0 and k == 0), stop=False)
                            ins = pe.matmul(ps[:, b % 2, :], a, lo[:, k, :], start=False,
                                            stop=(h == 1 and k == 3))
                        ins.then_inc(s_pe, 1)
                    if b >= 1:
                        turn(b - 1)
                turn(ADA_B - 1)

            def norm(s):
                for kt in range(KT):
                    if kt >= 2:
                        pe.wait_ge(s_hf, KT * s + kt - 1)
                    for t in range(NT):
                        if kt == 0:
                            pe.wait_ge(s_xn, NT * s + t + 1)
                        ins = pe.transpose(ps[:, 6 + kt % 2, P * t:P * t + P], f[:, t, P * kt:P * kt + P], ident[:, :])
                    ins.then_inc(s_tr, 1)

            def win(l):
                for b in range(WIN_B):
                    if b >= 2:
                        pe.wait_ge(s_pr, NT * WIN_B * l + NT * (b - 1))
                    w, kk = (512, 4) if b < 5 else (256, 8)
                    for h in range(2 if b < 5 else 1):
                        n = WIN0[l] + 2 * b + h
                        pe.wait_ge(s_lo, n + 1)
                        hi, lo = halves(n, kk)
                        for t in range(NT):
                            for k in range(kk):
                                kt = 4 * h + k
                                if t == 0:
                                    pe.wait_ge(s_xlo, KT * 2 * l + kt + 1)
                                a = P * t
                                last = kt == KT - 1
                                ins = three(ps[:, 2 * t + b % 2, 0:w], xhi[:, kt, a:a + P], xlo[:, kt, a:a + P],
                                            hi[:, k, :], lo[:, k, :], kt == 0, last)
                            if last and t < NT - 1:
                                ins.then_inc(s_win, 1)
                        pe_done(ins)

            def pe_done(ins):
                ins.then_inc(s_pe, 1)

            def mixer(l):
                pe.wait_ge(s_ld[l][1], 16)
                for h in range(4):
                    ins = pe.transpose(ps[:, 6, P * h:P * h + P], ws[:, h, :], ident[:, :])
                ins.then_inc(s_wsp, 1)
                pe.wait_ge(s_vn, l + 1)
                pe.wait_ge(s_wst, l + 1)
                for t in range(NT):
                    for h in range(4):
                        ins = pe.matmul(ps[:, t, 64 * h:64 * h + 64], wsT[:, h, :],
                                        pr[:, t, OVM + 64 * h:OVM + 64 * h + 64], start=True, stop=True)
                ins.then_inc(s_mix, 1)
                pe.wait_ge(s_z, l + 1)
                for t in range(NT):
                    near = [(0, 0, t), (1, 256, t)]
                    if t == 1:
                        near.append((3, 256, 2))
                    if t == 2:
                        near.insert(1, (2, 0, 1))
                    for i, o, src in near:
                        start = i < 2
                        stop = not ((t == 1 and i == 1) or (t == 2 and i == 0))
                        ins = pe.matmul(ps[:, 3 + t, o:o + 256], shift[:, i, :], z[:, src, :], start=start, stop=stop)
                ins.then_inc(s_sh, 1)
                for i in range(9):
                    if i >= 2:
                        pe.wait_ge(s_qka if i % 2 == 0 else s_qkd, (5 if i % 2 == 0 else 4) * l + i // 2)
                    if i == 8:
                        pe.wait_ge(s_ld[l][4], 16)
                        for j in range(4):
                            ins = pe.transpose(ps[:, 6, P * j:P * j + P], ck[:, P * j:P * j + P], ident[:, :])
                    else:
                        o = OQ + P * i if i < 4 else OK + P * (i - 4)
                        for t in range(NT):
                            ins = pe.transpose(ps[:, 6 + i % 2, P * t:P * t + P], pr[:, t, o:o + P], ident[:, :])
                    ins.then_inc(s_qk, 1)
                pe.wait_ge(s_qka, 5 * (l + 1))
                pe.wait_ge(s_qkd, 4 * (l + 1))
                pe.wait_ge(s_cm, l + 1)
                pe.wait_ge(s_cvd, l + 1)
                pe.wait_ge(s_ld[l][5], 16)

                def score(u):
                    t, h = UNITS[u]
                    j, r = h // 2, 64 * (h % 2)
                    if u >= 2:
                        pe.wait_ge(s_sm, NU * l + u - 1)
                    q = qT[r:r + 64, j, P * t:P * t + P]
                    if t == 0:
                        ins = pe.matmul(ps[:, u % 2, 0:P], q, kT[r:r + 64, j, 0:P], start=True, stop=True)
                    else:
                        pe.matmul(ps[:, u % 2, 0:256], q, kT[r:r + 64, j, P:3 * P], start=True, stop=True)
                        ins = pe.matmul(ps[:, u % 2, 256:384], q, ckT[r:r + 64, j, :], start=True, stop=True)
                    ins.then_inc(s_sc, 1)

                def turn(u):
                    pe.wait_ge(s_ex, NU * l + u + 1)
                    if u >= 2:
                        pe.wait_ge(s_ptc, NU * l + u - 1)
                    for j in range(1 if UNITS[u][0] == 0 else 3):
                        ins = pe.transpose(ps[:, 2 + u % 2, P * j:P * j + P], pS[:, u % 2, P * j:P * j + P],
                                           ident[:, :])
                    ins.then_inc(s_pt, 1)

                def value(u):
                    t, h = UNITS[u]
                    pe.wait_ge(s_ptc, NU * l + u + 1)
                    if u >= 2:
                        pe.wait_ge(s_o, NU * l + u - 1)
                    o = 64 * h
                    vs = [pr[:, 0, OV + o:OV + o + 64]] if t == 0 else [
                        pr[:, 1, OV + o:OV + o + 64], pr[:, 2, OV + o:OV + o + 64], cv[:, o:o + 64]]
                    for j, v in enumerate(vs):
                        ins = pe.matmul(ps[:, 4 + u % 2, 0:64], pT[:, u % 2, P * j:P * j + P], v,
                                        start=(j == 0), stop=(j == len(vs) - 1))
                    ins.then_inc(s_pv, 1)

                for u in range(NU + 2):
                    if u < NU:
                        score(u)
                    if 1 <= u <= NU:
                        turn(u - 1)
                    if u >= 2:
                        value(u - 2)
                pe.wait_ge(s_o, NU * (l + 1))
                for kt in range(KT):
                    if kt >= 2:
                        pe.wait_ge(s_mlo, KT * l + kt - 1)
                    o = mix_col(kt)
                    for t in range(NT):
                        ins = pe.transpose(ps[:, 6 + kt % 2, P * t:P * t + P], pr[:, t, o:o + P], ident[:, :])
                    ins.then_inc(s_mt, 1)

            def down(T, hi_of, lo_of, n0, nk, wait, s_done):
                for q in range(nk // 2):
                    wait(q)
                    hi, lo = halves(n0 + q, 2)
                    for t in range(T):
                        for k in range(2):
                            kt = 2 * q + k
                            for h in range(2):
                                o = slice(512 * h, 512 * h + 512)
                                ins = three(ps[:, 2 * t + h, :], hi_of[:, kt, P * t:P * t + P],
                                            lo_of[:, kt, P * t:P * t + P], hi[:, k, o], lo[:, k, o],
                                            kt == 0, kt == nk - 1)
                        if q == nk // 2 - 1 and t < NT - 1 and s_done is not None:
                            ins.then_inc(s_done, 1)
                    pe_done(ins)

            def wout(l):
                def wait(q):
                    pe.wait_ge(s_lo, WOUT0[l] + q + 1)
                    pe.wait_ge(s_mlo, KT * l + 2 * q + 2)
                down(NT, xhi, xlo, WOUT0[l], KT, wait, s_y)

            def gates(s, gate):
                if s < 3:
                    pe.wait_ge(s_yc, NT * s + 2)
                else:
                    pe.wait_ge(s_acc, NT * NE + 1)
                for g in range(2):
                    for h in range(2):
                        ins = pe.matmul(ps[:, 2 * g + h, :], selb[:, g, :], gate[:, 512 * h:512 * h + 512],
                                        start=True, stop=True)
                    ins.then_inc(s_gt, 1)

            def ffn(T, k, n0, e=None):
                def wait_lo(j):
                    if e is None:
                        pe.wait_ge(s_lo, n0 + j + 1)
                    else:
                        pe.wait_ge(s_lo, e * N_FFN + (EXP0 + j + 1))

                m0 = n0 if e is None else 0

                def turn(b):
                    pe.wait_ge(s_pm, k * GU_B + b + 1)
                    for i in range(2):
                        if b:
                            pe.wait_ge(s_hlo, k * 2 * GU_B + 2 * (b - 1) + i + 1)
                        for t in range(T):
                            ins = pe.transpose(ps[:, 6 + i, P * t:P * t + P], pg[:, t, P * i:P * i + P], ident[:, :])
                        ins.then_inc(s_ht, 1)

                for b in range(GU_B):
                    if b >= 2:
                        pe.wait_ge(s_pm, k * GU_B + b - 1)
                    for h in range(2):
                        wait_lo(2 * b + h)
                        hi, lo = halves(m0 + 2 * b + h, 4)
                        for t in range(T):
                            for kk in range(4):
                                kt = 4 * h + kk
                                ins = three(ps[:, 2 * t + b % 2, :], xhi[:, kt, P * t:P * t + P],
                                            xlo[:, kt, P * t:P * t + P], hi[:, kk, :], lo[:, kk, :],
                                            kt == 0, kt == KT - 1)
                        pe_done(ins)
                    if b:
                        turn(b - 1)
                turn(GU_B - 1)

                def wait(q):
                    wait_lo(N_GU + q)
                    pe.wait_ge(s_hlo, k * 2 * GU_B + 2 * q + 2)
                down(T, hhi, hlo, m0 + N_GU, FK, wait, None if e is not None else s_y)

            def expert(T, e):
                k = e + 1
                pe.wait_ge(s_perm, e + 1)
                for kt in range(KT):
                    if kt >= 2:
                        pe.wait_ge(s_glo, e * KT + kt - 1)
                    for t in range(NT):
                        ins = pe.matmul(ps[:, 6 + kt % 2, 0:P * T], x[:, t, P * kt:P * kt + P], perm[:, t, 0:P * T],
                                        start=(t == 0), stop=(t == NT - 1))
                    ins.then_inc(s_ga, 1)
                pe.wait_ge(s_glo, e * KT + KT)
                pe.wait_ge(s_acc, e * NT + 1)
                ffn(T, k, None, e)
                for t in range(T):
                    if t >= 2:
                        pe.wait_ge(s_pmc, e * NT + 1)
                    for i in range(NT):
                        ins = pe.transpose(ps[:, 6 + t % 2, P * i:P * i + P], perm[:, i, P * t:P * t + P], ident[:, :])
                    ins.then_inc(s_pmt, 1)
                pe.wait_ge(s_ylo, e + 1)
                pe.wait_ge(s_pmc, e * NT + NT)
                if T < NT:
                    pe.sem_inc(s_pmt, NT - T)
                for i in range(NT):
                    for h in range(2):
                        for t in range(T):
                            a, o = permT[:, t, P * i:P * i + P], slice(512 * h, 512 * h + 512)
                            pe.matmul(ps[:, 2 * i + h, :], a, yhi[:, t, o], start=(t == 0), stop=False)
                            ins = pe.matmul(ps[:, 2 * i + h, :], a, ylo[:, t, o], start=False, stop=(t == T - 1))
                    ins.then_inc(s_scm, 1)

            pe.wait_ge(s_const, N_CONST)
            for l in range(DEPTH):
                ada(l)
                norm(2 * l)
                win(l)
                mixer(l)
                wout(l)
                gates(2 * l, gate_m)
                norm(2 * l + 1)
                if l == 0:
                    pe.wait_ge(s_xlo, KT * 2)
                    ffn(NT, 0, FFN0)
                    gates(1, gate_f)
            for i in range(6):
                t, h = divmod(i, 2)
                pe.wait_ge(s_hf, KT * 4)
                if i >= 2:
                    pe.wait_ge(s_btc, i - 1)
                for j in range(4):
                    ins = pe.transpose(ps[:, 6 + i % 2, P * j:P * j + P], hf[:, 4 * h + j, P * t:P * t + P], ident[:, :])
                ins.then_inc(s_bt, 1)
            pe.wait_ge(s_wr, 16)
            for t in range(NT):
                for kt in range(KT):
                    ins = pe.matmul(ps[:, t, 0:NE], hf[:, kt, P * t:P * t + P], wr[:, kt, :],
                                    start=(kt == 0), stop=(kt == KT - 1))
            ins.then_inc(s_lg, 1)
            pe.wait_ge(s_hot, 1)
            pe.wait_ge(s_tri, 1)
            for t in range(NT):
                for i in range(t + 1):
                    pe.matmul(ps[:, t, 64:64 + NE], ones[:, :] if i < t else before[:, :], rt[:, 2, i, :],
                              start=(i == 0), stop=(i == t))
            for t in range(NT):
                ins = pe.matmul(ps[:, 3, 0:NE], ones[:, :], rt[:, 2, t, :], start=(t == 0), stop=(t == NT - 1))
            ins.then_inc(s_pos, 1)
            pe.wait_ge(s_btc, 6)
            pe.wait_ge(s_nt, 1)
            with pe.Fori(0, NE) as e:
                T = pe.value_load(ntile[0:1, bass.ds(e, 1)], min_val=1, max_val=3)
                with pe.If(T < 2):
                    expert(1, e)
                with pe.Else():
                    with pe.If(T < 3):
                        expert(2, e)
                    with pe.Else():
                        expert(3, e)
            gates(3, gate_f)


_INS = ['x_prompt', 'x_sample', 'cache_k', 'cache_v', 'c', 'c_ctx', 'w_ada', 'b_ada', 'norm_g', 'w_in', 'w_out',
        'rpb', 'g_v', 'w_s', 'b_s', 'w_conv', 'w_ffn_gu', 'w_ffn_d', 'w_router', 'w_moe_gu', 'w_moe_d']
_OUTS = [(1, P, D), (1, 2 * P, D), (1, DEPTH, P, NH, HD), (1, DEPTH, P, NH, HD)]


def kernel(**inputs):
    import numpy as _np
    import concourse.bacc as _bacc
    from concourse.bass_utils import run_bass_kernel_spmd as _run

    nc = _bacc.Bacc("TRN2", target_bir_lowering=False, num_devices=1)
    arrays, args = {}, []
    for name in _INS:
        a = _np.ascontiguousarray(inputs[name])
        arrays[f"in_{name}_dram"] = a
        args.append(nc.dram_tensor(f"in_{name}_dram", a.shape, mybir.dt.from_np(a.dtype), kind="ExternalInput").ap())
    for i, shape in enumerate(_OUTS):
        args.append(nc.dram_tensor(f"out_{i}_dram", shape, F32, kind="ExternalOutput").ap())
    args.append(nc.dram_tensor("x_park", (NT * P, D), F32, kind="Internal").ap())
    args.append(nc.dram_tensor("rpb_pad", (DEPTH, 7 * NH, GW, 127), F32, kind="Internal").ap())
    build(nc, *args)
    r = _run(nc, [arrays], core_ids=[0])
    return tuple(r.results[0][f"out_{i}_dram"] for i in range(len(_OUTS)))
```

```python
from contextlib import ExitStack

import concourse.bass as bass
from concourse import mybir

F32 = mybir.dt.float32
F32R = mybir.dt.float32r
I32 = mybir.dt.int32
U32 = mybir.dt.uint32
ALU = mybir.AluOpType
ACT = mybir.ActivationFunctionType
AX_X = mybir.AxisListType.X

P = 128
NT = 3
D = 1024
KT = D // P
DEPTH = 2
HD = 64
NH = 8
D_ATT, D_CM, D_CV = 512, 256, 256
D_IN = 3 * D_ATT + 2 * D_CM + 3 * D_CV
OQ, OK, OV = 0, D_ATT, 2 * D_ATT
OU = 3 * D_ATT
OVM = OU + D_CM
OB = OVM + D_CM
OC = OB + D_CV
OH = OC + D_CV
D_FF = 2816
FK = D_FF // P
NE = 8
N_MOD = 6
EPS = 1e-6
NEG = -1e30
GW = 64
KH, KW = 8, 16
NDR = 6
ROWS = 4
SCALE = HD ** -0.5

CHUNK = 2048
RAW = 3
SPL = 3
ADA_B = N_MOD * D // 512
WIN_B = 6
N_ADA, N_WIN, N_WOUT = 2 * ADA_B, 11, 4
GU_B = D_FF // 256
N_GU, N_WD = 2 * GU_B, FK // 2
N_FFN = N_GU + N_WD
ADA_SEQ = [0, 1, 2, 3, 4, 5, 10, 11, 6, 7, 8, 9]
HEAD = 4
ADA_IN_WIN = {w: HEAD + w - 1 for w in range(1, 1 + ADA_B - HEAD)}
ADA_IN_WD = {2 * i + 1: i for i in range(HEAD)}


def stream():
    out = [("ada", 0, j) for j in range(2 * HEAD)]
    for l in range(DEPTH):
        for w in range(N_WIN):
            out.append(("win", l, w))
            if w in ADA_IN_WIN:
                out += [("ada", l, 2 * ADA_IN_WIN[w] + h) for h in range(2)]
        out += [("wout", l, q) for q in range(N_WOUT)]
        if l == 0:
            for j in range(N_FFN):
                out.append(("ffn", 0, j))
                if j - N_GU in ADA_IN_WD:
                    out += [("ada", 1, 2 * ADA_IN_WD[j - N_GU] + h) for h in range(2)]
    return out


STREAM = stream()
PLACE = {c: n for n, c in enumerate(STREAM)}
EXP0 = len(STREAM)
assert EXP0 % RAW == 0 and N_FFN % RAW == 0


def turned(i):
    return sum(b // 2 not in (2, 5) for b in ADA_SEQ[:i + 1])


def mix_col(kt):
    return [OQ, OQ + 128, OQ + 256, OQ + 384, OU, OU + 128, OB, OB + 128][kt]


def build(nc, x_prompt, x_sample, cache_k, cache_v, c, c_ctx, w_ada, b_ada, norm_g, w_in, w_out, rpb,
          g_v, w_s, b_s, w_conv, w_ffn_gu, w_ffn_d, w_router, w_moe_gu, w_moe_d,
          y_prompt, y_sample, new_k, new_v, x_park, rpb_pad):
    with ExitStack() as ctx:
        ctx.enter_context(nc.allow_non_contiguous_dma(reason="a few small vectors go to columns"))

        def sb(name, shape, dt=F32):
            return ctx.enter_context(nc.sbuf_tensor(name, shape, dt))

        def sem(name):
            return ctx.enter_context(nc.semaphore(name))

        raw = [sb(f"raw{i}", [P, CHUNK]) for i in range(RAW)]
        whi = [sb(f"whi{i}", [P, CHUNK], F32R) for i in range(SPL)]
        wlo = [sb(f"wlo{i}", [P, CHUNK], F32R) for i in range(SPL)]
        xhi = sb("xhi", [P, KT, NT * P], F32R)
        xlo = sb("xlo", [P, KT, NT * P], F32R)
        x = sb("x", [P, NT, D])
        f = sb("f", [P, NT, D])
        pS = f[:, :, :].rearrange("p t n -> p (t n)").rearrange("p (s h k) -> p s h k", s=4, h=2)
        ident = sb("ident", [P, P])
        shift = sb("shift", [P, 4, P])
        iota = sb("iota", [P, NT * P])
        sel = sb("sel", [P, 2])
        selb = sb("selb", [P, 2, P])
        win_mask = sb("win_mask", [P, GW])
        sil = sb("sil", [P, KT, 2])
        silh = sb("silh", [P, KT, 2], F32R)
        sill = sb("sill", [P, KT, 2])
        gcol = sb("gcol", [P, DEPTH, 2, KT])
        modc = sb("modc", [P, 4, KT, 2])
        ss = sb("ss", [P, 10, NT])
        rs = sb("rs", [P, 10, NT])
        nm = sb("nm", [P, 4, 2, 2])
        den = sb("den", [P, 4, 2])
        rden = sb("rden", [P, 4, 2])
        gate_f = sb("gate_f", [P, D])
        arena = nc.sbuf_base
        arena += -arena % 64
        end = [arena]

        def at(name, off, shape, dt=F32):
            n = 4
            for s in shape[1:]:
                n *= s
            end[0] = max(end[0], arena + off + n)
            assert arena + off + n <= nc.sbuf_usable_end, (name, arena + off + n, nc.sbuf_usable_end)
            return nc.alloc_sbuf_tensor_at(name, shape, dt, offset=arena + off)

        hf = at("hf", 0, [P, KT, NT * P])
        pr = at("pr", 0, [P, NT, D_IN])
        qT = at("qT", 33792, [P, 4, NT * P])
        kT = at("kT", 39936, [P, 4, NT * P])
        stage = at("stage", 33792, [P, NT, D])
        ckT = at("ckT", 46080, [P, 4, P])
        bias = at("bias", 48128, [P, NH, NDR * GW])
        cv = at("cv", 60416, [P, D_ATT])
        ck = at("ck", 62464, [P, D_ATT])
        pT = at("pT", 62464, [P, 2, 2, NT * P])
        z = at("z", 65536, [P, NT, D_CV])
        cS = at("cS", 70656, [P, KT, P], F32R)
        ws = at("ws", 68608, [P, 4, P])
        wsT = at("wsT", 68608, [P, 4, P])
        gvb = at("gvb", 70656, [P, D_CM])
        wcb = at("wcb", 71680, [P, D_CV, 3])
        bs = at("bs", 74752, [P, 4])
        gate_m = at("gate_m", 74784, [P, D])
        hhi = at("hhi", 0, [P, FK, NT * P], F32R)
        hlo = at("hlo", 33792, [P, FK, NT * P], F32R)
        pg = at("pg", 67584, [P, NT, 256])
        perm = at("perm", 70656, [P, NT, NT * P])
        yhi = at("yhi", 0, [P, NT, D], F32R)
        ylo = at("ylo", 12288, [P, NT, D], F32R)
        permT = at("permT", 24576, [P, NT, NT * P], F32R)
        wr = at("wr", 33792, [P, KT, NE])
        lg = at("lg", 34048, [P, NT, NE])
        m8 = at("m8", 34144, [P, NT, NE])
        ix = at("ix", 34240, [P, NT, NE], U32)
        ixf = at("ixf", 34336, [P, NT, NE])
        hot = at("hot", 34432, [P, NT, NE])
        ge = at("ge", 34528, [P, NT, 4])
        hot1 = at("hot1", 34624, [P, NT, NE])
        rt = at("rt", 75264, [P, 3, NT, NE])
        cnt = at("cnt", 75264 + 288, [P, NE])
        ntile = at("ntile", 75264 + 320, [P, NE], I32)
        cur = at("cur", 75264 + 352, [P, 3, NT])
        ones = at("ones", 75904, [P, P])
        before = at("before", 76416, [P, P])
        pad = at("pad", 60416, [P, 127])

        ps = ctx.enter_context(nc.psum_tensor("ps", [P, 8, 512], F32))

        s_const = sem("s_const")
        s_x = sem("s_x")
        s_c = sem("s_c")
        s_gcol = sem("s_gcol")
        s_raw = [sem(f"s_raw{i}") for i in range(RAW)]
        s_hi = sem("s_hi")
        s_lo = sem("s_lo")
        s_pe = sem("s_pe")
        s_dv = sem("s_dv")
        s_ac = sem("s_ac")
        s_po = sem("s_po")
        s_sil = sem("s_sil")
        s_cs = sem("s_cs")
        s_brz = sem("s_brz")
        s_brow = [sem(f"s_brow{i}") for i in range(2)]
        s_gb = sem("s_gb")
        s_ada = sem("s_ada")
        s_modr = sem("s_modr")
        s_colmm = sem("s_colmm")
        s_modc = sem("s_modc")
        s_ss = sem("s_ss")
        s_ms = sem("s_ms")
        s_sq = sem("s_sq")
        s_xn = sem("s_xn")
        s_tr = sem("s_tr")
        s_hf = sem("s_hf")
        s_xhi = sem("s_xhi")
        s_xlo = sem("s_xlo")
        s_win = sem("s_win")
        s_pr = sem("s_pr")
        s_kv = sem("s_kv")
        s_ld = [[sem(f"s_ld{l}_{n}") for n in range(6)] for l in range(DEPTH)]
        s_pad = sem("s_pad")
        s_bias = sem("s_bias")
        s_gel = sem("s_gel")
        s_wsp = sem("s_wsp")
        s_wst = sem("s_wst")
        s_vn = sem("s_vn")
        s_mix = sem("s_mix")
        s_cm = sem("s_cm")
        s_z = sem("s_z")
        s_sh = sem("s_sh")
        s_cvd = sem("s_cvd")
        s_qk = sem("s_qk")
        s_qka = sem("s_qka")
        s_qkd = sem("s_qkd")
        s_sc = sem("s_sc")
        s_sm = sem("s_sm")
        s_ex = sem("s_ex")
        s_pt = sem("s_pt")
        s_ptc = sem("s_ptc")
        s_pv = sem("s_pv")
        s_o = sem("s_o")
        s_mt = sem("s_mt")
        s_mhi = sem("s_mhi")
        s_mlo = sem("s_mlo")
        s_y = sem("s_y")
        s_yc = sem("s_yc")
        s_gt = sem("s_gt")
        s_xr = sem("s_xr")
        s_gu = sem("s_gu")
        s_sg = sem("s_sg")
        s_pm = sem("s_pm")
        s_ht = sem("s_ht")
        s_hhi = sem("s_hhi")
        s_hlo = sem("s_hlo")
        s_yf = sem("s_yf")
        s_park = sem("s_park")
        s_back = sem("s_back")
        s_wr = sem("s_wr")
        s_bt = sem("s_bt")
        s_btc = sem("s_btc")
        s_lg = sem("s_lg")
        s_rt = sem("s_rt")
        s_rte = sem("s_rte")
        s_hot = sem("s_hot")
        s_cur = sem("s_cur")
        s_tri = sem("s_tri")
        s_pos = sem("s_pos")
        s_nt = sem("s_nt")
        s_perm = sem("s_perm")
        s_ga = sem("s_ga")
        s_ghi = sem("s_ghi")
        s_glo = sem("s_glo")
        s_yhi = sem("s_yhi")
        s_ylo = sem("s_ylo")
        s_pmt = sem("s_pmt")
        s_pmc = sem("s_pmc")
        s_scm = sem("s_scm")
        s_acc = sem("s_acc")
        s_out = sem("s_out")

        N_CONST = 10

        UNITS = [(t, h) for t in range(NT) for h in range(0, NH, 2)]
        NU = len(UNITS)

        def chunk_src(n):
            def rows(w, k):
                w = w.rearrange("(k p) n -> p k n", p=P)
                return [w[:, 0:k // 2, :], w[:, k // 2:k, :]], k

            kind, l, j = STREAM[n]
            b, h = divmod(j, 2)
            if kind == "ada":
                b = ADA_SEQ[b]
                return rows(w_ada[l, 512 * h:512 * h + 512, 512 * b:512 * b + 512], 4)
            if kind == "win":
                if b == 5:
                    return rows(w_in[l, :, 2560:2816], 8)
                return rows(w_in[l, 512 * h:512 * h + 512, 512 * b:512 * b + 512], 4)
            if kind == "wout":
                return rows(w_out[l, 256 * j:256 * j + 256, :], 2)
            return ffn_src(w_ffn_gu[0], w_ffn_d[0], j)

        def ada_stage(l, i):
            return f if l and i < HEAD else stage

        def ffn_src(gu, dn, j):
            if j < N_GU:
                b, h = divmod(j, 2)
                v = gu.rearrange("(k p) n -> p k n", p=P)
                return [v[:, 4 * h:4 * h + 4, o + 256 * b:o + 256 * b + 256] for o in (0, D_FF)], 0
            q = j - N_GU
            v = dn.rearrange("(k p) n -> p k n", p=P)
            return [v[:, 2 * q:2 * q + 1, :], v[:, 2 * q + 1:2 * q + 2, :]], 2

        def raw_parts(i, k):
            if k == 0:
                v = raw[i][:, :].rearrange("p (k n) -> p k n", k=4)
                return [v[:, :, 0:256], v[:, :, 256:512]]
            v = raw[i][:, :].rearrange("p (k n) -> p k n", k=k)
            return [v[:, 0:k // 2, :], v[:, k // 2:k, :]]

        class Chain:

            def __init__(self, eng, s):
                self.eng, self.s, self.n = eng, s, 0

            def __call__(self, ins):
                self.n += 1
                ins.then_inc(self.s, 1)
                self.eng.wait_ge(self.s, self.n)

        block = ctx.enter_context(nc.Block())

        @block.sync
        def _(sp):
            def load(n):
                if n >= RAW:
                    sp.wait_ge(s_lo, n - RAW + 1)
                src, k = chunk_src(n)
                for to, of in zip(raw_parts(n % RAW, k), src):
                    sp.dma_start(to, of).then_inc(s_raw[n % RAW], 16)

            sp.dma_start(sil[:, :, 0], c_ctx.rearrange("(k p) -> p k", p=P)).then_inc(s_c, 16)
            sp.dma_start(sil[:, :, 1], c[0].rearrange("(k p) -> p k", p=P)).then_inc(s_c, 16)
            for n in range(RAW):
                load(n)
            sp.dma_start(x[:, 0, :], x_prompt[0]).then_inc(s_x, 16)
            sp.dma_start(x[:, 1:3, :], x_sample[0].rearrange("(t p) d -> p t d", p=P)).then_inc(s_x, 16)
            for n in range(RAW, EXP0):
                load(n)
            with sp.Fori(0, NE) as e:
                gu = w_moe_gu[0, bass.ds(e, 1), :, :].rearrange("e k n -> (e k) n")
                dn = w_moe_d[0, bass.ds(e, 1), :, :].rearrange("e k n -> (e k) n")
                for j in range(N_FFN):
                    sp.wait_ge(s_lo, e * N_FFN + (EXP0 + j - RAW + 1))
                    src, k = ffn_src(gu, dn, j)
                    for to, of in zip(raw_parts(j % RAW, k), src):
                        sp.dma_start(to, of).then_inc(s_raw[j % RAW], 16)

        @block.gpsimd
        def _(pool):
            chain = Chain(pool, s_po)
            for l in range(DEPTH):
                for i in range(2):
                    pool.dma_start(gcol[:, l, i, :], norm_g[l, 2 * i].rearrange("(k p) -> p k", p=P)
                                   ).then_inc(s_gcol, 16)

            def clear_brow(l, i):
                chain(pool.memset(ada_stage(l, i)[:, 2, :], 0.0))

            def brow(l, i):
                if i >= 2:
                    pool.wait_ge(s_modr, ADA_B * l + i - 1)
                o = b_ada[l, 512 * ADA_SEQ[i]:512 * ADA_SEQ[i] + 512].offset
                pool.dma_start(ada_stage(l, i)[0:33:32, 2, 512 * (i % 2):512 * (i % 2) + 512],
                               bass.AP(b_ada.tensor, o, [[0, 2], [1, 512]])).then_inc(s_brow[i % 2], 16)

            def norm_row(l, j):
                pool.dma_start(stage[:, 1, :], bass.AP(norm_g.tensor, norm_g[l, j, :].offset, [[0, P], [1, D]])
                               ).then_inc(s_gb, 16)

            clear_brow(0, 0)
            brow(0, 0)
            brow(0, 1)
            const = Chain(pool, s_const)
            chain(pool.memset(ident[:, :], 0.0))
            chain(pool.memset(shift[:, :, :], 0.0))
            chain(pool.memset(sel[:, :], 0.0))
            chain(pool.memset(win_mask[:, :], 0.0))
            const(pool.iota(iota[:, :], [[1, NT * P]], base=0, channel_multiplier=0,
                            allow_small_or_imprecise_dtypes=True))
            const(pool.affine_select(out=ident[:, :], in_=ident[:, :], compare_op=ALU.not_equal, fill=1.0,
                                     base=0, pattern=[[-1, P]], channel_multiplier=1))
            for i, base in enumerate((1, -1, -(P - 1), P - 1)):
                const(pool.affine_select(out=shift[:, i, :], in_=shift[:, i, :], compare_op=ALU.not_equal,
                                         fill=1.0, base=base, pattern=[[-1, P]], channel_multiplier=1))
            for o in (0, 64):
                chain(pool.affine_select(out=sel[:, :], in_=sel[:, :], compare_op=ALU.not_equal, fill=1.0,
                                         base=-o, pattern=[[-32, 2]], channel_multiplier=1))
            for g in range(2):
                const(pool.tensor_copy(selb[:, g, :], sel[:, g:g + 1].to_broadcast([P, P])))
            for o in (0, GW):
                m = win_mask[o:o + GW, 0:GW - KW]
                chain(pool.affine_select(out=m, in_=m, compare_op=ALU.is_ge, fill=NEG, base=KW // 2,
                                         pattern=[[1, GW - KW]], channel_multiplier=-1))
                m = win_mask[o:o + GW, KW:GW]
                const(pool.affine_select(out=m, in_=m, compare_op=ALU.is_ge, fill=NEG, base=KW // 2 - 1 - KW,
                                         pattern=[[-1, GW - KW]], channel_multiplier=1))

            for l in range(DEPTH):
                if l:
                    pool.wait_ge(s_tr, 2 * KT)
                    clear_brow(l, 0)
                    brow(l, 0)
                    brow(l, 1)
                brow(l, 2)
                brow(l, 3)
                if l:
                    pool.wait_ge(s_xr, 6)
                    clear_brow(l, HEAD)
                norm_row(l, 1)
                brow(l, 4)
                brow(l, 5)
                chain(pool.memset(pad[:, :], NEG))
                for h in range(NH):
                    pool.dma_start(pad[7 * h:7 * h + 7, 48:79], rpb[l, h, 4:11, :]).then_inc(s_pad, 16)
                pool.wait_ge(s_pad, (16 * NH + 16) * (l + 1) - 16)
                pool.dma_start(rpb_pad[l], pad[0:56, :].rearrange("p (a k) -> p a k", a=1).to_broadcast([56, GW, 127])
                               ).then_inc(s_pad, 16)
                brow(l, 6)
                brow(l, 7)
                norm_row(l, 3)
                pool.wait_ge(s_pad, (16 * NH + 16) * (l + 1))
                for h in range(NH):
                    for r2 in range(2):
                        o = rpb_pad[l].offset + (7 * h + 1 - r2) * GW * 127 + GW - 1
                        pool.dma_start(bias[GW * r2:GW * r2 + GW, h, :].rearrange("p (m k) -> p m k", m=NDR),
                                       bass.AP(rpb_pad.tensor, o, [[126, GW], [GW * 127, NDR], [1, GW]])
                                       ).then_inc(s_ld[l][0], 16)
                    if h % 2:
                        brow(l, 8 + h // 2)
                pool.dma_start(ck[:, :], cache_k[0, l].rearrange("p h d -> p (h d)")).then_inc(s_ld[l][4], 16)
                pool.dma_start(ws[:, :, :], w_s[l].rearrange("h p q -> p h q")).then_inc(s_ld[l][1], 16)
                pool.dma_start(cv[:, :], cache_v[0, l].rearrange("p h d -> p (h d)")).then_inc(s_ld[l][5], 16)
                pool.dma_start(bs[:, :], b_s[l].rearrange("h p -> p h")).then_inc(s_ld[l][2], 16)
                pool.wait_ge(s_modc, 2 * l + 2)
                pool.dma_start(gvb[:, :], bass.AP(g_v.tensor, g_v[l].offset, [[0, P], [1, D_CM]])
                               ).then_inc(s_ld[l][2], 16)
                pool.dma_start(wcb[:, :, :].rearrange("p c j -> p (c j)"),
                               bass.AP(w_conv.tensor, w_conv[l].offset, [[0, P], [1, 3 * D_CV]])
                               ).then_inc(s_ld[l][3], 16)
            pool.wait_ge(s_xr, 9)
            pool.dma_start(x_park.rearrange("(t p) d -> p t d", p=P), x[:, :, :]).then_inc(s_park, 16)
            pool.dma_start(wr[:, :, :], w_router[0].rearrange("(k p) e -> p k e", p=P)).then_inc(s_wr, 16)
            chain(pool.memset(ones[:, :], 1.0))
            chain(pool.memset(before[:, :], 1.0))
            pool.affine_select(out=before[:, :], in_=before[:, :], compare_op=ALU.is_gt, fill=0.0, base=0,
                               pattern=[[1, P]], channel_multiplier=-1).then_inc(s_tri, 1)
            pool.wait_ge(s_acc, NT * NE + 1)
            pool.wait_ge(s_park, 16)
            pool.dma_start(x[:, :, :], x_park.rearrange("(t p) d -> p t d", p=P)).then_inc(s_back, 16)

        @block.scalar
        def _(act):
            chain = Chain(act, s_ac)
            state = {"n": 0}

            def split(n, j=None):
                s = (n if j is None else j) % SPL
                if j is None:
                    act.wait_ge(s_raw[s], 32 * (n // RAW + 1))
                    if n >= SPL:
                        act.wait_ge(s_pe, n - SPL + 1)
                else:
                    e = n
                    act.wait_ge(s_raw[s], e * (32 * N_FFN // RAW) + 32 * ((EXP0 + j) // RAW + 1))
                    act.wait_ge(s_pe, e * N_FFN + (EXP0 + j - SPL + 1))
                act.activation(whi[s][:, :], raw[s][:, :], ACT.Copy).then_inc(s_hi, 1)

            def upto(n):
                while state["n"] <= min(n, EXP0 + 1):
                    split(state["n"])
                    state["n"] += 1

            def squares(r, src):
                for t in range(NT):
                    ins = act.activation(src[1][t], src[0][t], ACT.Square, accum_out=ss[:, r, t:t + 1])
                ins.then_inc(s_ss, 1)

            def root(r):
                act.wait_ge(s_ms, r + 1)
                act.activation(ss[:, r, :], rs[:, r, :], ACT.Sqrt).then_inc(s_sq, 1)

            def rms(r, src, width):
                squares(r, src)
                root(r)

            def norm(s, l, half, n_next):
                r = 5 * l + 3 * half
                if s:
                    act.wait_ge(s_xr, 3 * s)
                else:
                    act.wait_ge(s_x, 32)
                flat = hf[:, :, :].rearrange("p a n -> p (a n)")
                squares(r, ([x[:, t, :] for t in range(NT)], [flat[:, D * t:D * t + D] for t in range(NT)]))
                upto(n_next)
                root(r)
                act.wait_ge(s_modc, 2 * l + half + 1)
                for kt in range(KT):
                    act.wait_ge(s_tr, KT * s + kt + 1)
                    p6 = ps[:, 6 + kt % 2, :]
                    sh, sc = modc[:, 2 * half, kt, :], modc[:, 2 * half + 1, kt, :]
                    act.activation(hf[:, kt, 0:P], p6[:, 0:P], ACT.Identity, bias=sh[:, 0:1], scale=sc[:, 0:1])
                    ins = act.activation(hf[:, kt, P:3 * P], p6[:, P:3 * P], ACT.Identity,
                                         bias=sh[:, 1:2], scale=sc[:, 1:2])
                    ins.then_inc(s_hf, 1)
                    if s == 3:
                        continue
                    act.wait_ge(s_hf, KT * s + kt + 1)
                    act.activation(xhi[:, kt, :], hf[:, kt, :], ACT.Copy).then_inc(s_xhi, 1)

            def residual(s, l, half):
                r = 5 * l + 2 + 2 * half
                if s == 1:
                    act.wait_ge(s_colmm, turned(ADA_B) + HEAD)
                if s < 3:
                    for t in range(NT):
                        if t < NT - 1:
                            act.wait_ge(s_y, 2 * s + t + 1)
                        else:
                            last = ("wout", l, N_WOUT - 1) if half == 0 else ("ffn", 0, N_FFN - 1)
                            act.wait_ge(s_pe, PLACE[last] + 1)
                        act.activation(f[:, t, :], ps[:, 2 * t:2 * t + 2, :].rearrange("p a n -> p (a n)"),
                                       ACT.Copy).then_inc(s_yc, 1)
                    act.wait_ge(s_yc, NT * (s + 1))
                else:
                    act.wait_ge(s_acc, NT * NE + 1)
                flat = hf[:, :, :].rearrange("p a n -> p (a n)")
                junk = [flat[:, D * t:D * t + D] for t in range(NT)]
                rms(r, ([f[:, t, :] for t in range(NT)], junk), D)

            act.wait_ge(s_c, 32)
            chain(act.activation(sil[:, :, :], sil[:, :, :], ACT.Silu))
            act.activation(silh[:, :, :], sil[:, :, :], ACT.Copy).then_inc(s_sil, 1)

            def ffn(T, k, e=None):
                def ahead(j):
                    if e is None:
                        upto(PLACE["ffn", 0, j])
                    else:
                        while state["j"] <= min(j, N_FFN - 1):
                            split(e, state["j"])
                            state["j"] += 1

                state["j"] = 2

                def hi(b):
                    for i in range(2):
                        act.wait_ge(s_ht, k * 2 * GU_B + 2 * b + i + 1)
                        act.activation(hhi[:, 2 * b + i, 0:P * T], ps[:, 6 + i, 0:P * T], ACT.Copy
                                       ).then_inc(s_hhi, 1)

                for b in range(GU_B):
                    ahead(2 * b + 3)
                    if e is None:
                        act.wait_ge(s_pe, PLACE["ffn", 0, 2 * b + 1] + 1)
                    else:
                        act.wait_ge(s_pe, e * N_FFN + (EXP0 + 2 * b + 2))
                    if b:
                        act.wait_ge(s_ht, k * 2 * GU_B + 2 * b)
                    for t in range(T):
                        ins = act.activation(pg[:, t, :], ps[:, 2 * t + b % 2, 0:256], ACT.Silu)
                    ins.then_inc(s_sg, 1)
                    if b:
                        hi(b - 1)
                hi(GU_B - 1)
                for j in range(N_GU, N_FFN):
                    ahead(j)

            def expert(T, e):
                k = e + 1
                for kt in range(KT):
                    act.wait_ge(s_ga, e * KT + kt + 1)
                    act.activation(xhi[:, kt, 0:P * T], ps[:, 6 + kt % 2, 0:P * T], ACT.Copy).then_inc(s_ghi, 1)
                ffn(T, k, e)
                act.wait_ge(s_pe, e * N_FFN + (EXP0 + N_FFN))
                for t in range(T):
                    ins = act.activation(yhi[:, t, :], ps[:, 2 * t:2 * t + 2, :].rearrange("p a n -> p (a n)"),
                                         ACT.Copy)
                ins.then_inc(s_yhi, 1)
                for t in range(T):
                    act.wait_ge(s_pmt, e * NT + t + 1)
                    act.activation(permT[:, t, :], ps[:, 6 + t % 2, 0:NT * P], ACT.Copy).then_inc(s_pmc, 1)
                if T < NT:
                    act.wait_ge(s_pmc, e * NT + T)
                    act.sem_inc(s_pmc, NT - T)

            upto(2 * HEAD - 3)
            for l in range(DEPTH):
                norm(2 * l, l, 0, PLACE["win", l, 0] + 1)
                for b in range(WIN_B):
                    n = PLACE["win", l, min(2 * b + 1, N_WIN - 1)]
                    upto(n + 2)
                    w = 512 if b < 5 else 256
                    for t in range(NT):
                        if t < NT - 1:
                            act.wait_ge(s_win, 2 * WIN_B * l + 2 * b + t + 1)
                        else:
                            act.wait_ge(s_pe, n + 1)
                        act.activation(pr[:, t, 512 * b:512 * b + w], ps[:, 2 * t + b % 2, 0:w], ACT.Copy
                                       ).then_inc(s_pr, 1)
                    if b == 2:
                        act.wait_ge(s_pr, NT * WIN_B * l + 9)
                        act.dma_start(new_k[0, l].rearrange("p h d -> p (h d)"), pr[:, 0, OK:OK + D_ATT]
                                      ).then_inc(s_kv, 16)
                        act.dma_start(new_v[0, l].rearrange("p h d -> p (h d)"), pr[:, 0, OV:OV + D_ATT]
                                      ).then_inc(s_kv, 16)
                for i in range(0, 9, 2):
                    act.wait_ge(s_qk, 9 * l + i + 1)
                    if i == 8:
                        dst, w = ckT[:, :, :].rearrange("p a n -> p (a n)"), 4 * P
                    else:
                        dst, w = (qT if i < 4 else kT)[:, i % 4, :], NT * P
                    act.activation(dst, ps[:, 6 + i % 2, 0:w], ACT.Copy).then_inc(s_qka, 1)
                act.wait_ge(s_pr, NT * WIN_B * (l + 1))
                act.activation(pr[:, :, OU:OU + 512], pr[:, :, OU:OU + 512], ACT.Gelu_apprx_tanh).then_inc(s_gel, 1)
                act.wait_ge(s_gel, l + 1)
                rms(5 * l + 1, ([pr[:, t, OVM:OVM + D_CM] for t in range(NT)],
                                [f[:, t, 0:D_CM] for t in range(NT)]), D_CM)
                def exp(u):
                    w = P if UNITS[u][0] == 0 else NT * P
                    s = u % 4
                    act.wait_ge(s_sm, NU * l + u + 1)
                    if u >= 4:
                        act.wait_ge(s_o, NU * l + u - 3)
                    for a in range(2):
                        ins = act.activation(pS[:, s, a, 0:w], pS[:, s, a, 0:w], ACT.Exp, bias=nm[:, s, 1, a:a + 1],
                                             accum_out=den[:, s, a:a + 1])
                    ins.then_inc(s_ex, 1)

                def pt_copy(u):
                    w = P if UNITS[u][0] == 0 else NT * P
                    act.wait_ge(s_pt, NU * l + u + 1)
                    if u >= 2:
                        act.wait_ge(s_pv, NU * l + u - 1)
                    act.activation(pT[:, u % 2, :, 0:w], ps[:, 4:6, 0:w], ACT.Copy).then_inc(s_ptc, 1)

                for u in range(NU + 2):
                    if u < NU:
                        exp(u)
                    if u >= 2:
                        pt_copy(u - 2)
                for kt in range(KT):
                    act.wait_ge(s_mt, KT * l + kt + 1)
                    act.activation(xhi[:, kt, :], ps[:, 6 + kt % 2, 0:384], ACT.Copy).then_inc(s_mhi, 1)
                n = PLACE["wout", l, N_WOUT - 1] + 2
                upto(n)
                act.wait_ge(s_kv, 32 * (l + 1))
                residual(2 * l, l, 0)
                norm(2 * l + 1, l, 1, n)
                if l == 0:
                    ffn(NT, 0)
                    upto(PLACE["win", 1, 0] + 1)
                    residual(1, 0, 1)
            act.wait_ge(s_park, 16)
            for i in range(6):
                act.wait_ge(s_bt, i + 1)
                t, h = divmod(i, 2)
                act.activation(x[:, t, 512 * h:512 * h + 512], ps[:, 6 + i % 2, :], ACT.Copy).then_inc(s_btc, 1)
            for t in range(NT):
                act.wait_ge(s_rt, 1)
                ins = act.activation(ge[:, t, 1:2], ge[:, t, 0:1], ACT.Exp)
            ins.then_inc(s_rte, 1)
            upto(EXP0 + 1)
            act.wait_ge(s_nt, 1)
            with act.Fori(0, NE) as e:
                T = act.value_load(ntile[0:1, bass.ds(e, 1)], min_val=1, max_val=3)
                with act.If(T < 2):
                    expert(1, e)
                with act.Else():
                    with act.If(T < 3):
                        expert(2, e)
                    with act.Else():
                        expert(3, e)
                with act.If(e < NE - 1):
                    split(e + 1, 0)
                    split(e + 1, 1)
            residual(3, 1, 1)
            for t in range(NT):
                act.wait_ge(s_xr, 9 + t + 1)
                out = y_prompt[0] if t == 0 else y_sample[0, P * (t - 1):P * t, :]
                act.dma_start(out, x[:, t, :]).then_inc(s_out, 16)
            act.wait_ge(s_out, 48)

        @block.vector
        def _(dve):
            chain = Chain(dve, s_dv)
            state = {"n": 0}

            def split(n, j=None):
                s = (n if j is None else j) % SPL
                if j is None:
                    dve.wait_ge(s_hi, n + 1)
                else:
                    dve.wait_ge(s_hi, n * N_FFN + (EXP0 + j + 1))
                dve.tensor_tensor(wlo[s][:, :], raw[s][:, :], whi[s][:, :].bitcast(F32), ALU.subtract
                                  ).then_inc(s_lo, 1)

            def upto(n):
                while state["n"] <= min(n, EXP0 + 1):
                    split(state["n"])
                    state["n"] += 1

            def rms(r, width):
                dve.wait_ge(s_ss, r + 1)
                dve.tensor_scalar(rs[:, r, :], ss[:, r, :], 1.0 / width, EPS, ALU.mult, ALU.add).then_inc(s_ms, 1)
                dve.wait_ge(s_sq, r + 1)
                chain(dve.reciprocal(rs[:, r, :], ss[:, r, :]))

            def build_cs():
                for i in range(4):
                    src = silh[:, :, :].bitcast(F32) if i < 2 else sill[:, :, :]
                    g = i % 2
                    ins = dve.tensor_copy(cS[:, :, 32 * i:32 * i + 32], src[:, :, g:g + 1].to_broadcast([P, KT, 32]))
                ins.then_inc(s_cs, 1)

            def ada(l, i):
                n = PLACE["ada", l, 2 * i + 1]
                upto(n + 2)
                dve.wait_ge(s_pe, n + 1)
                dve.wait_ge(s_brow[i % 2], 16 * (ADA_B // 2 * l + i // 2 + 1))
                mod, h = divmod(ADA_SEQ[i], 2)
                st = ada_stage(l, i)
                row = st[:, 2, 512 * (i % 2):512 * (i % 2) + 512]
                if mod in (2, 5):
                    dve.wait_ge(s_gb, 32 * l + (16 if mod == 2 else 32))
                    gate = (gate_m if mod == 2 else gate_f)[:, 512 * h:512 * h + 512]
                    chain(dve.tensor_tensor(gate, ps[:, 6, :], row, ALU.add))
                    dve.tensor_tensor(gate, gate, st[:, 1, 512 * h:512 * h + 512], ALU.mult).then_inc(s_modr, 1)
                else:
                    if i >= 2:
                        dve.wait_ge(s_colmm, turned(ADA_B) * l + turned(i - 2))
                    dve.tensor_tensor(st[:, 0, 512 * (i % 2):512 * (i % 2) + 512], ps[:, 6, :], row, ALU.add
                                      ).then_inc(s_modr, 1)

            def mod_columns(l, half):
                dve.wait_ge(s_colmm, turned(ADA_B) * l + HEAD * (half + 1))
                dve.wait_ge(s_gcol, 16 * 2 * DEPTH)
                m = 2 * half
                src = [ps[:, 7, 16 * i:16 * i + 16].rearrange("p (k g) -> p k g", g=2) for i in (m, m + 1)]
                dve.tensor_copy(modc[:, m, :, :], src[0])
                for g in range(2):
                    ins = dve.scalar_tensor_tensor(out=modc[:, m + 1, :, g], in0=src[1][:, :, g], scalar=1.0,
                                                   in1=gcol[:, l, half, :], op0=ALU.add, op1=ALU.mult)
                ins.then_inc(s_modc, 1)

            def norm(s, l, half):
                r = 5 * l + 3 * half
                rms(r, D)
                for t in range(NT):
                    dve.tensor_scalar(f[:, t, :], x[:, t, :], rs[:, r, t:t + 1], None, ALU.mult).then_inc(s_xn, 1)
                if s == 0:
                    mod_columns(0, 0)
                for kt in range(KT if s < 3 else 0):
                    dve.wait_ge(s_xhi, KT * s + kt + 1)
                    dve.tensor_tensor(xlo[:, kt, :], hf[:, kt, :], xhi[:, kt, :].bitcast(F32), ALU.subtract
                                      ).then_inc(s_xlo, 1)

            def residual(s, l, half):
                r = 5 * l + 2 + 2 * half
                rms(r, D)
                for t in range(NT):
                    g = min(t, 1)
                    dve.wait_ge(s_gt, 2 * s + g + 1)
                    if s == 3 and t == 0:
                        dve.wait_ge(s_back, 16)
                    chain(dve.scalar_tensor_tensor(
                        out=f[:, t, :], in0=f[:, t, :], scalar=rs[:, r, t:t + 1],
                        in1=ps[:, 2 * g:2 * g + 2, :].rearrange("p a n -> p (a n)"), op0=ALU.mult, op1=ALU.mult))
                    dve.tensor_tensor(x[:, t, :], x[:, t, :], f[:, t, :], ALU.add).then_inc(s_xr, 1)

            dve.wait_ge(s_sil, 1)
            chain(dve.tensor_tensor(sill[:, :, :], sil[:, :, :], silh[:, :, :].bitcast(F32), ALU.subtract))

            def ffn(T, k, e=None):
                def ahead(j):
                    if e is None:
                        upto(PLACE["ffn", 0, j])
                    else:
                        while state["j"] <= min(j, N_FFN - 1):
                            split(e, state["j"])
                            state["j"] += 1

                state["j"] = 2

                def lo(b):
                    for i in range(2):
                        dve.wait_ge(s_hhi, k * 2 * GU_B + 2 * b + i + 1)
                        dve.tensor_tensor(hlo[:, 2 * b + i, 0:P * T], ps[:, 6 + i, 0:P * T],
                                          hhi[:, 2 * b + i, 0:P * T].bitcast(F32), ALU.subtract).then_inc(s_hlo, 1)

                for b in range(GU_B):
                    ahead(2 * b + 3)
                    dve.wait_ge(s_sg, k * GU_B + b + 1)
                    for t in range(T):
                        ins = dve.tensor_tensor(pg[:, t, :], pg[:, t, :], ps[:, 2 * t + b % 2, 256:512], ALU.mult)
                    ins.then_inc(s_pm, 1)
                    if b:
                        lo(b - 1)
                lo(GU_B - 1)
                for j in range(N_GU, N_FFN):
                    ahead(j)
                    if e is None and j - N_GU in ADA_IN_WD:
                        ada(1, ADA_IN_WD[j - N_GU])
                if e is None:
                    mod_columns(1, 0)

            def expert(T, e):
                k = e + 1
                dve.wait_ge(s_cur, e + 1)
                for t in range(NT):
                    ins = dve.tensor_scalar(perm[:, t, 0:P * T], iota[:, 0:P * T], cur[:, 1, t:t + 1],
                                            cur[:, 2, t:t + 1], ALU.is_equal, ALU.mult)
                ins.then_inc(s_perm, 1)
                for kt in range(KT):
                    dve.wait_ge(s_ghi, e * KT + kt + 1)
                    dve.tensor_tensor(xlo[:, kt, 0:P * T], ps[:, 6 + kt % 2, 0:P * T],
                                      xhi[:, kt, 0:P * T].bitcast(F32), ALU.subtract).then_inc(s_glo, 1)
                ffn(T, k, e)
                dve.wait_ge(s_yhi, e + 1)
                for t in range(T):
                    ins = dve.tensor_tensor(ylo[:, t, :], ps[:, 2 * t:2 * t + 2, :].rearrange("p a n -> p (a n)"),
                                            yhi[:, t, :].bitcast(F32), ALU.subtract)
                ins.then_inc(s_ylo, 1)

            build_cs()
            for i in range(HEAD):
                ada(0, i)
            for l in range(DEPTH):
                upto(PLACE["win", l, 0] + 1)
                norm(2 * l, l, 0)
                for i in range(HEAD, ADA_B):
                    ada(l, i)
                mod_columns(l, 1)
                upto(PLACE["win", l, N_WIN - 1] + 2)
                for i in range(1, 9, 2):
                    dve.wait_ge(s_qk, 9 * l + i + 1)
                    dst = qT[:, i, :] if i < 4 else kT[:, i - 4, :]
                    dve.tensor_copy(dst, ps[:, 7, 0:384]).then_inc(s_qkd, 1)
                dve.wait_ge(s_pr, NT * WIN_B * (l + 1))
                dve.tensor_tensor(z[:, :, :], pr[:, :, OC:OC + D_CV], pr[:, :, OH:OH + D_CV], ALU.mult
                                  ).then_inc(s_z, 1)
                dve.wait_ge(s_ld[l][0], 16 * 2 * NH)
                dve.wait_ge(s_const, N_CONST)
                dve.tensor_tensor(bias[:, :, :].rearrange("p h (m k) -> p (h m) k", k=GW),
                                  bias[:, :, :].rearrange("p h (m k) -> p (h m) k", k=GW),
                                  win_mask[:, :].rearrange("p (a k) -> p a k", a=1).to_broadcast([P, NH * NDR, GW]),
                                  ALU.add).then_inc(s_bias, 1)
                dve.wait_ge(s_ld[l][2], 32)
                rms(5 * l + 1, D_CM)
                for t in range(NT):
                    v = pr[:, t, OVM:OVM + D_CM]
                    ins = dve.scalar_tensor_tensor(out=v, in0=v, scalar=rs[:, 5 * l + 1, t:t + 1],
                                                   in1=gvb[:, :], op0=ALU.mult, op1=ALU.mult)
                ins.then_inc(s_vn, 1)
                dve.wait_ge(s_wsp, l + 1)
                dve.tensor_copy(wsT[:, :, :].rearrange("p a n -> p (a n)"), ps[:, 6, :]).then_inc(s_wst, 1)
                dve.wait_ge(s_mix, l + 1)
                for t in range(NT):
                    for h in range(4):
                        u = pr[:, t, OU + 64 * h:OU + 64 * h + 64]
                        ins = dve.scalar_tensor_tensor(out=u, in0=ps[:, t, 64 * h:64 * h + 64],
                                                       scalar=bs[:, h:h + 1], in1=u, op0=ALU.add, op1=ALU.mult)
                ins.then_inc(s_cm, 1)
                dve.wait_ge(s_sh, l + 1)
                dve.wait_ge(s_ld[l][3], 16)
                dve.wait_ge(s_z, l + 1)

                def tap(j):
                    return wcb[:, :, j].rearrange("p (a c) -> p a c", a=1).to_broadcast([P, NT, D_CV])

                yc, yt = pr[:, :, OC:OC + D_CV], pr[:, :, OH:OH + D_CV]
                yb = pr[:, :, OB:OB + D_CV]
                chain(dve.tensor_tensor(yc, z[:, :, :], tap(1), ALU.mult))
                chain(dve.tensor_tensor(yt, ps[:, 3:6, 0:256], tap(0), ALU.mult))
                chain(dve.tensor_tensor(yc, yc, yt, ALU.add))
                chain(dve.tensor_tensor(yt, ps[:, 3:6, 256:512], tap(2), ALU.mult))
                chain(dve.tensor_tensor(yc, yc, yt, ALU.add))
                dve.tensor_tensor(yb, yb, yc, ALU.mult).then_inc(s_cvd, 1)
                dve.wait_ge(s_bias, l + 1)

                def soft(u):
                    t, h = UNITS[u]
                    s, b = u % 4, 2 * (u % 2)
                    dve.wait_ge(s_sc, NU * l + u + 1)
                    if u >= 4:
                        dve.wait_ge(s_pt, NU * l + u - 3)
                    if t == 0:
                        w = P
                        chain(dve.tensor_scalar(pS[:, s, :, 0:P], ps[:, b:b + 2, 0:P], SCALE, None, ALU.mult))
                    else:
                        w = NT * P
                        m0 = 2 - 2 * (t - 1)
                        dve.scalar_tensor_tensor(out=pS[:, s, :, 0:256], in0=ps[:, b:b + 2, 0:256], scalar=SCALE,
                                                 in1=bias[:, h:h + 2, GW * m0:GW * (m0 + 4)],
                                                 op0=ALU.mult, op1=ALU.add)
                        chain(dve.tensor_scalar(pS[:, s, :, 256:384], ps[:, b:b + 2, 256:384], SCALE, None,
                                                ALU.mult))
                    chain(dve.tensor_reduce(nm[:, s, 0, :], pS[:, s, :, 0:w], AX_X, ALU.max))
                    dve.tensor_scalar(nm[:, s, 1, :], nm[:, s, 0, :], -1.0, None, ALU.mult).then_inc(s_sm, 1)

                def out(u):
                    t, h = UNITS[u]
                    s = u % 4
                    dve.wait_ge(s_pv, NU * l + u + 1)
                    chain(dve.reciprocal(rden[:, s, :], den[:, s, :]))
                    dve.tensor_tensor(pr[:, t, 64 * h:64 * h + 128].rearrange("p (a d) -> p a d", a=2),
                                      ps[:, 6 + u % 2, 0:128].rearrange("p (a d) -> p a d", a=2),
                                      rden[:, s, :].rearrange("p (a d) -> p a d", d=1).to_broadcast([P, 2, HD]),
                                      ALU.mult).then_inc(s_o, 1)

                for u in range(NU + 3):
                    if u < NU:
                        soft(u)
                    if u >= 3:
                        out(u - 3)
                for kt in range(KT):
                    dve.wait_ge(s_mhi, KT * l + kt + 1)
                    dve.tensor_tensor(xlo[:, kt, :], ps[:, 6 + kt % 2, 0:384], xhi[:, kt, :].bitcast(F32),
                                      ALU.subtract).then_inc(s_mlo, 1)
                upto(PLACE["wout", l, N_WOUT - 1] + 2)
                residual(2 * l, l, 0)
                norm(2 * l + 1, l, 1)
                if l == 0:
                    dve.wait_ge(s_cvd, 1)
                    build_cs()
                    ffn(NT, 0)
                    upto(PLACE["win", 1, 0] + 1)
                    residual(1, 0, 1)
            dve.wait_ge(s_lg, 1)
            for t in range(NT):
                chain(dve.tensor_copy(lg[:, t, :], ps[:, t, 0:NE]))
                chain(dve.max(m8[:, t, :], lg[:, t, :]))
                ins = dve.tensor_tensor(ge[:, t, 0:1], m8[:, t, 1:2], m8[:, t, 0:1], ALU.subtract)
            ins.then_inc(s_rt, 1)
            for t in range(NT):
                chain(dve.max_index(ix[:, t, :], m8[:, t, :], lg[:, t, :]))
                chain(dve.tensor_copy(ixf[:, t, :], ix[:, t, :]))
            dve.wait_ge(s_rte, 1)
            for t in range(NT):
                chain(dve.tensor_scalar(ge[:, t, 2:3], ge[:, t, 1:2], 1.0, None, ALU.add))
                chain(dve.reciprocal(ge[:, t, 2:3], ge[:, t, 2:3]))
                chain(dve.tensor_tensor(ge[:, t, 3:4], ge[:, t, 1:2], ge[:, t, 2:3], ALU.mult))
                chain(dve.tensor_scalar(hot[:, t, :], iota[:, 0:NE], ixf[:, t, 0:1], None, ALU.is_equal))
                chain(dve.tensor_scalar(hot1[:, t, :], iota[:, 0:NE], ixf[:, t, 1:2], None, ALU.is_equal))
                chain(dve.tensor_scalar(rt[:, 0, t, :], hot1[:, t, :], ge[:, t, 3:4], None, ALU.mult))
                chain(dve.scalar_tensor_tensor(out=rt[:, 0, t, :], in0=hot[:, t, :], scalar=ge[:, t, 2:3],
                                               in1=rt[:, 0, t, :], op0=ALU.mult, op1=ALU.add))
                ins = dve.tensor_tensor(rt[:, 2, t, :], hot[:, t, :], hot1[:, t, :], ALU.add)
            ins.then_inc(s_hot, 1)
            dve.wait_ge(s_pos, 1)
            for t in range(NT):
                chain(dve.tensor_copy(rt[:, 1, t, :], ps[:, t, 64:64 + NE]))
            chain(dve.tensor_scalar(cnt[:, :], ps[:, 3, 0:NE], float(P), None, ALU.is_gt))
            chain(dve.tensor_scalar(lg[:, 0, :], ps[:, 3, 0:NE], float(2 * P), 1.0, ALU.is_gt, ALU.add))
            dve.tensor_tensor(ntile[:, :], cnt[:, :], lg[:, 0, :], ALU.add).then_inc(s_nt, 1)
            dve.wait_ge(s_nt, 1)
            dve.memset(f[:, :, :], 0.0).then_inc(s_acc, 1)
            upto(EXP0 + 1)
            with dve.Fori(0, NE) as e:
                T = dve.value_load(ntile[0:1, bass.ds(e, 1)], min_val=1, max_val=3)
                dve.wait_ge(s_acc, e * NT + 1)
                for i in range(3):
                    for t in range(NT):
                        ins = dve.tensor_copy(cur[:, i, t:t + 1], rt[:, i, t, bass.ds(e, 1)])
                ins.then_inc(s_cur, 1)
                with dve.If(T < 2):
                    expert(1, e)
                with dve.Else():
                    with dve.If(T < 3):
                        expert(2, e)
                    with dve.Else():
                        expert(3, e)
                for t in range(NT):
                    dve.wait_ge(s_scm, e * NT + t + 1)
                    dve.scalar_tensor_tensor(out=f[:, t, :], in0=ps[:, 2 * t:2 * t + 2, :].rearrange("p a n -> p (a n)"),
                                             scalar=cur[:, 0, t:t + 1], in1=f[:, t, :], op0=ALU.mult, op1=ALU.add
                                             ).then_inc(s_acc, 1)
                with dve.If(e < NE - 1):
                    split(e + 1, 0)
                    split(e + 1, 1)
            residual(3, 1, 1)

        @block.tensor
        def _(pe):
            def pe_done(ins):
                ins.then_inc(s_pe, 1)

            def three(out, a_hi, a_lo, w_hi, w_lo, start, stop):
                pe.matmul(out, a_hi, w_hi, start=start, stop=False)
                pe.matmul(out, a_hi, w_lo, start=False, stop=False)
                return pe.matmul(out, a_lo, w_hi, start=False, stop=stop)

            def halves(n, k):
                return (whi[n % SPL][:, :].rearrange("p (k n) -> p k n", k=k),
                        wlo[n % SPL][:, :].rearrange("p (k n) -> p k n", k=k))

            def ada_turn(l, i):
                mod, h = divmod(ADA_SEQ[i], 2)
                if mod in (2, 5):
                    return
                m = [0, 1, None, 2, 3][mod]
                pe.wait_ge(s_modr, ADA_B * l + i + 1)
                for j in range(4):
                    o = 16 * m + 2 * (4 * h + j)
                    a = 512 * (i % 2) + P * j
                    ins = pe.matmul(ps[:, 7, o:o + 2], ada_stage(l, i)[:, 0, a:a + P], sel[:, :],
                                    start=True, stop=True)
                ins.then_inc(s_colmm, 1)

            def ada(l, i):
                if i == 0:
                    pe.wait_ge(s_cs, l + 1)
                if i:
                    pe.wait_ge(s_modr, ADA_B * l + i)
                for h in range(2):
                    n = PLACE["ada", l, 2 * i + h]
                    pe.wait_ge(s_lo, n + 1)
                    hi, lo = halves(n, 4)
                    for k in range(4):
                        a = cS[:, 4 * h + k, :]
                        pe.matmul(ps[:, 6, :], a, hi[:, k, :], start=(h == 0 and k == 0), stop=False)
                        ins = pe.matmul(ps[:, 6, :], a, lo[:, k, :], start=False, stop=(h == 1 and k == 3))
                    pe_done(ins)
                if i not in (0, HEAD):
                    ada_turn(l, i - 1)
                if i == HEAD - 1:
                    ada_turn(l, i)

            def norm(s):
                for kt in range(KT):
                    if kt == 1 and s % 2 == 0:
                        pe.wait_ge(s_modc, s + 1)
                    if kt >= 2:
                        pe.wait_ge(s_hf, KT * s + kt - 1)
                    for t in range(NT):
                        if kt == 0:
                            pe.wait_ge(s_xn, NT * s + t + 1)
                        ins = pe.transpose(ps[:, 6 + kt % 2, P * t:P * t + P], f[:, t, P * kt:P * kt + P], ident[:, :])
                    ins.then_inc(s_tr, 1)

            def win(l):
                for b in range(WIN_B):
                    if b >= 2:
                        pe.wait_ge(s_pr, NT * WIN_B * l + NT * (b - 1))
                    w, kk = (512, 4) if b < 5 else (256, 8)
                    for h in range(2 if b < 5 else 1):
                        n = PLACE["win", l, 2 * b + h]
                        pe.wait_ge(s_lo, n + 1)
                        hi, lo = halves(n, kk)
                        for t in range(NT):
                            for k in range(kk):
                                kt = 4 * h + k
                                if t == 0:
                                    pe.wait_ge(s_xlo, KT * 2 * l + kt + 1)
                                a = P * t
                                last = kt == KT - 1
                                ins = three(ps[:, 2 * t + b % 2, 0:w], xhi[:, kt, a:a + P], xlo[:, kt, a:a + P],
                                            hi[:, k, :], lo[:, k, :], kt == 0, last)
                            if last and t < NT - 1:
                                ins.then_inc(s_win, 1)
                        pe_done(ins)
                        if 2 * b + h in ADA_IN_WIN:
                            ada(l, ADA_IN_WIN[2 * b + h])
                        if 2 * b + h == max(ADA_IN_WIN) + 1:
                            ada_turn(l, ADA_B - 1)

            def mixer(l):
                pe.wait_ge(s_pr, NT * WIN_B * l + 9)
                pe.wait_ge(s_modc, 2 * l + 2)
                for i in range(9):
                    if i >= 2:
                        pe.wait_ge(s_qka if i % 2 == 0 else s_qkd, (5 if i % 2 == 0 else 4) * l + i // 2)
                    if i == 8:
                        pe.wait_ge(s_ld[l][4], 16)
                        for j in range(4):
                            ins = pe.transpose(ps[:, 6, P * j:P * j + P], ck[:, P * j:P * j + P], ident[:, :])
                    else:
                        o = OQ + P * i if i < 4 else OK + P * (i - 4)
                        for t in range(NT):
                            ins = pe.transpose(ps[:, 6 + i % 2, P * t:P * t + P], pr[:, t, o:o + P], ident[:, :])
                    ins.then_inc(s_qk, 1)
                pe.wait_ge(s_qka, 5 * (l + 1))
                pe.wait_ge(s_ld[l][1], 16)
                for h in range(4):
                    ins = pe.transpose(ps[:, 6, P * h:P * h + P], ws[:, h, :], ident[:, :])
                ins.then_inc(s_wsp, 1)
                pe.wait_ge(s_vn, l + 1)
                pe.wait_ge(s_wst, l + 1)
                for t in range(NT):
                    for h in range(4):
                        ins = pe.matmul(ps[:, t, 64 * h:64 * h + 64], wsT[:, h, :],
                                        pr[:, t, OVM + 64 * h:OVM + 64 * h + 64], start=True, stop=True)
                ins.then_inc(s_mix, 1)
                pe.wait_ge(s_z, l + 1)
                for t in range(NT):
                    near = [(0, 0, t), (1, 256, t)]
                    if t == 1:
                        near.append((3, 256, 2))
                    if t == 2:
                        near.insert(1, (2, 0, 1))
                    for i, o, src in near:
                        start = i < 2
                        stop = not ((t == 1 and i == 1) or (t == 2 and i == 0))
                        ins = pe.matmul(ps[:, 3 + t, o:o + 256], shift[:, i, :], z[:, src, :], start=start, stop=stop)
                ins.then_inc(s_sh, 1)
                pe.wait_ge(s_qka, 5 * (l + 1))
                pe.wait_ge(s_qkd, 4 * (l + 1))
                pe.wait_ge(s_cm, l + 1)
                pe.wait_ge(s_cvd, l + 1)
                pe.wait_ge(s_ld[l][5], 16)

                def score(u):
                    t, h = UNITS[u]
                    j = h // 2
                    if u >= 2:
                        pe.wait_ge(s_sm, NU * l + u - 1)
                    for a in range(2):
                        o = ps[:, 2 * (u % 2) + a, :]
                        r = slice(64 * a, 64 * a + 64)
                        q = qT[r, j, P * t:P * t + P]
                        if t == 0:
                            ins = pe.matmul(o[:, 0:P], q, kT[r, j, 0:P], start=True, stop=True)
                        else:
                            pe.matmul(o[:, 0:256], q, kT[r, j, P:3 * P], start=True, stop=True)
                            ins = pe.matmul(o[:, 256:384], q, ckT[r, j, :], start=True, stop=True)
                    ins.then_inc(s_sc, 1)

                def turn(u):
                    pe.wait_ge(s_ex, NU * l + u + 1)
                    if u >= 1:
                        pe.wait_ge(s_ptc, NU * l + u)
                    for a in range(2):
                        for j in range(1 if UNITS[u][0] == 0 else NT):
                            ins = pe.transpose(ps[:, 4 + a, P * j:P * j + P], pS[:, u % 4, a, P * j:P * j + P],
                                               ident[:, :])
                    ins.then_inc(s_pt, 1)

                def value(u):
                    t, h = UNITS[u]
                    pe.wait_ge(s_ptc, NU * l + u + 1)
                    if u >= 2:
                        pe.wait_ge(s_o, NU * l + u - 1)
                    for a in range(2):
                        o = 64 * (h + a)
                        vs = [pr[:, 0, OV + o:OV + o + 64]] if t == 0 else [
                            pr[:, 1, OV + o:OV + o + 64], pr[:, 2, OV + o:OV + o + 64], cv[:, o:o + 64]]
                        for j, v in enumerate(vs):
                            ins = pe.matmul(ps[:, 6 + u % 2, 64 * a:64 * a + 64], pT[:, u % 2, a, P * j:P * j + P], v,
                                            start=(j == 0), stop=(j == len(vs) - 1))
                    ins.then_inc(s_pv, 1)

                for u in range(NU + 3):
                    if u < NU:
                        score(u)
                    if 2 <= u < NU + 2:
                        turn(u - 2)
                    if u >= 3:
                        value(u - 3)
                pe.wait_ge(s_o, NU * (l + 1))
                for kt in range(KT):
                    if kt >= 2:
                        pe.wait_ge(s_mlo, KT * l + kt - 1)
                    o = mix_col(kt)
                    for t in range(NT):
                        ins = pe.transpose(ps[:, 6 + kt % 2, P * t:P * t + P], pr[:, t, o:o + P], ident[:, :])
                    ins.then_inc(s_mt, 1)

            def down(T, hi_of, lo_of, place, nk, wait, s_done, between=None):
                for q in range(nk // 2):
                    wait(q)
                    hi, lo = halves(place(q), 2)
                    for t in range(T):
                        for k in range(2):
                            kt = 2 * q + k
                            for h in range(2):
                                o = slice(512 * h, 512 * h + 512)
                                ins = three(ps[:, 2 * t + h, :], hi_of[:, kt, P * t:P * t + P],
                                            lo_of[:, kt, P * t:P * t + P], hi[:, k, o], lo[:, k, o],
                                            kt == 0, kt == nk - 1)
                        if q == nk // 2 - 1 and t < NT - 1 and s_done is not None:
                            ins.then_inc(s_done, 1)
                    pe_done(ins)
                    if between is not None:
                        between(q)

            def wout(l):
                def wait(q):
                    pe.wait_ge(s_lo, PLACE["wout", l, q] + 1)
                    pe.wait_ge(s_mlo, KT * l + 2 * q + 2)
                down(NT, xhi, xlo, lambda q: PLACE["wout", l, q], KT, wait, s_y)

            def gates(s, gate):
                if s < 3:
                    pe.wait_ge(s_yc, NT * s + 2)
                else:
                    pe.wait_ge(s_acc, NT * NE + 1)
                for g in range(2):
                    for h in range(2):
                        ins = pe.matmul(ps[:, 2 * g + h, :], selb[:, g, :], gate[:, 512 * h:512 * h + 512],
                                        start=True, stop=True)
                    ins.then_inc(s_gt, 1)

            def ffn(T, k, e=None):
                def wait_lo(j):
                    if e is None:
                        pe.wait_ge(s_lo, PLACE["ffn", 0, j] + 1)
                    else:
                        pe.wait_ge(s_lo, e * N_FFN + (EXP0 + j + 1))

                def place(j):
                    return PLACE["ffn", 0, j] if e is None else j

                def head(q):
                    if q in ADA_IN_WD:
                        if q == min(ADA_IN_WD):
                            pe.wait_ge(s_hlo, 2 * GU_B)
                        ada(1, ADA_IN_WD[q])

                def turn(b):
                    pe.wait_ge(s_pm, k * GU_B + b + 1)
                    for i in range(2):
                        if b:
                            pe.wait_ge(s_hlo, k * 2 * GU_B + 2 * (b - 1) + i + 1)
                        for t in range(T):
                            ins = pe.transpose(ps[:, 6 + i, P * t:P * t + P], pg[:, t, P * i:P * i + P], ident[:, :])
                        ins.then_inc(s_ht, 1)

                for b in range(GU_B):
                    if b >= 2:
                        pe.wait_ge(s_pm, k * GU_B + b - 1)
                    for h in range(2):
                        wait_lo(2 * b + h)
                        hi, lo = halves(place(2 * b + h), 4)
                        for t in range(T):
                            for kk in range(4):
                                kt = 4 * h + kk
                                ins = three(ps[:, 2 * t + b % 2, :], xhi[:, kt, P * t:P * t + P],
                                            xlo[:, kt, P * t:P * t + P], hi[:, kk, :], lo[:, kk, :],
                                            kt == 0, kt == KT - 1)
                        pe_done(ins)
                    if b:
                        turn(b - 1)
                turn(GU_B - 1)

                def wait(q):
                    wait_lo(N_GU + q)
                    pe.wait_ge(s_hlo, k * 2 * GU_B + 2 * q + 2)
                down(T, hhi, hlo, lambda q: place(N_GU + q), FK, wait, None if e is not None else s_y,
                     head if e is None else None)

            def expert(T, e):
                k = e + 1
                pe.wait_ge(s_perm, e + 1)
                for kt in range(KT):
                    if kt >= 2:
                        pe.wait_ge(s_glo, e * KT + kt - 1)
                    for t in range(NT):
                        ins = pe.matmul(ps[:, 6 + kt % 2, 0:P * T], x[:, t, P * kt:P * kt + P], perm[:, t, 0:P * T],
                                        start=(t == 0), stop=(t == NT - 1))
                    ins.then_inc(s_ga, 1)
                pe.wait_ge(s_glo, e * KT + KT)
                pe.wait_ge(s_acc, e * NT + 1)
                ffn(T, k, e)
                for t in range(T):
                    if t >= 2:
                        pe.wait_ge(s_pmc, e * NT + 1)
                    for i in range(NT):
                        ins = pe.transpose(ps[:, 6 + t % 2, P * i:P * i + P], perm[:, i, P * t:P * t + P], ident[:, :])
                    ins.then_inc(s_pmt, 1)
                pe.wait_ge(s_ylo, e + 1)
                pe.wait_ge(s_pmc, e * NT + NT)
                if T < NT:
                    pe.sem_inc(s_pmt, NT - T)
                for i in range(NT):
                    for h in range(2):
                        for t in range(T):
                            a, o = permT[:, t, P * i:P * i + P], slice(512 * h, 512 * h + 512)
                            pe.matmul(ps[:, 2 * i + h, :], a, yhi[:, t, o], start=(t == 0), stop=False)
                            ins = pe.matmul(ps[:, 2 * i + h, :], a, ylo[:, t, o], start=False, stop=(t == T - 1))
                    ins.then_inc(s_scm, 1)

            pe.wait_ge(s_const, N_CONST)
            for i in range(HEAD):
                ada(0, i)
            for l in range(DEPTH):
                norm(2 * l)
                win(l)
                mixer(l)
                wout(l)
                gates(2 * l, gate_m)
                norm(2 * l + 1)
                if l == 0:
                    pe.wait_ge(s_xlo, KT * 2)
                    ffn(NT, 0)
                    gates(1, gate_f)
            for i in range(6):
                t, h = divmod(i, 2)
                pe.wait_ge(s_hf, KT * 4)
                if i >= 2:
                    pe.wait_ge(s_btc, i - 1)
                for j in range(4):
                    ins = pe.transpose(ps[:, 6 + i % 2, P * j:P * j + P], hf[:, 4 * h + j, P * t:P * t + P], ident[:, :])
                ins.then_inc(s_bt, 1)
            pe.wait_ge(s_wr, 16)
            for t in range(NT):
                for kt in range(KT):
                    ins = pe.matmul(ps[:, t, 0:NE], hf[:, kt, P * t:P * t + P], wr[:, kt, :],
                                    start=(kt == 0), stop=(kt == KT - 1))
            ins.then_inc(s_lg, 1)
            pe.wait_ge(s_hot, 1)
            pe.wait_ge(s_tri, 1)
            for t in range(NT):
                for i in range(t + 1):
                    pe.matmul(ps[:, t, 64:64 + NE], ones[:, :] if i < t else before[:, :], rt[:, 2, i, :],
                              start=(i == 0), stop=(i == t))
            for t in range(NT):
                ins = pe.matmul(ps[:, 3, 0:NE], ones[:, :], rt[:, 2, t, :], start=(t == 0), stop=(t == NT - 1))
            ins.then_inc(s_pos, 1)
            pe.wait_ge(s_btc, 6)
            pe.wait_ge(s_nt, 1)
            with pe.Fori(0, NE) as e:
                T = pe.value_load(ntile[0:1, bass.ds(e, 1)], min_val=1, max_val=3)
                with pe.If(T < 2):
                    expert(1, e)
                with pe.Else():
                    with pe.If(T < 3):
                        expert(2, e)
                    with pe.Else():
                        expert(3, e)
            gates(3, gate_f)


_INS = ['x_prompt', 'x_sample', 'cache_k', 'cache_v', 'c', 'c_ctx', 'w_ada', 'b_ada', 'norm_g', 'w_in', 'w_out',
        'rpb', 'g_v', 'w_s', 'b_s', 'w_conv', 'w_ffn_gu', 'w_ffn_d', 'w_router', 'w_moe_gu', 'w_moe_d']
_OUTS = [(1, P, D), (1, 2 * P, D), (1, DEPTH, P, NH, HD), (1, DEPTH, P, NH, HD)]


def kernel(**inputs):
    import numpy as _np
    import concourse.bacc as _bacc
    from concourse.bass_utils import run_bass_kernel_spmd as _run

    nc = _bacc.Bacc("TRN2", target_bir_lowering=False, num_devices=1)
    arrays, args = {}, []
    for name in _INS:
        a = _np.ascontiguousarray(inputs[name])
        arrays[f"in_{name}_dram"] = a
        args.append(nc.dram_tensor(f"in_{name}_dram", a.shape, mybir.dt.from_np(a.dtype), kind="ExternalInput").ap())
    for i, shape in enumerate(_OUTS):
        args.append(nc.dram_tensor(f"out_{i}_dram", shape, F32, kind="ExternalOutput").ap())
    args.append(nc.dram_tensor("x_park", (NT * P, D), F32, kind="Internal").ap())
    args.append(nc.dram_tensor("rpb_pad", (DEPTH, 7 * NH, GW, 127), F32, kind="Internal").ap())
    build(nc, *args)
    r = _run(nc, [arrays], core_ids=[0])
    return tuple(r.results[0][f"out_{i}_dram"] for i in range(len(_OUTS)))
```

```python
from contextlib import ExitStack

import concourse.bass as bass
from concourse import mybir

F32 = mybir.dt.float32
F32R = mybir.dt.float32r
I32 = mybir.dt.int32
U32 = mybir.dt.uint32
ALU = mybir.AluOpType
ACT = mybir.ActivationFunctionType
AX_X = mybir.AxisListType.X

P = 128
NT = 3
D = 1024
KT = D // P
DEPTH = 2
HD = 64
NH = 8
D_ATT, D_CM, D_CV = 512, 256, 256
D_IN = 3 * D_ATT + 2 * D_CM + 3 * D_CV
OQ, OK, OV = 0, D_ATT, 2 * D_ATT
OU = 3 * D_ATT
OVM = OU + D_CM
OB = OVM + D_CM
OC = OB + D_CV
OH = OC + D_CV
D_FF = 2816
FK = D_FF // P
NE = 8
N_MOD = 6
EPS = 1e-6
NEG = -1e30
GW = 64
KH, KW = 8, 16
NDR = 6
ROWS = 4
SCALE = HD ** -0.5

CHUNK = 2048
RAW = 3
X_AFTER = 5
SPL = 3
ADA_B = N_MOD * D // 512
WIN_B = 6
N_ADA, N_WIN, N_WOUT = 2 * ADA_B, 11, 4
GU_B = D_FF // 256
N_GU, N_WD = 2 * GU_B, FK // 2
N_FFN = N_GU + N_WD
ADA_SEQ = [0, 1, 2, 3, 4, 5, 10, 11, 6, 7, 8, 9]
HEAD = 4
ADA_IN_WIN = {w: HEAD + w - 1 for w in range(1, 1 + ADA_B - HEAD)}
ADA_IN_WD = {2 * i + 1: i for i in range(HEAD)}


def stream():
    out = [("ada", 0, j) for j in range(2 * HEAD)]
    for l in range(DEPTH):
        for w in range(N_WIN):
            out.append(("win", l, w))
            if w in ADA_IN_WIN:
                out += [("ada", l, 2 * ADA_IN_WIN[w] + h) for h in range(2)]
        out += [("wout", l, q) for q in range(N_WOUT)]
        if l == 0:
            for j in range(N_FFN):
                out.append(("ffn", 0, j))
                if j - N_GU in ADA_IN_WD:
                    out += [("ada", 1, 2 * ADA_IN_WD[j - N_GU] + h) for h in range(2)]
    return out


STREAM = stream()
PLACE = {c: n for n, c in enumerate(STREAM)}
EXP0 = len(STREAM)
assert EXP0 % RAW == 0 and N_FFN % RAW == 0


def turned(i):
    return sum(b // 2 not in (2, 5) for b in ADA_SEQ[:i + 1])


def mix_col(kt):
    return [OQ, OQ + 128, OQ + 256, OQ + 384, OU, OU + 128, OB, OB + 128][kt]


def build(nc, x_prompt, x_sample, cache_k, cache_v, c, c_ctx, w_ada, b_ada, norm_g, w_in, w_out, rpb,
          g_v, w_s, b_s, w_conv, w_ffn_gu, w_ffn_d, w_router, w_moe_gu, w_moe_d,
          y_prompt, y_sample, new_k, new_v, x_park, rpb_pad):
    with ExitStack() as ctx:
        ctx.enter_context(nc.allow_non_contiguous_dma(reason="a few small vectors go to columns"))

        def sb(name, shape, dt=F32):
            return ctx.enter_context(nc.sbuf_tensor(name, shape, dt))

        def sem(name):
            return ctx.enter_context(nc.semaphore(name))

        raw = [sb(f"raw{i}", [P, CHUNK]) for i in range(RAW)]
        whi = [sb(f"whi{i}", [P, CHUNK], F32R) for i in range(SPL)]
        wlo = [sb(f"wlo{i}", [P, CHUNK], F32R) for i in range(SPL)]
        xhi = sb("xhi", [P, KT, NT * P], F32R)
        xlo = sb("xlo", [P, KT, NT * P], F32R)
        x = sb("x", [P, NT, D])
        f = sb("f", [P, NT, D])
        pS = f[:, :, :].rearrange("p t n -> p (t n)").rearrange("p (s h k) -> p s h k", s=4, h=2)
        ident = sb("ident", [P, P])
        iota = sb("iota", [P, NT * P])
        sel = sb("sel", [P, 2])
        selb = sb("selb", [P, 2, P])
        sil = sb("sil", [P, KT, 2])
        silh = sb("silh", [P, KT, 2], F32R)
        sill = sb("sill", [P, KT, 2])
        gcol = sb("gcol", [P, DEPTH, 2, KT])
        modc = sb("modc", [P, 4, KT, 2])
        ss = sb("ss", [P, 10, NT])
        rs = sb("rs", [P, 10, NT])
        nm = sb("nm", [P, 4, 2, 2])
        den = sb("den", [P, 4, 2])
        rden = sb("rden", [P, 4, 2])
        eps = sb("eps", [P, 1])
        gate_f = sb("gate_f", [P, D])
        arena = nc.sbuf_base
        arena += -arena % 64
        end = [arena]

        def at(name, off, shape, dt=F32):
            n = 4
            for s in shape[1:]:
                n *= s
            end[0] = max(end[0], arena + off + n)
            assert arena + off + n <= nc.sbuf_usable_end, (name, arena + off + n, nc.sbuf_usable_end)
            return nc.alloc_sbuf_tensor_at(name, shape, dt, offset=arena + off)

        hf = at("hf", 0, [P, KT, NT * P])
        pr = at("pr", 0, [P, NT, D_IN])
        qT = at("qT", 33792, [P, 4, NT * P])
        kT = at("kT", 39936, [P, 4, NT * P])
        stage = at("stage", 33792, [P, NT, D])
        ckT = at("ckT", 46080, [P, 4, P])
        bias = at("bias", 48128, [P, NH, NDR * GW])
        cv = at("cv", 60416, [P, D_ATT])
        ck = at("ck", 62464, [P, D_ATT])
        pT = at("pT", 62464, [P, 2, 2, NT * P])
        z = at("z", 65536, [P, NT, D_CV])
        cS = at("cS", 70656, [P, KT, P], F32R)
        ws = at("ws", 68608, [P, 4, P])
        wsT = at("wsT", 68608, [P, 4, P])
        gvb = at("gvb", 64512, [P, D_CM])
        wcb = at("wcb", 71680, [P, D_CV, 3])
        bs = at("bs", 74752, [P, 4])
        gate_m = at("gate_m", 74784, [P, D])
        shift = at("shift", 78912, [P, 4, P])
        win_mask = at("win_mask", 80960, [P, GW])
        hhi = at("hhi", 0, [P, FK, NT * P], F32R)
        hlo = at("hlo", 33792, [P, FK, NT * P], F32R)
        pg = at("pg", 67584, [P, NT, 256])
        perm = at("perm", 70656, [P, NT, NT * P])
        yhi = at("yhi", 0, [P, NT, D], F32R)
        ylo = at("ylo", 12288, [P, NT, D], F32R)
        junk = at("junk", 24576, [P, D])
        permT = at("permT", 76928, [P, NT, NT * P], F32R)
        wr = at("wr", 33792, [P, KT, NE])
        lg = at("lg", 34048, [P, NT, NE])
        m8 = at("m8", 34144, [P, NT, NE])
        ix = at("ix", 34240, [P, NT, NE], U32)
        ixf = at("ixf", 34336, [P, NT, NE])
        hot = at("hot", 34432, [P, NT, NE])
        ge = at("ge", 34528, [P, NT, 4])
        hot1 = at("hot1", 34624, [P, NT, NE])
        rt = at("rt", 75264, [P, NE + 1, 3, NT])
        cnt = at("cnt", 75616, [P, NE])
        ntile = at("ntile", 75648, [P, NE + 1], I32)
        cur = at("cur", 75712, [P, 3, NT])
        gate_e = at("gate_e", 75776, [P, NT])
        ones = at("ones", 75904, [P, P])
        before = at("before", 76416, [P, P])
        pad = at("pad", 60416, [P, 127])

        ps = ctx.enter_context(nc.psum_tensor("ps", [P, 8, 512], F32))

        s_const = sem("s_const")
        s_x = sem("s_x")
        s_c = sem("s_c")
        s_gcol = sem("s_gcol")
        s_raw = [sem(f"s_raw{i}") for i in range(RAW)]
        s_hi = sem("s_hi")
        s_lo = sem("s_lo")
        s_pe = sem("s_pe")
        s_dv = sem("s_dv")
        s_ac = sem("s_ac")
        s_po = sem("s_po")
        s_sil = sem("s_sil")
        s_cs = sem("s_cs")
        s_brow = [sem(f"s_brow{i}") for i in range(2)]
        s_gb = sem("s_gb")
        s_modr = sem("s_modr")
        s_colmm = sem("s_colmm")
        s_modc = sem("s_modc")
        s_ss = sem("s_ss")
        s_sq = sem("s_sq")
        s_xn = sem("s_xn")
        s_tr = sem("s_tr")
        s_hf = sem("s_hf")
        s_xhi = sem("s_xhi")
        s_xlo = sem("s_xlo")
        s_win = sem("s_win")
        s_pr = sem("s_pr")
        s_kv = sem("s_kv")
        s_ld = [[sem(f"s_ld{l}_{n}") for n in range(6)] for l in range(DEPTH)]
        s_pad = sem("s_pad")
        s_bias = sem("s_bias")
        s_gel = sem("s_gel")
        s_wsp = sem("s_wsp")
        s_wst = sem("s_wst")
        s_vn = sem("s_vn")
        s_mix = sem("s_mix")
        s_cm = sem("s_cm")
        s_z = sem("s_z")
        s_sh = sem("s_sh")
        s_cvd = sem("s_cvd")
        s_qk = sem("s_qk")
        s_qka = sem("s_qka")
        s_qkd = sem("s_qkd")
        s_sc = sem("s_sc")
        s_sm = sem("s_sm")
        s_ex = sem("s_ex")
        s_pt = sem("s_pt")
        s_ptc = sem("s_ptc")
        s_pv = sem("s_pv")
        s_o = sem("s_o")
        s_mt = sem("s_mt")
        s_mhi = sem("s_mhi")
        s_mlo = sem("s_mlo")
        s_y = sem("s_y")
        s_gtc = sem("s_gtc")
        s_gt = sem("s_gt")
        s_xr = sem("s_xr")
        s_sg = sem("s_sg")
        s_pm = sem("s_pm")
        s_ht = sem("s_ht")
        s_hhi = sem("s_hhi")
        s_hlo = sem("s_hlo")
        s_park = sem("s_park")
        s_back = sem("s_back")
        s_wr = sem("s_wr")
        s_bt = sem("s_bt")
        s_btc = sem("s_btc")
        s_lg = sem("s_lg")
        s_rt = sem("s_rt")
        s_rte = sem("s_rte")
        s_hot = sem("s_hot")
        s_cur = sem("s_cur")
        s_gte = sem("s_gte")
        s_tri = sem("s_tri")
        s_pos = sem("s_pos")
        s_nt = sem("s_nt")
        s_perm = sem("s_perm")
        s_ga = sem("s_ga")
        s_ghi = sem("s_ghi")
        s_glo = sem("s_glo")
        s_yhi = sem("s_yhi")
        s_ylo = sem("s_ylo")
        s_pmt = sem("s_pmt")
        s_pmc = sem("s_pmc")
        s_scm = sem("s_scm")
        s_acc = sem("s_acc")
        s_out = sem("s_out")

        N_CONST = 11
        SPLITS_IN_GATHER = {1: 1, 3: 2}
        GATHER_BANK = [6, 7, 0, 1, 2, 3, 4, 5]

        UNITS = [(t, h) for t in (1, 2, 0) for h in range(0, NH, 2)]
        NU = len(UNITS)

        def chunk_src(n):
            def rows(w, k):
                w = w.rearrange("(k p) n -> p k n", p=P)
                return [w[:, 0:k // 2, :], w[:, k // 2:k, :]], k

            kind, l, j = STREAM[n]
            b, h = divmod(j, 2)
            if kind == "ada":
                b = ADA_SEQ[b]
                return rows(w_ada[l, 512 * h:512 * h + 512, 512 * b:512 * b + 512], 4)
            if kind == "win":
                if b == 5:
                    return rows(w_in[l, :, 2560:2816], 8)
                return rows(w_in[l, 512 * h:512 * h + 512, 512 * b:512 * b + 512], 4)
            if kind == "wout":
                return rows(w_out[l, 256 * j:256 * j + 256, :], 2)
            return ffn_src(w_ffn_gu[0], w_ffn_d[0], j)

        def ada_stage(l, i):
            return f if l and i < HEAD else stage

        def ffn_src(gu, dn, j):
            if j < N_GU:
                b, h = divmod(j, 2)
                v = gu.rearrange("(k p) n -> p k n", p=P)
                return [v[:, 4 * h:4 * h + 4, o + 256 * b:o + 256 * b + 256] for o in (0, D_FF)], 0
            q = j - N_GU
            v = dn.rearrange("(k p) n -> p k n", p=P)
            return [v[:, 2 * q:2 * q + 1, :], v[:, 2 * q + 1:2 * q + 2, :]], 2

        def raw_parts(i, k):
            if k == 0:
                v = raw[i][:, :].rearrange("p (k n) -> p k n", k=4)
                return [v[:, :, 0:256], v[:, :, 256:512]]
            v = raw[i][:, :].rearrange("p (k n) -> p k n", k=k)
            return [v[:, 0:k // 2, :], v[:, k // 2:k, :]]

        class Chain:

            def __init__(self, eng, s):
                self.eng, self.s, self.n = eng, s, 0

            def __call__(self, ins):
                self.n += 1
                ins.then_inc(self.s, 1)
                self.eng.wait_ge(self.s, self.n)

        def by_tiles(eng, T, part, e, none=None):
            with eng.If(T < 2):
                if none is not None:
                    with eng.If(T > 0):
                        part(1, e)
                    with eng.Else():
                        none()
                else:
                    part(1, e)
            with eng.Else():
                with eng.If(T < 3):
                    part(2, e)
                with eng.Else():
                    part(3, e)

        block = ctx.enter_context(nc.Block())

        @block.sync
        def _(sp):
            def load(n):
                if n >= RAW:
                    sp.wait_ge(s_lo, n - RAW + 1)
                src, k = chunk_src(n)
                for to, of in zip(raw_parts(n % RAW, k), src):
                    sp.dma_start(to, of).then_inc(s_raw[n % RAW], 16)

            sp.dma_start(sil[:, :, 0], c_ctx.rearrange("(k p) -> p k", p=P)).then_inc(s_c, 16)
            sp.dma_start(sil[:, :, 1], c[0].rearrange("(k p) -> p k", p=P)).then_inc(s_c, 16)
            for n in range(X_AFTER):
                load(n)
            sp.dma_start(x[:, 0, :], x_prompt[0]).then_inc(s_x, 16)
            sp.dma_start(x[:, 1:3, :], x_sample[0].rearrange("(t p) d -> p t d", p=P)).then_inc(s_x, 16)
            for n in range(X_AFTER, EXP0):
                load(n)
            with sp.Fori(0, NE) as e:
                gu = w_moe_gu[0, bass.ds(e, 1), :, :].rearrange("e k n -> (e k) n")
                dn = w_moe_d[0, bass.ds(e, 1), :, :].rearrange("e k n -> (e k) n")
                for j in range(N_FFN):
                    sp.wait_ge(s_lo, e * N_FFN + (EXP0 + j - RAW + 1))
                    src, k = ffn_src(gu, dn, j)
                    for to, of in zip(raw_parts(j % RAW, k), src):
                        sp.dma_start(to, of).then_inc(s_raw[j % RAW], 16)

        @block.gpsimd
        def _(pool):
            chain = Chain(pool, s_po)
            for l in range(DEPTH):
                for i in range(2):
                    pool.dma_start(gcol[:, l, i, :], norm_g[l, 2 * i].rearrange("(k p) -> p k", p=P)
                                   ).then_inc(s_gcol, 16)

            def clear_brow(l, i):
                chain(pool.memset(ada_stage(l, i)[:, 2, :], 0.0))

            def brow(l, i):
                if i >= 2:
                    pool.wait_ge(s_modr, ADA_B * l + i - 1)
                o = b_ada[l, 512 * ADA_SEQ[i]:512 * ADA_SEQ[i] + 512].offset
                pool.dma_start(ada_stage(l, i)[0:33:32, 2, 512 * (i % 2):512 * (i % 2) + 512],
                               bass.AP(b_ada.tensor, o, [[0, 2], [1, 512]])).then_inc(s_brow[i % 2], 16)

            def norm_row(l, j):
                pool.dma_start(stage[:, 1, :], bass.AP(norm_g.tensor, norm_g[l, j, :].offset, [[0, P], [1, D]])
                               ).then_inc(s_gb, 16)

            clear_brow(0, 0)
            brow(0, 0)
            brow(0, 1)
            const = Chain(pool, s_const)
            chain(pool.memset(ident[:, :], 0.0))
            chain(pool.memset(shift[:, :, :], 0.0))
            chain(pool.memset(sel[:, :], 0.0))
            chain(pool.memset(win_mask[:, :], 0.0))
            const(pool.memset(eps[:, :], EPS))
            const(pool.iota(iota[:, :], [[1, NT * P]], base=0, channel_multiplier=0,
                            allow_small_or_imprecise_dtypes=True))
            const(pool.affine_select(out=ident[:, :], in_=ident[:, :], compare_op=ALU.not_equal, fill=1.0,
                                     base=0, pattern=[[-1, P]], channel_multiplier=1))
            for i, base in enumerate((1, -1, -(P - 1), P - 1)):
                const(pool.affine_select(out=shift[:, i, :], in_=shift[:, i, :], compare_op=ALU.not_equal,
                                         fill=1.0, base=base, pattern=[[-1, P]], channel_multiplier=1))
            for o in (0, 64):
                chain(pool.affine_select(out=sel[:, :], in_=sel[:, :], compare_op=ALU.not_equal, fill=1.0,
                                         base=-o, pattern=[[-32, 2]], channel_multiplier=1))
            for g in range(2):
                const(pool.tensor_copy(selb[:, g, :], sel[:, g:g + 1].to_broadcast([P, P])))
            for o in (0, GW):
                m = win_mask[o:o + GW, 0:GW - KW]
                chain(pool.affine_select(out=m, in_=m, compare_op=ALU.is_ge, fill=NEG, base=KW // 2,
                                         pattern=[[1, GW - KW]], channel_multiplier=-1))
                m = win_mask[o:o + GW, KW:GW]
                const(pool.affine_select(out=m, in_=m, compare_op=ALU.is_ge, fill=NEG, base=KW // 2 - 1 - KW,
                                         pattern=[[-1, GW - KW]], channel_multiplier=1))

            for l in range(DEPTH):
                if l:
                    pool.wait_ge(s_tr, 2 * KT)
                    clear_brow(l, 0)
                    brow(l, 0)
                    brow(l, 1)
                brow(l, 2)
                brow(l, 3)
                if l:
                    pool.wait_ge(s_xr, 6)
                    clear_brow(l, HEAD)
                norm_row(l, 1)
                brow(l, 4)
                brow(l, 5)
                chain(pool.memset(pad[:, :], NEG))
                for h in range(NH):
                    pool.dma_start(pad[7 * h:7 * h + 7, 48:79], rpb[l, h, 4:11, :]).then_inc(s_pad, 16)
                pool.wait_ge(s_pad, (16 * NH + 16) * (l + 1) - 16)
                pool.dma_start(rpb_pad[l], pad[0:56, :].rearrange("p (a k) -> p a k", a=1).to_broadcast([56, GW, 127])
                               ).then_inc(s_pad, 16)
                brow(l, 6)
                brow(l, 7)
                norm_row(l, 3)
                pool.wait_ge(s_pad, (16 * NH + 16) * (l + 1))
                for h in range(NH):
                    for r2 in range(2):
                        o = rpb_pad[l].offset + (7 * h + 1 - r2) * GW * 127 + GW - 1
                        pool.dma_start(bias[GW * r2:GW * r2 + GW, h, :].rearrange("p (m k) -> p m k", m=NDR),
                                       bass.AP(rpb_pad.tensor, o, [[126, GW], [GW * 127, NDR], [1, GW]])
                                       ).then_inc(s_ld[l][0], 16)
                brow(l, 8)
                pool.dma_start(gvb[:, :], bass.AP(g_v.tensor, g_v[l].offset, [[0, P], [1, D_CM]])
                               ).then_inc(s_ld[l][2], 16)
                pool.dma_start(ck[:, :], cache_k[0, l].rearrange("p h d -> p (h d)")).then_inc(s_ld[l][4], 16)
                pool.dma_start(ws[:, :, :], w_s[l].rearrange("h p q -> p h q")).then_inc(s_ld[l][1], 16)
                pool.dma_start(cv[:, :], cache_v[0, l].rearrange("p h d -> p (h d)")).then_inc(s_ld[l][5], 16)
                pool.dma_start(bs[:, :], b_s[l].rearrange("h p -> p h")).then_inc(s_ld[l][2], 16)
                for i in range(9, ADA_B):
                    brow(l, i)
                pool.wait_ge(s_modc, 2 * l + 2)
                pool.dma_start(wcb[:, :, :].rearrange("p c j -> p (c j)"),
                               bass.AP(w_conv.tensor, w_conv[l].offset, [[0, P], [1, 3 * D_CV]])
                               ).then_inc(s_ld[l][3], 16)
            pool.wait_ge(s_mlo, 2 * KT)
            pool.dma_start(wr[:, :, :], w_router[0].rearrange("(k p) e -> p k e", p=P)).then_inc(s_wr, 16)
            pool.wait_ge(s_xr, 9)
            pool.dma_start(x_park.rearrange("(t p) d -> p t d", p=P), x[:, :, :]).then_inc(s_park, 16)
            chain(pool.memset(ones[:, :], 1.0))
            chain(pool.memset(before[:, :], 1.0))
            pool.affine_select(out=before[:, :], in_=before[:, :], compare_op=ALU.is_gt, fill=0.0, base=0,
                               pattern=[[1, P]], channel_multiplier=-1).then_inc(s_tri, 1)
            pool.wait_ge(s_ga, NE * KT)
            pool.wait_ge(s_park, 16)
            pool.dma_start(x[:, :, :], x_park.rearrange("(t p) d -> p t d", p=P)).then_inc(s_back, 16)

        @block.scalar
        def _(act):
            chain = Chain(act, s_ac)
            state = {"n": 0}

            def split(n, j=None):
                s = (n if j is None else j) % SPL
                if j is None:
                    act.wait_ge(s_raw[s], 32 * (n // RAW + 1))
                    if n >= SPL:
                        act.wait_ge(s_pe, n - SPL + 1)
                else:
                    e = n
                    act.wait_ge(s_raw[s], e * (32 * N_FFN // RAW) + 32 * ((EXP0 + j) // RAW + 1))
                    act.wait_ge(s_pe, e * N_FFN + (EXP0 + j - SPL + 1))
                act.activation(whi[s][:, :], raw[s][:, :], ACT.Copy).then_inc(s_hi, 1)

            def upto(n):
                while state["n"] <= min(n, EXP0 + 2):
                    split(state["n"])
                    state["n"] += 1

            def rms(r, t, src, junk, width):
                act.activation(junk, src, ACT.Square, accum_out=ss[:, r, t:t + 1]).then_inc(s_ss, 1)
                act.wait_ge(s_ss, NT * r + t + 1)
                act.activation(rs[:, r, t:t + 1], ss[:, r, t:t + 1], ACT.Sqrt, bias=eps[:, 0:1], scale=1.0 / width
                               ).then_inc(s_sq, 1)

            def norm(s, l, half, n_next):
                r = 5 * l + 3 * half
                flat = hf[:, :, :].rearrange("p a n -> p (a n)")
                if s == 0:
                    act.wait_ge(s_x, 32)
                    act.wait_ge(s_const, N_CONST)
                for t in range(NT):
                    if s:
                        act.wait_ge(s_xr, NT * (s - 1) + t + 1)
                    rms(r, t, x[:, t, :], flat[:, D * t:D * t + D], D)
                upto(n_next)
                act.wait_ge(s_modc, 2 * l + half + 1)
                for kt in range(KT):
                    act.wait_ge(s_tr, KT * s + kt + 1)
                    p6 = ps[:, 6 + kt % 2, :]
                    sh, sc = modc[:, 2 * half, kt, :], modc[:, 2 * half + 1, kt, :]
                    act.activation(hf[:, kt, 0:P], p6[:, 0:P], ACT.Identity, bias=sh[:, 0:1], scale=sc[:, 0:1])
                    ins = act.activation(hf[:, kt, P:3 * P], p6[:, P:3 * P], ACT.Identity,
                                         bias=sh[:, 1:2], scale=sc[:, 1:2])
                    ins.then_inc(s_hf, 1)

            def residual(s, l, half):
                r = 5 * l + 2 + 2 * half
                flat = hf[:, :, :].rearrange("p a n -> p (a n)")
                for t in range(NT):
                    if s == 3:
                        act.wait_ge(s_acc, NT * NE + t + 1)
                        src = f[:, t, :]
                    else:
                        if t < NT - 1:
                            act.wait_ge(s_y, 2 * s + t + 1)
                        else:
                            last = ("wout", l, N_WOUT - 1) if half == 0 else ("ffn", 0, N_FFN - 1)
                            act.wait_ge(s_pe, PLACE[last] + 1)
                        src = ps[:, 2 * t:2 * t + 2, :].rearrange("p a n -> p (a n)")
                    rms(r, t, src, flat[:, D * t:D * t + D] if s < 3 else junk[:, :], D)

            def gates(s):
                for i in range(4):
                    act.wait_ge(s_gt, 4 * s + i + 1)
                    act.activation(f[:, i // 2, 512 * (i % 2):512 * (i % 2) + 512], ps[:, 6 + i % 2, :], ACT.Copy
                                   ).then_inc(s_gtc, 1)

            act.wait_ge(s_c, 32)
            chain(act.activation(sil[:, :, :], sil[:, :, :], ACT.Silu))
            act.activation(silh[:, :, :], sil[:, :, :], ACT.Copy).then_inc(s_sil, 1)

            def ahead(j, e):
                if e is None:
                    upto(PLACE["ffn", 0, j])
                else:
                    while state["j"] <= j:
                        split(e, state["j"])
                        state["j"] += 1

            def gate_up(T, k, e=None):
                state["j"] = 3

                def hi(b):
                    for i in range(2):
                        act.wait_ge(s_ht, k * 2 * GU_B + 2 * b + i + 1)
                        act.activation(hhi[:, 2 * b + i, 0:P * T], ps[:, 6 + i, 0:P * T], ACT.Copy
                                       ).then_inc(s_hhi, 1)

                for b in range(GU_B):
                    ahead(2 * b + 3, e)
                    if e is None:
                        act.wait_ge(s_pe, PLACE["ffn", 0, 2 * b + 1] + 1)
                    else:
                        act.wait_ge(s_pe, e * N_FFN + (EXP0 + 2 * b + 2))
                    if b:
                        act.wait_ge(s_ht, k * 2 * GU_B + 2 * b)
                    for t in range(T):
                        ins = act.activation(pg[:, t, :], ps[:, 2 * t + b % 2, 0:256], ACT.Silu)
                    ins.then_inc(s_sg, 1)
                    if b:
                        hi(b - 1)
                ahead(N_GU + 2, e)
                hi(GU_B - 1)

            def gather(T, e, splits=()):
                for kt in range(KT):
                    if kt in splits:
                        split(e, splits[kt])
                    act.wait_ge(s_ga, e * KT + kt + 1)
                    act.activation(xhi[:, kt, 0:P * T], ps[:, GATHER_BANK[kt], 0:P * T], ACT.Copy
                                   ).then_inc(s_ghi, 1)

            def gather_next(T, e):
                gather(T, e, SPLITS_IN_GATHER)

            def expert(T, e):
                for t in range(T):
                    act.wait_ge(s_pmt, e * NT + t + 1)
                    act.activation(permT[:, t, :], ps[:, 6 + t % 2, 0:NT * P], ACT.Copy).then_inc(s_pmc, 1)
                if T < NT:
                    act.wait_ge(s_pmc, e * NT + T)
                    act.sem_inc(s_pmc, NT - T)
                gate_up(T, e + 1, e)
                ahead(N_FFN - 1, e)
                with act.If(e < NE - 1):
                    split(e + 1, 0)
                act.wait_ge(s_pe, e * N_FFN + (EXP0 + N_FFN))
                for t in range(T):
                    ins = act.activation(yhi[:, t, :], ps[:, 2 * t:2 * t + 2, :].rearrange("p a n -> p (a n)"),
                                         ACT.Copy)
                ins.then_inc(s_yhi, 1)

            upto(2 * HEAD - 1)
            for l in range(DEPTH):
                norm(2 * l, l, 0, PLACE["win", l, 0] + 1)
                for b in range(WIN_B):
                    n = PLACE["win", l, min(2 * b + 1, N_WIN - 1)]
                    upto(n + 2)
                    w = 512 if b < 5 else 256
                    for t in range(NT):
                        if t < NT - 1:
                            act.wait_ge(s_win, 2 * WIN_B * l + 2 * b + t + 1)
                        else:
                            act.wait_ge(s_pe, n + 1)
                        act.activation(pr[:, t, 512 * b:512 * b + w], ps[:, 2 * t + b % 2, 0:w], ACT.Copy
                                       ).then_inc(s_pr, 1)
                    if b == 2:
                        act.wait_ge(s_pr, NT * WIN_B * l + 9)
                        act.dma_start(new_k[0, l].rearrange("p h d -> p (h d)"), pr[:, 0, OK:OK + D_ATT]
                                      ).then_inc(s_kv, 16)
                        act.dma_start(new_v[0, l].rearrange("p h d -> p (h d)"), pr[:, 0, OV:OV + D_ATT]
                                      ).then_inc(s_kv, 16)
                    if b == 4:
                        act.wait_ge(s_pr, NT * WIN_B * l + 12)
                        act.activation(pr[:, :, OU:OU + 512], pr[:, :, OU:OU + 512], ACT.Gelu_apprx_tanh
                                       ).then_inc(s_gel, 1)
                        act.wait_ge(s_gel, l + 1)
                        for t in range(NT):
                            rms(5 * l + 1, t, pr[:, t, OVM:OVM + D_CM], f[:, t, 0:D_CM], D_CM)
                for i in range(0, 9, 2):
                    act.wait_ge(s_qk, 9 * l + i + 1)
                    if i == 8:
                        dst, w = ckT[:, :, :].rearrange("p a n -> p (a n)"), 4 * P
                    else:
                        dst, w = (qT if i < 4 else kT)[:, i % 4, :], NT * P
                    act.activation(dst, ps[:, 6 + i % 2, 0:w], ACT.Copy).then_inc(s_qka, 1)
                def exp(u):
                    w = P if UNITS[u][0] == 0 else NT * P
                    s = u % 4
                    act.wait_ge(s_sm, NU * l + u + 1)
                    if u >= 4:
                        act.wait_ge(s_o, NU * l + u - 3)
                    for a in range(2):
                        ins = act.activation(pS[:, s, a, 0:w], pS[:, s, a, 0:w], ACT.Exp, bias=nm[:, s, 1, a:a + 1],
                                             accum_out=den[:, s, a:a + 1])
                    ins.then_inc(s_ex, 1)

                def pt_copy(u):
                    w = P if UNITS[u][0] == 0 else NT * P
                    act.wait_ge(s_pt, NU * l + u + 1)
                    if u >= 2:
                        act.wait_ge(s_pv, NU * l + u - 1)
                    act.activation(pT[:, u % 2, :, 0:w], ps[:, 4:6, 0:w], ACT.Copy).then_inc(s_ptc, 1)

                for u in range(NU + 2):
                    if u < NU:
                        exp(u)
                    if u >= 2:
                        pt_copy(u - 2)
                for kt in range(KT):
                    act.wait_ge(s_mt, KT * l + kt + 1)
                    act.activation(xhi[:, kt, :], ps[:, 6 + kt % 2, 0:384], ACT.Copy).then_inc(s_mhi, 1)
                n = PLACE["wout", l, N_WOUT - 1] + 2
                upto(n - 1)
                gates(2 * l)
                upto(n)
                act.wait_ge(s_kv, 32 * (l + 1))
                residual(2 * l, l, 0)
                norm(2 * l + 1, l, 1, n)
                if l == 0:
                    gate_up(NT, 0)
                    ahead(N_FFN - 1, None)
                    gates(1)
                    upto(PLACE["win", 1, 0] + 1)
                    residual(1, 0, 1)
            act.wait_ge(s_rt, 1)
            act.activation(ge[:, :, 1], ge[:, :, 0], ACT.Exp).then_inc(s_rte, 1)
            act.wait_ge(s_park, 16)
            for i in range(6):
                act.wait_ge(s_bt, i + 1)
                t, h = divmod(i, 2)
                act.activation(x[:, t, 512 * h:512 * h + 512], ps[:, 6 + i % 2, :], ACT.Copy).then_inc(s_btc, 1)
            upto(EXP0 + 2)
            act.wait_ge(s_nt, 1)
            T0 = act.value_load(ntile[0:1, 0:1], min_val=0, max_val=3)
            by_tiles(act, T0, gather, 0)
            with act.Fori(0, NE) as e:
                T = act.value_load(ntile[0:1, bass.ds(e, 1)], min_val=0, max_val=3)
                next_T = act.value_load(ntile[0:1, bass.ds(e + 1, 1)], min_val=0, max_val=3)
                by_tiles(act, T, expert, e)
                by_tiles(act, next_T, gather_next, e + 1, lambda: None)
            residual(3, 1, 1)
            for t in range(NT):
                act.wait_ge(s_xr, 9 + t + 1)
                out = y_prompt[0] if t == 0 else y_sample[0, P * (t - 1):P * t, :]
                act.dma_start(out, x[:, t, :]).then_inc(s_out, 16)
            act.wait_ge(s_out, 48)

        @block.vector
        def _(dve):
            chain = Chain(dve, s_dv)
            state = {"n": 0}

            def split(n, j=None):
                s = (n if j is None else j) % SPL
                if j is None:
                    dve.wait_ge(s_hi, n + 1)
                else:
                    dve.wait_ge(s_hi, n * N_FFN + (EXP0 + j + 1))
                dve.tensor_tensor(wlo[s][:, :], raw[s][:, :], whi[s][:, :].bitcast(F32), ALU.subtract
                                  ).then_inc(s_lo, 1)

            def upto(n):
                while state["n"] <= min(n, EXP0 + 2):
                    split(state["n"])
                    state["n"] += 1

            def inverse_rms(r, t):
                dve.wait_ge(s_sq, NT * r + t + 1)
                chain(dve.reciprocal(rs[:, r, t:t + 1], rs[:, r, t:t + 1]))

            def build_cs():
                for i in range(4):
                    src = silh[:, :, :].bitcast(F32) if i < 2 else sill[:, :, :]
                    g = i % 2
                    ins = dve.tensor_copy(cS[:, :, 32 * i:32 * i + 32], src[:, :, g:g + 1].to_broadcast([P, KT, 32]))
                ins.then_inc(s_cs, 1)

            def ada(l, i):
                n = PLACE["ada", l, 2 * i + 1]
                upto(n + 2)
                dve.wait_ge(s_pe, n + 1)
                dve.wait_ge(s_brow[i % 2], 16 * (ADA_B // 2 * l + i // 2 + 1))
                mod, h = divmod(ADA_SEQ[i], 2)
                st = ada_stage(l, i)
                row = st[:, 2, 512 * (i % 2):512 * (i % 2) + 512]
                if mod in (2, 5):
                    dve.wait_ge(s_gb, 32 * l + (16 if mod == 2 else 32))
                    gate = (gate_m if mod == 2 else gate_f)[:, 512 * h:512 * h + 512]
                    chain(dve.tensor_tensor(gate, ps[:, 6, :], row, ALU.add))
                    dve.tensor_tensor(gate, gate, st[:, 1, 512 * h:512 * h + 512], ALU.mult).then_inc(s_modr, 1)
                else:
                    if i >= 2:
                        dve.wait_ge(s_colmm, turned(ADA_B) * l + turned(i - 2))
                    dve.tensor_tensor(st[:, 0, 512 * (i % 2):512 * (i % 2) + 512], ps[:, 6, :], row, ALU.add
                                      ).then_inc(s_modr, 1)

            def mod_columns(l, half):
                dve.wait_ge(s_colmm, turned(ADA_B) * l + HEAD * (half + 1))
                dve.wait_ge(s_gcol, 16 * 2 * DEPTH)
                m = 2 * half
                src = [ps[:, 7, 16 * i:16 * i + 16].rearrange("p (k g) -> p k g", g=2) for i in (m, m + 1)]
                dve.tensor_copy(modc[:, m, :, :], src[0])
                for g in range(2):
                    ins = dve.scalar_tensor_tensor(out=modc[:, m + 1, :, g], in0=src[1][:, :, g], scalar=1.0,
                                                   in1=gcol[:, l, half, :], op0=ALU.add, op1=ALU.mult)
                ins.then_inc(s_modc, 1)

            def norm(s, l, half):
                r = 5 * l + 3 * half
                for t in range(NT):
                    inverse_rms(r, t)
                    dve.tensor_scalar(f[:, t, :], x[:, t, :], rs[:, r, t:t + 1], None, ALU.mult).then_inc(s_xn, 1)
                if s == 0:
                    mod_columns(0, 0)
                for kt in range(KT if s < 3 else 0):
                    dve.wait_ge(s_hf, KT * s + kt + 1)
                    dve.tensor_copy(xhi[:, kt, :], hf[:, kt, :]).then_inc(s_xhi, 1)
                    dve.wait_ge(s_xhi, KT * s + kt + 1)
                    dve.tensor_tensor(xlo[:, kt, :], hf[:, kt, :], xhi[:, kt, :].bitcast(F32), ALU.subtract
                                      ).then_inc(s_xlo, 1)

            def residual(s, l, half):
                r = 5 * l + 2 + 2 * half
                for t in range(NT):
                    g = min(t, 1)
                    inverse_rms(r, t)
                    if s == 3:
                        dve.wait_ge(s_gt, 12 + g + 1)
                        dve.wait_ge(s_back, 16)
                        y, z1 = f[:, t, :], f[:, t, :]
                        gate = ps[:, 2 * g:2 * g + 2, :].rearrange("p a n -> p (a n)")
                    else:
                        dve.wait_ge(s_gtc, 4 * s + 4)
                        y, z1 = ps[:, 2 * t:2 * t + 2, :].rearrange("p a n -> p (a n)"), f[:, 2, :]
                        gate = f[:, g, :]
                    chain(dve.scalar_tensor_tensor(out=z1, in0=y, scalar=rs[:, r, t:t + 1], in1=gate,
                                                   op0=ALU.mult, op1=ALU.mult))
                    dve.tensor_tensor(x[:, t, :], x[:, t, :], z1, ALU.add).then_inc(s_xr, 1)

            dve.wait_ge(s_sil, 1)
            chain(dve.tensor_tensor(sill[:, :, :], sil[:, :, :], silh[:, :, :].bitcast(F32), ALU.subtract))

            def ahead(j, e):
                if e is None:
                    upto(PLACE["ffn", 0, j])
                else:
                    while state["j"] <= j:
                        split(e, state["j"])
                        state["j"] += 1

            def choose(e):
                dve.tensor_copy(cur[:, :, :], rt[:, e, :, :] if isinstance(e, int) else
                                rt[:, bass.ds(e, 1), :, :].rearrange("p e i t -> p (e i) t")).then_inc(s_cur, 1)
                dve.wait_ge(s_cur, e + 1)
                for t in range(NT):
                    ins = dve.tensor_scalar(perm[:, t, :], iota[:, :], cur[:, 1, t:t + 1],
                                            cur[:, 2, t:t + 1], ALU.is_equal, ALU.mult)
                ins.then_inc(s_perm, 1)

            def gate_up(T, k, e=None):
                state["j"] = 3

                def lo(b):
                    for i in range(2):
                        dve.wait_ge(s_hhi, k * 2 * GU_B + 2 * b + i + 1)
                        dve.tensor_tensor(hlo[:, 2 * b + i, 0:P * T], ps[:, 6 + i, 0:P * T],
                                          hhi[:, 2 * b + i, 0:P * T].bitcast(F32), ALU.subtract).then_inc(s_hlo, 1)

                for b in range(GU_B):
                    ahead(2 * b + 3, e)
                    dve.wait_ge(s_sg, k * GU_B + b + 1)
                    for t in range(T):
                        ins = dve.tensor_tensor(pg[:, t, :], pg[:, t, :], ps[:, 2 * t + b % 2, 256:512], ALU.mult)
                    ins.then_inc(s_pm, 1)
                    if b:
                        lo(b - 1)
                    if e is not None and b == 3:
                        dve.wait_ge(s_pmt, e * NT + NT)
                        choose(e + 1)
                ahead(N_GU + 2, e)
                lo(GU_B - 1)

            def gather(T, e, splits=()):
                for kt in range(KT):
                    if kt in splits:
                        split(e, splits[kt])
                    dve.wait_ge(s_ghi, e * KT + kt + 1)
                    dve.tensor_tensor(xlo[:, kt, 0:P * T], ps[:, GATHER_BANK[kt], 0:P * T],
                                      xhi[:, kt, 0:P * T].bitcast(F32), ALU.subtract).then_inc(s_glo, 1)

            def gather_next(T, e):
                gather(T, e, SPLITS_IN_GATHER)

            def expert(T, e):
                gate_up(T, e + 1, e)
                ahead(N_FFN - 1, e)
                with dve.If(e < NE - 1):
                    split(e + 1, 0)
                dve.wait_ge(s_yhi, e + 1)
                for t in range(T):
                    ins = dve.tensor_tensor(ylo[:, t, :], ps[:, 2 * t:2 * t + 2, :].rearrange("p a n -> p (a n)"),
                                            yhi[:, t, :].bitcast(F32), ALU.subtract)
                ins.then_inc(s_ylo, 1)

            build_cs()
            for i in range(HEAD):
                ada(0, i)
            for l in range(DEPTH):
                upto(PLACE["win", l, 0] + 1)
                norm(2 * l, l, 0)
                for i in range(HEAD, ADA_B):
                    ada(l, i)
                mod_columns(l, 1)
                dve.wait_ge(s_ld[l][0], 16 * 2 * NH)
                dve.wait_ge(s_const, N_CONST)
                dve.tensor_tensor(bias[:, :, :].rearrange("p h (m k) -> p (h m) k", k=GW),
                                  bias[:, :, :].rearrange("p h (m k) -> p (h m) k", k=GW),
                                  win_mask[:, :].rearrange("p (a k) -> p a k", a=1).to_broadcast([P, NH * NDR, GW]),
                                  ALU.add).then_inc(s_bias, 1)
                dve.wait_ge(s_ld[l][2], 32)
                for t in range(NT):
                    inverse_rms(5 * l + 1, t)
                    v = pr[:, t, OVM:OVM + D_CM]
                    ins = dve.scalar_tensor_tensor(out=v, in0=v, scalar=rs[:, 5 * l + 1, t:t + 1],
                                                   in1=gvb[:, :], op0=ALU.mult, op1=ALU.mult)
                ins.then_inc(s_vn, 1)
                upto(PLACE["win", l, N_WIN - 1] + 2)
                dve.wait_ge(s_wsp, l + 1)
                dve.tensor_copy(wsT[:, :, :].rearrange("p a n -> p (a n)"), ps[:, 0, :]).then_inc(s_wst, 1)
                for i in range(1, 9, 2):
                    dve.wait_ge(s_qk, 9 * l + i + 1)
                    dst = qT[:, i, :] if i < 4 else kT[:, i - 4, :]
                    dve.tensor_copy(dst, ps[:, 7, 0:384]).then_inc(s_qkd, 1)
                dve.wait_ge(s_pr, NT * WIN_B * (l + 1))
                dve.tensor_tensor(z[:, :, :], pr[:, :, OC:OC + D_CV], pr[:, :, OH:OH + D_CV], ALU.mult
                                  ).then_inc(s_z, 1)
                dve.wait_ge(s_mix, l + 1)
                for t in range(NT):
                    for h in range(4):
                        u = pr[:, t, OU + 64 * h:OU + 64 * h + 64]
                        ins = dve.scalar_tensor_tensor(out=u, in0=ps[:, t, 64 * h:64 * h + 64],
                                                       scalar=bs[:, h:h + 1], in1=u, op0=ALU.add, op1=ALU.mult)
                ins.then_inc(s_cm, 1)
                def convolve():
                    dve.wait_ge(s_sh, l + 1)
                    dve.wait_ge(s_ld[l][3], 16)
                    dve.wait_ge(s_z, l + 1)

                    def tap(j):
                        return wcb[:, :, j].rearrange("p (a c) -> p a c", a=1).to_broadcast([P, NT, D_CV])

                    yc, yt = pr[:, :, OC:OC + D_CV], pr[:, :, OH:OH + D_CV]
                    yb = pr[:, :, OB:OB + D_CV]
                    chain(dve.tensor_tensor(yc, z[:, :, :], tap(1), ALU.mult))
                    chain(dve.tensor_tensor(yt, ps[:, 4:7, 0:256], tap(0), ALU.mult))
                    chain(dve.tensor_tensor(yc, yc, yt, ALU.add))
                    chain(dve.tensor_tensor(yt, ps[:, 4:7, 256:512], tap(2), ALU.mult))
                    chain(dve.tensor_tensor(yc, yc, yt, ALU.add))
                    dve.tensor_tensor(yb, yb, yc, ALU.mult).then_inc(s_cvd, 1)

                dve.wait_ge(s_bias, l + 1)

                def soft(u):
                    t, h = UNITS[u]
                    s, b = u % 4, 2 * (u % 2)
                    dve.wait_ge(s_sc, NU * l + u + 1)
                    if u >= 4:
                        dve.wait_ge(s_pt, NU * l + u - 3)
                    if t == 0:
                        w = P
                        chain(dve.tensor_scalar(pS[:, s, :, 0:P], ps[:, b:b + 2, 0:P], SCALE, None, ALU.mult))
                    else:
                        w = NT * P
                        m0 = 2 - 2 * (t - 1)
                        dve.scalar_tensor_tensor(out=pS[:, s, :, 0:256], in0=ps[:, b:b + 2, 0:256], scalar=SCALE,
                                                 in1=bias[:, h:h + 2, GW * m0:GW * (m0 + 4)],
                                                 op0=ALU.mult, op1=ALU.add)
                        chain(dve.tensor_scalar(pS[:, s, :, 256:384], ps[:, b:b + 2, 256:384], SCALE, None,
                                                ALU.mult))
                    chain(dve.tensor_reduce(nm[:, s, 0, :], pS[:, s, :, 0:w], AX_X, ALU.max))
                    dve.tensor_scalar(nm[:, s, 1, :], nm[:, s, 0, :], -1.0, None, ALU.mult).then_inc(s_sm, 1)

                def out(u):
                    t, h = UNITS[u]
                    s = u % 4
                    dve.wait_ge(s_pv, NU * l + u + 1)
                    chain(dve.reciprocal(rden[:, s, :], den[:, s, :]))
                    dve.tensor_tensor(pr[:, t, 64 * h:64 * h + 128].rearrange("p (a d) -> p a d", a=2),
                                      ps[:, 6 + u % 2, 0:128].rearrange("p (a d) -> p a d", a=2),
                                      rden[:, s, :].rearrange("p (a d) -> p a d", d=1).to_broadcast([P, 2, HD]),
                                      ALU.mult).then_inc(s_o, 1)

                for u in range(NU + 3):
                    if u < NU:
                        soft(u)
                    if u == 1:
                        convolve()
                    if u >= 3:
                        out(u - 3)
                for kt in range(KT):
                    dve.wait_ge(s_mhi, KT * l + kt + 1)
                    dve.tensor_tensor(xlo[:, kt, :], ps[:, 6 + kt % 2, 0:384], xhi[:, kt, :].bitcast(F32),
                                      ALU.subtract).then_inc(s_mlo, 1)
                upto(PLACE["wout", l, N_WOUT - 1] + 2)
                residual(2 * l, l, 0)
                norm(2 * l + 1, l, 1)
                if l == 0:
                    dve.wait_ge(s_cvd, 1)
                    build_cs()
                    gate_up(NT, 0)
                    for j in range(N_GU, N_FFN):
                        ahead(j, None)
                        if j - N_GU in ADA_IN_WD:
                            ada(1, ADA_IN_WD[j - N_GU])
                        if j - N_GU == max(ADA_IN_WD):
                            mod_columns(1, 0)
                    upto(PLACE["win", 1, 0] + 1)
                    residual(1, 0, 1)
            dve.wait_ge(s_tr, 4 * KT)
            for t in range(NT):
                dve.memset(f[:, t, :], 0.0).then_inc(s_acc, 1)
            dve.wait_ge(s_lg, 1)
            chain(dve.tensor_copy(lg[:, :, :], ps[:, 0:NT, 0:NE]))
            for t in range(NT):
                ins = dve.max(m8[:, t, :], lg[:, t, :])
            chain(ins)
            dve.tensor_tensor(ge[:, :, 0], m8[:, :, 1], m8[:, :, 0], ALU.subtract).then_inc(s_rt, 1)
            for t in range(NT):
                ins = dve.max_index(ix[:, t, :], m8[:, t, :], lg[:, t, :])
            chain(ins)
            chain(dve.tensor_copy(ixf[:, :, :], ix[:, :, :]))
            places = iota[:, 0:NE].rearrange("p (a e) -> p a e", a=1).to_broadcast([P, NT, NE])
            by_expert = rt[:, 0:NE, :, :].rearrange("p e i t -> p i t e")
            chain(dve.tensor_tensor(hot[:, :, :], places, ixf[:, :, 0:1].to_broadcast([P, NT, NE]), ALU.is_equal))
            chain(dve.tensor_tensor(hot1[:, :, :], places, ixf[:, :, 1:2].to_broadcast([P, NT, NE]), ALU.is_equal))
            chain(dve.memset(rt[:, NE, :, :], 0.0))
            dve.tensor_tensor(by_expert[:, 2], hot[:, :, :], hot1[:, :, :], ALU.add).then_inc(s_hot, 1)
            dve.wait_ge(s_rte, 1)
            chain(dve.tensor_scalar(ge[:, :, 2], ge[:, :, 1], 1.0, None, ALU.add))
            chain(dve.reciprocal(ge[:, :, 2], ge[:, :, 2]))
            chain(dve.tensor_tensor(ge[:, :, 3], ge[:, :, 1], ge[:, :, 2], ALU.mult))
            chain(dve.tensor_tensor(hot[:, :, :], hot[:, :, :], ge[:, :, 2:3].to_broadcast([P, NT, NE]), ALU.mult))
            chain(dve.tensor_tensor(hot1[:, :, :], hot1[:, :, :], ge[:, :, 3:4].to_broadcast([P, NT, NE]), ALU.mult))
            chain(dve.tensor_tensor(by_expert[:, 0], hot[:, :, :], hot1[:, :, :], ALU.add))
            upto(EXP0 + 2)
            dve.wait_ge(s_pos, 1)
            chain(dve.tensor_copy(by_expert[:, 1], ps[:, 0:NT, 64:64 + NE]))
            chain(dve.memset(ntile[:, :], 0))
            chain(dve.tensor_scalar(cnt[:, :], ps[:, 3, 0:NE], float(P), None, ALU.is_gt))
            chain(dve.tensor_scalar(lg[:, 0, :], ps[:, 3, 0:NE], float(2 * P), 1.0, ALU.is_gt, ALU.add))
            dve.tensor_tensor(ntile[:, 0:NE], cnt[:, :], lg[:, 0, :], ALU.add).then_inc(s_nt, 1)
            choose(0)
            dve.wait_ge(s_nt, 1)
            T0 = dve.value_load(ntile[0:1, 0:1], min_val=0, max_val=3)
            by_tiles(dve, T0, gather, 0)
            with dve.Fori(0, NE) as e:
                T = dve.value_load(ntile[0:1, bass.ds(e, 1)], min_val=0, max_val=3)
                next_T = dve.value_load(ntile[0:1, bass.ds(e + 1, 1)], min_val=0, max_val=3)
                by_tiles(dve, T, expert, e)
                by_tiles(dve, next_T, gather_next, e + 1, lambda: dve.sem_inc(s_glo, KT))
                dve.tensor_copy(gate_e[:, :], rt[:, bass.ds(e, 1), 0, :].rearrange("p e t -> p (e t)")
                                ).then_inc(s_gte, 1)
                dve.wait_ge(s_gte, e + 1)
                for t in range(NT):
                    dve.wait_ge(s_scm, e * NT + t + 1)
                    dve.scalar_tensor_tensor(out=f[:, t, :], in0=ps[:, 2 * t:2 * t + 2, :].rearrange("p a n -> p (a n)"),
                                             scalar=gate_e[:, t:t + 1], in1=f[:, t, :], op0=ALU.mult, op1=ALU.add
                                             ).then_inc(s_acc, 1)
            residual(3, 1, 1)

        @block.tensor
        def _(pe):
            def pe_done(ins):
                ins.then_inc(s_pe, 1)

            def three(out, a_hi, a_lo, w_hi, w_lo, start, stop):
                pe.matmul(out, a_hi, w_hi, start=start, stop=False)
                pe.matmul(out, a_hi, w_lo, start=False, stop=False)
                return pe.matmul(out, a_lo, w_hi, start=False, stop=stop)

            def halves(n, k):
                return (whi[n % SPL][:, :].rearrange("p (k n) -> p k n", k=k),
                        wlo[n % SPL][:, :].rearrange("p (k n) -> p k n", k=k))

            def ada_turn(l, i):
                mod, h = divmod(ADA_SEQ[i], 2)
                if mod in (2, 5):
                    return
                m = [0, 1, None, 2, 3][mod]
                pe.wait_ge(s_modr, ADA_B * l + i + 1)
                for j in range(4):
                    o = 16 * m + 2 * (4 * h + j)
                    a = 512 * (i % 2) + P * j
                    ins = pe.matmul(ps[:, 7, o:o + 2], ada_stage(l, i)[:, 0, a:a + P], sel[:, :],
                                    start=True, stop=True)
                ins.then_inc(s_colmm, 1)

            def ada(l, i):
                if i == 0:
                    pe.wait_ge(s_cs, l + 1)
                if i:
                    pe.wait_ge(s_modr, ADA_B * l + i)
                for h in range(2):
                    n = PLACE["ada", l, 2 * i + h]
                    pe.wait_ge(s_lo, n + 1)
                    hi, lo = halves(n, 4)
                    for k in range(4):
                        a = cS[:, 4 * h + k, :]
                        pe.matmul(ps[:, 6, :], a, hi[:, k, :], start=(h == 0 and k == 0), stop=False)
                        ins = pe.matmul(ps[:, 6, :], a, lo[:, k, :], start=False, stop=(h == 1 and k == 3))
                    pe_done(ins)
                if i not in (0, HEAD):
                    ada_turn(l, i - 1)
                if i == HEAD - 1:
                    ada_turn(l, i)

            def logits(kt):
                for t in range(NT):
                    ins = pe.matmul(ps[:, t, 0:NE], hf[:, kt, P * t:P * t + P], wr[:, kt, :],
                                    start=(kt == 0), stop=(kt == KT - 1))
                if kt == KT - 1:
                    ins.then_inc(s_lg, 1)

            def norm(s):
                for kt in range(KT):
                    if kt == 1 and s % 2 == 0:
                        pe.wait_ge(s_modc, s + 1)
                    if kt >= 2:
                        pe.wait_ge(s_hf, KT * s + kt - 1)
                    for t in range(NT):
                        if kt == 0:
                            pe.wait_ge(s_xn, NT * s + t + 1)
                        ins = pe.transpose(ps[:, 6 + kt % 2, P * t:P * t + P], f[:, t, P * kt:P * kt + P], ident[:, :])
                    ins.then_inc(s_tr, 1)
                    if s == 3 and kt >= 2:
                        if kt == 2:
                            pe.wait_ge(s_wr, 16)
                        logits(kt - 2)
                if s == 3:
                    for kt in (KT - 2, KT - 1):
                        pe.wait_ge(s_hf, KT * s + kt + 1)
                        logits(kt)

            def win(l):
                for b in range(WIN_B):
                    if b >= 2:
                        pe.wait_ge(s_pr, NT * WIN_B * l + NT * (b - 1))
                    w, kk = (512, 4) if b < 5 else (256, 8)
                    for h in range(2 if b < 5 else 1):
                        n = PLACE["win", l, 2 * b + h]
                        pe.wait_ge(s_lo, n + 1)
                        hi, lo = halves(n, kk)
                        for t in range(NT):
                            for k in range(kk):
                                kt = 4 * h + k
                                if t == 0:
                                    pe.wait_ge(s_xlo, KT * 2 * l + kt + 1)
                                a = P * t
                                last = kt == KT - 1
                                ins = three(ps[:, 2 * t + b % 2, 0:w], xhi[:, kt, a:a + P], xlo[:, kt, a:a + P],
                                            hi[:, k, :], lo[:, k, :], kt == 0, last)
                            if last and t < NT - 1:
                                ins.then_inc(s_win, 1)
                        pe_done(ins)
                        if 2 * b + h in ADA_IN_WIN:
                            ada(l, ADA_IN_WIN[2 * b + h])
                        if 2 * b + h == max(ADA_IN_WIN) + 1:
                            ada_turn(l, ADA_B - 1)

            def mixer(l):
                pe.wait_ge(s_pr, NT * WIN_B * l + 13)
                pe.wait_ge(s_ld[l][1], 16)
                for h in range(4):
                    ins = pe.transpose(ps[:, 0, P * h:P * h + P], ws[:, h, :], ident[:, :])
                ins.then_inc(s_wsp, 1)
                pe.wait_ge(s_modc, 2 * l + 2)
                for i in range(9):
                    if i >= 2:
                        pe.wait_ge(s_qka if i % 2 == 0 else s_qkd, (5 if i % 2 == 0 else 4) * l + i // 2)
                    if i == 8:
                        pe.wait_ge(s_ld[l][4], 16)
                        for j in range(4):
                            ins = pe.transpose(ps[:, 6, P * j:P * j + P], ck[:, P * j:P * j + P], ident[:, :])
                    else:
                        o = OQ + P * i if i < 4 else OK + P * (i - 4)
                        for t in range(NT):
                            ins = pe.transpose(ps[:, 6 + i % 2, P * t:P * t + P], pr[:, t, o:o + P], ident[:, :])
                    ins.then_inc(s_qk, 1)
                pe.wait_ge(s_vn, l + 1)
                pe.wait_ge(s_wst, l + 1)
                pe.wait_ge(s_pr, NT * WIN_B * (l + 1))
                for t in range(NT):
                    for h in range(4):
                        ins = pe.matmul(ps[:, t, 64 * h:64 * h + 64], wsT[:, h, :],
                                        pr[:, t, OVM + 64 * h:OVM + 64 * h + 64], start=True, stop=True)
                ins.then_inc(s_mix, 1)
                pe.wait_ge(s_z, l + 1)
                pe.wait_ge(s_qka, 5 * (l + 1))
                for t in range(NT):
                    near = [(0, 0, t), (1, 256, t)]
                    if t == 1:
                        near.append((3, 256, 2))
                    if t == 2:
                        near.insert(1, (2, 0, 1))
                    for i, o, src in near:
                        start = i < 2
                        stop = not ((t == 1 and i == 1) or (t == 2 and i == 0))
                        ins = pe.matmul(ps[:, 4 + t, o:o + 256], shift[:, i, :], z[:, src, :], start=start, stop=stop)
                ins.then_inc(s_sh, 1)
                pe.wait_ge(s_qka, 5 * (l + 1))
                pe.wait_ge(s_qkd, 4 * (l + 1))
                pe.wait_ge(s_cm, l + 1)
                pe.wait_ge(s_ld[l][5], 16)

                def score(u):
                    t, h = UNITS[u]
                    j = h // 2
                    if u >= 2:
                        pe.wait_ge(s_sm, NU * l + u - 1)
                    for a in range(2):
                        o = ps[:, 2 * (u % 2) + a, :]
                        r = slice(64 * a, 64 * a + 64)
                        q = qT[r, j, P * t:P * t + P]
                        if t == 0:
                            ins = pe.matmul(o[:, 0:P], q, kT[r, j, 0:P], start=True, stop=True)
                        else:
                            pe.matmul(o[:, 0:256], q, kT[r, j, P:3 * P], start=True, stop=True)
                            ins = pe.matmul(o[:, 256:384], q, ckT[r, j, :], start=True, stop=True)
                    ins.then_inc(s_sc, 1)

                def turn(u):
                    pe.wait_ge(s_ex, NU * l + u + 1)
                    if u >= 1:
                        pe.wait_ge(s_ptc, NU * l + u)
                    for a in range(2):
                        for j in range(1 if UNITS[u][0] == 0 else NT):
                            ins = pe.transpose(ps[:, 4 + a, P * j:P * j + P], pS[:, u % 4, a, P * j:P * j + P],
                                               ident[:, :])
                    ins.then_inc(s_pt, 1)

                def value(u):
                    t, h = UNITS[u]
                    pe.wait_ge(s_ptc, NU * l + u + 1)
                    if u >= 2:
                        pe.wait_ge(s_o, NU * l + u - 1)
                    for a in range(2):
                        o = 64 * (h + a)
                        vs = [pr[:, 0, OV + o:OV + o + 64]] if t == 0 else [
                            pr[:, 1, OV + o:OV + o + 64], pr[:, 2, OV + o:OV + o + 64], cv[:, o:o + 64]]
                        for j, v in enumerate(vs):
                            ins = pe.matmul(ps[:, 6 + u % 2, 64 * a:64 * a + 64], pT[:, u % 2, a, P * j:P * j + P], v,
                                            start=(j == 0), stop=(j == len(vs) - 1))
                    ins.then_inc(s_pv, 1)

                for u in range(NU + 3):
                    if u < NU:
                        score(u)
                    if u == 2:
                        pe.wait_ge(s_cvd, l + 1)
                    if 2 <= u < NU + 2:
                        turn(u - 2)
                    if u >= 3:
                        value(u - 3)
                pe.wait_ge(s_o, NU * (l + 1))
                for kt in range(KT):
                    if kt >= 2:
                        pe.wait_ge(s_mlo, KT * l + kt - 1)
                    o = mix_col(kt)
                    for t in range(NT):
                        ins = pe.transpose(ps[:, 6 + kt % 2, P * t:P * t + P], pr[:, t, o:o + P], ident[:, :])
                    ins.then_inc(s_mt, 1)

            def down(T, hi_of, lo_of, place, nk, wait, s_done, between=None, even_banks=None):
                for q in range(nk // 2):
                    wait(q)
                    hi, lo = halves(place(q), 2)
                    steps = [(t, h) for h in (1, 0) for t in range(T)] if q == 0 else [
                        (t, h) for t in range(T) for h in (1, 0)]
                    for i, (t, h) in enumerate(steps):
                        if q == 0 and i == T and even_banks is not None:
                            even_banks()
                        for k in range(2):
                            kt, o = 2 * q + k, slice(512 * h, 512 * h + 512)
                            ins = three(ps[:, 2 * t + h, :], hi_of[:, kt, P * t:P * t + P],
                                        lo_of[:, kt, P * t:P * t + P], hi[:, k, o], lo[:, k, o],
                                        kt == 0, kt == nk - 1)
                        if q == nk // 2 - 1 and t < NT - 1 and h == 0 and s_done is not None:
                            ins.then_inc(s_done, 1)
                    pe_done(ins)
                    if between is not None:
                        between(q)

            def wout(l):
                def wait(q):
                    pe.wait_ge(s_lo, PLACE["wout", l, q] + 1)
                    pe.wait_ge(s_mlo, KT * l + 2 * q + 2)

                def between(q):
                    if q == 2:
                        pe.wait_ge(s_mlo, KT * (l + 1))
                        gates(2 * l, gate_m)
                down(NT, xhi, xlo, lambda q: PLACE["wout", l, q], KT, wait, s_y, between)

            def gates(s, gate):
                for i in range(4):
                    if i >= 2:
                        pe.wait_ge(s_gtc, 4 * s + i - 1)
                    ins = pe.matmul(ps[:, 6 + i % 2, :], selb[:, i // 2, :],
                                    gate[:, 512 * (i % 2):512 * (i % 2) + 512], start=True, stop=True)
                    ins.then_inc(s_gt, 1)

            def last_gates():
                pe.wait_ge(s_acc, NT * NE + NT)
                for g in range(2):
                    for h in range(2):
                        ins = pe.matmul(ps[:, 2 * g + h, :], selb[:, g, :], gate_f[:, 512 * h:512 * h + 512],
                                        start=True, stop=True)
                    ins.then_inc(s_gt, 1)

            def turn(T, k, b):
                pe.wait_ge(s_pm, k * GU_B + b + 1)
                for i in range(2):
                    if b:
                        pe.wait_ge(s_hlo, k * 2 * GU_B + 2 * (b - 1) + i + 1)
                    for t in range(T):
                        ins = pe.transpose(ps[:, 6 + i, P * t:P * t + P], pg[:, t, P * i:P * i + P], ident[:, :])
                    ins.then_inc(s_ht, 1)

            def gate_up(T, k, e=None):
                def wait_lo(j):
                    if e is None:
                        pe.wait_ge(s_lo, PLACE["ffn", 0, j] + 1)
                    else:
                        pe.wait_ge(s_lo, e * N_FFN + (EXP0 + j + 1))

                def place(j):
                    return PLACE["ffn", 0, j] if e is None else j

                for b in range(GU_B):
                    if b >= 2:
                        pe.wait_ge(s_pm, k * GU_B + b - 1)
                    if b == 1 and e is not None:
                        pe.wait_ge(s_pmc, e * NT + NT)
                        if T < NT:
                            pe.sem_inc(s_pmt, NT - T)
                    for h in range(2):
                        wait_lo(2 * b + h)
                        hi, lo = halves(place(2 * b + h), 4)
                        for t in range(T):
                            if e is not None and b == 0 and h == 0:
                                pe.wait_ge(s_acc, e * NT + t + 1)
                            for kk in range(4):
                                kt = 4 * h + kk
                                ins = three(ps[:, 2 * t + b % 2, :], xhi[:, kt, P * t:P * t + P],
                                            xlo[:, kt, P * t:P * t + P], hi[:, kk, :], lo[:, kk, :],
                                            kt == 0, kt == KT - 1)
                        pe_done(ins)
                    if b:
                        turn(T, k, b - 1)

            def project(T, k, e=None):
                def wait(q):
                    if e is None:
                        pe.wait_ge(s_lo, PLACE["ffn", 0, N_GU + q] + 1)
                    else:
                        pe.wait_ge(s_lo, e * N_FFN + (EXP0 + N_GU + q + 1))
                    pe.wait_ge(s_hlo, k * 2 * GU_B + 2 * q + 2)

                def between(q):
                    if q == 0:
                        turn(T, k, GU_B - 1)
                    if e is None and q in ADA_IN_WD:
                        if q == min(ADA_IN_WD):
                            pe.wait_ge(s_hlo, 2 * GU_B)
                        ada(1, ADA_IN_WD[q])

                    if e is None and q == max(ADA_IN_WD) + 1:
                        pe.wait_ge(s_modc, 3)
                        gates(1, gate_f)

                def even_banks():
                    pe.wait_ge(s_pm, (k + 1) * GU_B)

                if e is None:
                    down(T, hhi, hlo, lambda q: PLACE["ffn", 0, N_GU + q], FK, wait, s_y, between,
                         even_banks)
                else:
                    down(T, hhi, hlo, lambda q: N_GU + q, FK, wait, None, between, even_banks)

            def gather(T, e):
                pe.wait_ge(s_perm, e + 1)
                pe.wait_ge(s_hlo, e * 2 * GU_B + 2 * GU_B)
                for kt in range(KT):
                    if kt == 2 and not isinstance(e, int):
                        pe.wait_ge(s_ylo, e)
                    for t in range(NT):
                        ins = pe.matmul(ps[:, GATHER_BANK[kt], 0:P * T], x[:, t, P * kt:P * kt + P], perm[:, t, 0:P * T],
                                        start=(t == 0), stop=(t == NT - 1))
                    ins.then_inc(s_ga, 1)

            def expert(T, e):
                pe.wait_ge(s_glo, e * KT + KT)
                for t in range(T):
                    if t >= 2:
                        pe.wait_ge(s_pmc, e * NT + 1)
                    for i in range(NT):
                        ins = pe.transpose(ps[:, 6 + t % 2, P * i:P * i + P], perm[:, i, P * t:P * t + P], ident[:, :])
                    ins.then_inc(s_pmt, 1)
                gate_up(T, e + 1, e)
                project(T, e + 1, e)

            def scatter(T, e):
                pe.wait_ge(s_acc, e * NT + NT)
                pe.wait_ge(s_ylo, e + 1)
                for i in range(NT):
                    pe.wait_ge(s_glo, e * KT + (KT + 2 * i + 4))
                    for h in range(2):
                        for t in range(T):
                            a, o = permT[:, t, P * i:P * i + P], slice(512 * h, 512 * h + 512)
                            pe.matmul(ps[:, 2 * i + h, :], a, yhi[:, t, o], start=(t == 0), stop=False)
                            ins = pe.matmul(ps[:, 2 * i + h, :], a, ylo[:, t, o], start=False, stop=(t == T - 1))
                    ins.then_inc(s_scm, 1)

            pe.wait_ge(s_const, N_CONST)
            for i in range(HEAD):
                ada(0, i)
            for l in range(DEPTH):
                norm(2 * l)
                win(l)
                mixer(l)
                wout(l)
                norm(2 * l + 1)
                if l == 0:
                    pe.wait_ge(s_xlo, KT * 2)
                    gate_up(NT, 0)
                    project(NT, 0)
            for i in range(6):
                t, h = divmod(i, 2)
                if i >= 2:
                    pe.wait_ge(s_btc, i - 1)
                for j in range(4):
                    ins = pe.transpose(ps[:, 6 + i % 2, P * j:P * j + P], hf[:, 4 * h + j, P * t:P * t + P], ident[:, :])
                ins.then_inc(s_bt, 1)
            pe.wait_ge(s_hot, 1)
            pe.wait_ge(s_tri, 1)
            for t in range(NT):
                for i in range(t + 1):
                    pe.matmul(ps[:, t, 64:64 + NE], ones[:, :] if i < t else before[:, :], rt[:, 0:NE, 2, i],
                              start=(i == 0), stop=(i == t))
            for t in range(NT):
                ins = pe.matmul(ps[:, 3, 0:NE], ones[:, :], rt[:, 0:NE, 2, t], start=(t == 0), stop=(t == NT - 1))
            ins.then_inc(s_pos, 1)
            pe.wait_ge(s_btc, 6)
            pe.wait_ge(s_nt, 1)
            T0 = pe.value_load(ntile[0:1, 0:1], min_val=0, max_val=3)
            by_tiles(pe, T0, gather, 0)
            with pe.Fori(0, NE) as e:
                T = pe.value_load(ntile[0:1, bass.ds(e, 1)], min_val=0, max_val=3)
                next_T = pe.value_load(ntile[0:1, bass.ds(e + 1, 1)], min_val=0, max_val=3)
                by_tiles(pe, T, expert, e)
                by_tiles(pe, next_T, gather, e + 1, lambda: None)
                by_tiles(pe, T, scatter, e)
            last_gates()


_INS = ['x_prompt', 'x_sample', 'cache_k', 'cache_v', 'c', 'c_ctx', 'w_ada', 'b_ada', 'norm_g', 'w_in', 'w_out',
        'rpb', 'g_v', 'w_s', 'b_s', 'w_conv', 'w_ffn_gu', 'w_ffn_d', 'w_router', 'w_moe_gu', 'w_moe_d']
_OUTS = [(1, P, D), (1, 2 * P, D), (1, DEPTH, P, NH, HD), (1, DEPTH, P, NH, HD)]


def kernel(**inputs):
    import numpy as _np
    import concourse.bacc as _bacc
    from concourse.bass_utils import run_bass_kernel_spmd as _run

    nc = _bacc.Bacc("TRN2", target_bir_lowering=False, num_devices=1)
    arrays, args = {}, []
    for name in _INS:
        a = _np.ascontiguousarray(inputs[name])
        arrays[f"in_{name}_dram"] = a
        args.append(nc.dram_tensor(f"in_{name}_dram", a.shape, mybir.dt.from_np(a.dtype), kind="ExternalInput").ap())
    for i, shape in enumerate(_OUTS):
        args.append(nc.dram_tensor(f"out_{i}_dram", shape, F32, kind="ExternalOutput").ap())
    args.append(nc.dram_tensor("x_park", (NT * P, D), F32, kind="Internal").ap())
    args.append(nc.dram_tensor("rpb_pad", (DEPTH, 7 * NH, GW, 127), F32, kind="Internal").ap())
    build(nc, *args)
    r = _run(nc, [arrays], core_ids=[0])
    return tuple(r.results[0][f"out_{i}_dram"] for i in range(len(_OUTS)))
```
